# Optimizing a Trainium2 kernel written in Bass

```python
import math
import jax, jax.numpy as jnp
from jax import lax
import numpy as np

D_MODEL = 1024
BATCH = 1
SEQ = 512
DEPTH = 1

CHUNK = 64
D_MIX = D_MODEL
HGRN_WIDTH = D_MIX // 2
HGRN_EXPAND = 128
HGRN_HEADS = HGRN_WIDTH // HGRN_EXPAND
HGRN_DK = HGRN_EXPAND
HGRN_DV = HGRN_WIDTH // HGRN_HEADS
ATTN_WIDTH = D_MIX - HGRN_WIDTH
ATTN_HEAD_DIM = 64
ATTN_HEADS = ATTN_WIDTH // ATTN_HEAD_DIM
LEFT_CHUNKS = 8
BAND = (LEFT_CHUNKS + 1) * CHUNK
MAX_REL = 128
N_REL = 2 * MAX_REL + 1
N_GROUPS = 4
EXPERTS_PER_GROUP = 8
N_EXPERTS = N_GROUPS * EXPERTS_PER_GROUP
EXPERT_FF = D_MODEL // 4
TOP_K = 2
EPS = 1e-6
IN_SPLITS = [HGRN_WIDTH, 2 * HGRN_WIDTH, 3 * HGRN_WIDTH, 4 * HGRN_WIDTH,
             4 * HGRN_WIDTH + ATTN_WIDTH, 4 * HGRN_WIDTH + 2 * ATTN_WIDTH]
IN_COLS = 4 * HGRN_WIDTH + 3 * ATTN_WIDTH

kernel_name = "hymba_style_hgrn2_band_attn_hier_moe"

def rms_norm(x, w):
    xf = x.astype(jnp.float32)
    y = xf * lax.rsqrt(jnp.mean(xf * xf, axis=-1, keepdims=True) + EPS)
    return (y * w.astype(jnp.float32)).astype(x.dtype)

def hgrn2_mixer(q_pre, f_pre, i_in, g_pre, lb, gnorm_w):
    B, S, _ = q_pre.shape
    nC = S // CHUNK
    f32 = jnp.float32
    q = jax.nn.silu(q_pre.astype(f32))
    lbf = lb.astype(f32)
    log_f = jnp.logaddexp(jnp.log(lbf), jnp.log1p(-lbf) + jax.nn.log_sigmoid(f_pre.astype(f32)))
    k = -jnp.expm1(log_f)
    v = i_in.astype(f32)

    def to_chunks(t, d):
        return t.reshape(B, nC, CHUNK, HGRN_HEADS, d).transpose(1, 0, 3, 2, 4)

    qc, kc, vc, lfc = (to_chunks(q, HGRN_DK), to_chunks(k, HGRN_DK),
                       to_chunks(v, HGRN_DV), to_chunks(log_f, HGRN_DK))
    causal = jnp.tril(jnp.ones((CHUNK, CHUNK), dtype=bool))

    def step(state, inp):
        qb, kb, vb, lfb = inp
        bcum = jnp.cumsum(lfb, axis=2)
        diff = bcum[:, :, :, None, :] - bcum[:, :, None, :, :]
        decay = jnp.exp(jnp.where(causal[None, None, :, :, None], diff, -jnp.inf))
        scores = jnp.einsum('bhtd,bhsd,bhtsd->bhts', qb, kb, decay)
        o_intra = jnp.einsum('bhts,bhsv->bhtv', scores, vb)
        o_inter = jnp.einsum('bhtd,bhdv->bhtv', qb * jnp.exp(bcum), state)
        b_last = bcum[:, :, -1:, :]
        k_dec = kb * jnp.exp(b_last - bcum)
        new_state = jnp.exp(b_last[:, :, 0, :])[..., None] * state + \
            jnp.einsum('bhsd,bhsv->bhdv', k_dec, vb)
        return new_state, o_intra + o_inter

    s0 = jnp.zeros((B, HGRN_HEADS, HGRN_DK, HGRN_DV), f32)
    _, oc = lax.scan(step, s0, (qc, kc, vc, lfc))
    o = oc.transpose(1, 0, 3, 2, 4).reshape(B, S, HGRN_HEADS, HGRN_DV)
    o = o * lax.rsqrt(jnp.mean(o * o, axis=-1, keepdims=True) + EPS)
    o = o * gnorm_w.astype(f32).reshape(HGRN_HEADS, HGRN_DV)
    o = o.reshape(B, S, HGRN_WIDTH) * jax.nn.silu(g_pre.astype(f32))
    return o.astype(q_pre.dtype)

def chunked_band_attention(q, k, v, rel_bias, norm_w):
    B, S, _ = q.shape
    nC = S // CHUNK
    qh = q.reshape(B, nC, CHUNK, ATTN_HEADS, ATTN_HEAD_DIM)
    kh = k.reshape(B, nC, CHUNK, ATTN_HEADS, ATTN_HEAD_DIM)
    vh = v.reshape(B, nC, CHUNK, ATTN_HEADS, ATTN_HEAD_DIM)
    pad = ((0, 0), (LEFT_CHUNKS, 0), (0, 0), (0, 0), (0, 0))
    kp, vp = jnp.pad(kh, pad), jnp.pad(vh, pad)
    k_band = jnp.concatenate([kp[:, j:j + nC] for j in range(LEFT_CHUNKS + 1)], axis=2)
    v_band = jnp.concatenate([vp[:, j:j + nC] for j in range(LEFT_CHUNKS + 1)], axis=2)
    a = jnp.arange(CHUNK)[:, None]
    kk = jnp.arange(BAND)[None, :]
    rel_idx = jnp.clip(LEFT_CHUNKS * CHUNK + a - kk, -MAX_REL, MAX_REL) + MAX_REL
    bias = rel_bias.astype(jnp.float32)[:, rel_idx]
    valid = (jnp.arange(nC)[:, None] - LEFT_CHUNKS + kk // CHUNK) >= 0
    scale = 1.0 / math.sqrt(ATTN_HEAD_DIM)
    s = jnp.einsum('bnqhd,bnkhd->bhnqk', qh, k_band).astype(jnp.float32) * scale
    s = s + bias[:, None, :, :]
    s = jnp.where(valid[None, None, :, None, :], s, -jnp.inf)
    p = jax.nn.softmax(s, axis=-1).astype(v.dtype)
    o = jnp.einsum('bhnqk,bnkhd->bnqhd', p, v_band).reshape(B, S, ATTN_HEADS, ATTN_HEAD_DIM)
    of = o.astype(jnp.float32)
    of = of * lax.rsqrt(jnp.mean(of * of, axis=-1, keepdims=True) + EPS)
    of = of * norm_w.astype(jnp.float32).reshape(ATTN_HEADS, ATTN_HEAD_DIM)
    return of.reshape(B, S, ATTN_WIDTH).astype(q.dtype)

def hierarchical_moe(h, w_group, w_expert, w1, w3, w2):
    B, S, D = h.shape
    ht = h.reshape(B * S, D)
    g_logits = jnp.einsum('td,dg->tg', ht, w_group).astype(jnp.float32)
    g_prob = jax.nn.softmax(g_logits, axis=-1)
    g_gate, g_idx = lax.top_k(g_prob, 1)
    e_logits = jnp.einsum('td,de->te', ht, w_expert).astype(jnp.float32)
    e_logits = e_logits.reshape(-1, N_GROUPS, EXPERTS_PER_GROUP)
    e_in = jnp.take_along_axis(e_logits, g_idx[:, :, None], axis=1)[:, 0]
    top_v, top_i = lax.top_k(e_in, TOP_K)
    gate = jax.nn.softmax(top_v, axis=-1) * g_gate
    expert_id = g_idx * EXPERTS_PER_GROUP + top_i
    combine = jnp.sum(jax.nn.one_hot(expert_id, N_EXPERTS, dtype=jnp.float32) * gate[..., None], axis=1)
    hidden = jax.nn.silu(jnp.einsum('td,edf->tef', ht, w1)) * jnp.einsum('td,edf->tef', ht, w3)
    hidden = hidden * combine[:, :, None].astype(hidden.dtype)
    y = jnp.einsum('tef,efd->td', hidden, w2)
    return y.reshape(B, S, D).astype(h.dtype)

def setup_inputs(seed: int = 0) -> dict:
    key = jax.random.key(seed)
    ks = jax.random.split(key, 16)
    f32 = jnp.float32
    nrm = lambda k, shape, s: jax.random.normal(k, shape, f32) * s
    return {
        "x": nrm(ks[0], (BATCH, SEQ, D_MODEL), 1.0),
        "norm_mix_w": 1.0 + nrm(ks[1], (DEPTH, D_MODEL), 0.02),
        "w_in": nrm(ks[2], (DEPTH, D_MODEL, IN_COLS), D_MODEL ** -0.5),
        "hgrn_lower_bounds": nrm(ks[3], (DEPTH, HGRN_WIDTH), 0.5),
        "hgrn_gnorm_w": 1.0 + nrm(ks[4], (DEPTH, HGRN_WIDTH), 0.02),
        "attn_rel_bias": nrm(ks[5], (DEPTH, ATTN_HEADS, N_REL), 0.1),
        "attn_norm_w": 1.0 + nrm(ks[6], (DEPTH, ATTN_WIDTH), 0.02),
        "w_out": nrm(ks[7], (DEPTH, D_MIX, D_MODEL), D_MIX ** -0.5),
        "norm_ffn_w": 1.0 + nrm(ks[8], (DEPTH, D_MODEL), 0.02),
        "moe_w_group": nrm(ks[9], (DEPTH, D_MODEL, N_GROUPS), D_MODEL ** -0.5),
        "moe_w_expert": nrm(ks[10], (DEPTH, D_MODEL, N_EXPERTS), D_MODEL ** -0.5),
        "moe_w1": nrm(ks[11], (DEPTH, N_EXPERTS, D_MODEL, EXPERT_FF), D_MODEL ** -0.5),
        "moe_w3": nrm(ks[12], (DEPTH, N_EXPERTS, D_MODEL, EXPERT_FF), D_MODEL ** -0.5),
        "moe_w2": nrm(ks[13], (DEPTH, N_EXPERTS, EXPERT_FF, D_MODEL), EXPERT_FF ** -0.5),
        "final_norm_w": 1.0 + nrm(ks[14], (D_MODEL,), 0.02),
    }

def reference(x, norm_mix_w, w_in, hgrn_lower_bounds, hgrn_gnorm_w, attn_rel_bias, attn_norm_w,
              w_out, norm_ffn_w, moe_w_group, moe_w_expert, moe_w1, moe_w3, moe_w2, final_norm_w):
    lb_all = jnp.cumsum(jax.nn.softmax(hgrn_lower_bounds.astype(jnp.float32), axis=0), axis=0)
    lb_all = lb_all - lb_all[0]
    for l in range(DEPTH):
        h = rms_norm(x, norm_mix_w[l])
        proj = jnp.einsum('bsd,dc->bsc', h, w_in[l])
        hq, hf, hi, hg, aq, ak, av = jnp.split(proj, IN_SPLITS, axis=-1)
        y_rec = hgrn2_mixer(hq, hf, hi, hg, lb_all[l], hgrn_gnorm_w[l])
        y_att = chunked_band_attention(aq, ak, av, attn_rel_bias[l], attn_norm_w[l])
        mixed = jnp.concatenate([y_rec, y_att], axis=-1)
        x = x + jnp.einsum('bsc,cd->bsd', mixed, w_out[l])
        h = rms_norm(x, norm_ffn_w[l])
        x = x + hierarchical_moe(h, moe_w_group[l], moe_w_expert[l], moe_w1[l], moe_w3[l], moe_w2[l])
    return rms_norm(x, final_norm_w)


_drawn_inputs = setup_inputs


def setup_inputs(seed=0):
    import zlib

    import numpy as np

    out = dict(_drawn_inputs(seed))
    spreads = {}
    factors = {'hgrn_gnorm_w': 9.393, 'final_norm_w': 8.257, 'attn_norm_w': 5.348, 'norm_ffn_w': 3.992}
    for name, (base, spread) in spreads.items():
        noise = np.random.default_rng([zlib.crc32(name.encode()), seed]).standard_normal(out[name].shape)
        drawn = base * np.exp(spread * noise) if base else spread * noise
        out[name] = __import__('jax').numpy.asarray(drawn.astype(out[name].dtype))
    for name, factor in factors.items():
        out[name] = (out[name] * factor).astype(out[name].dtype)
    return out
```

```python
from contextlib import ExitStack

import numpy as np
import concourse.bass as bass
from concourse import mybir

ALU = mybir.AluOpType
ACT = mybir.ActivationFunctionType
AX_X = mybir.AxisListType.X
F32 = mybir.dt.float32
I32 = mybir.dt.int32
U32 = mybir.dt.uint32

P = 128
T = 512
D = 1024
NT = T // P
KD = D // P
HW_ = 512
RH = 4
AH, AD = 8, 64
NREL = 257
NG, NE, EPG, FF = 4, 32, 8, 256
SLOTS = 128
BLOCKS = T // SLOTS
OVF_MAX = 7
EPS = 1e-6
NEG = -1e30
FAR = 4096.0
HALVES = [64, 32, 16, 8, 4, 2, 1]
WSLOTS = 4
W13, W2, WE = KD * FF, 2 * D, 2 * KD * FF + 2 * D

C_ID, C_UP, C_ONE, C_IOTA, C_MASK, C_TOK, C_END = 0, 128, 256, 384, 512, 704, 712
V_MIX, V_LB, V_OUT, V_END = 0, 8, 12, 20
GROUPS = ["f", "q", "v", "ak", "aq", "av", "g"]
GROUP_COL = {"q": 0, "f": 512, "v": 1024, "g": 1536, "aq": 2048, "ak": 2560, "av": 3072}
GROUP_BUF = {"f": 0, "q": 1, "v": 2, "ak": 3, "aq": 0, "av": 1, "g": 2}


def psum_plan():
    seen, plan = [0] * 8, {}

    def use(bank, *name):
        plan[name] = (bank, seen[bank])
        seen[bank] += 1

    for i in range(NT):
        for half in range(2):
            use(2 + (2 * i + half) % 4, "xT", i, half)
    n = 0
    for g in ("f", "q", "v", "ak"):
        for j in range(4):
            use(n % 2, g, j)
            n += 1
    use(6, "diag")
    blocks = [("aq", 0), ("aq", 1), ("aq", 2), ("aq", 3), ("av", 0), ("av", 1), ("av", 2), ("av", 3)]
    for li in range(7):
        use(n % 2, *blocks[li])
        n += 1
        if li == 0:
            use(2, "level", 0, 0)
            use(3, "level", 0, 1)
        else:
            use([4, 5, 2, 3, 4, 5][li - 1], "level", li, 0)
    use(n % 2, "av", 3)
    n += 1
    for c, b in enumerate((6, 7, 2)):
        use(b, "kT", c)
    use(n % 2, "g", 0)
    n += 1
    for c, b in enumerate((3, 4, 5)):
        use(b, "delta", c)
    use(n % 2, "g", 1)
    n += 1
    use(6, "o", 0)
    use(7, "o", 1)
    use(n % 2, "g", 2)
    n += 1
    use(2, "o", 2)
    use(3, "o", 3)
    use(n % 2, "g", 3)
    for kind, i in STEPS:
        if kind == "att":
            for t in range(AH + 2):
                if t < AH:
                    use(4 + t % 2, "score", i, t)
                if 1 <= t <= AH:
                    use(2 + (t - 1) % 2, "pT", i, t - 1)
                if t == 2:
                    use(6 + i % 2, "pv", i)
        if kind == "mo":
            use(2, "mT", i, 0)
            use(3, "mT", i, 1)
            use(0, "out", i, 0)
            use(1, "out", i, 1)
        if kind == "rt":
            use(4, "hT2", i, 0)
            use(5, "hT2", i, 1)
            use(6, "logit", i)
        if kind == "rk":
            use(7, "rank", i)
        if kind == "list":
            use(2, "list")
    return plan, seen


STEPS = [("att", 0), ("att", 1), ("mo", 0), ("att", 2), ("mo", 1), ("rt", 0), ("att", 3), ("rk", 0), ("mo", 2),
         ("rt", 1), ("mo", 3), ("rk", 1), ("rt", 2), ("rk", 2), ("rt", 3), ("rk", 3), ("list", 0)]
PLAN, BANK_USES = psum_plan()


def trunk(nc, x, w_in, w_out, rel_ext, vecs, w_route, norm_ffn, norm_final, w1, w3, w2, consts, out):
    ctx = ExitStack()
    with ctx:
        def sem(name):
            return ctx.enter_context(nc.semaphore(name))

        arena = ctx.enter_context(nc.sbuf_tensor("arena", [P, 50944], F32))
        idx = ctx.enter_context(nc.sbuf_tensor("idx", [P, 2, BLOCKS * NE], U32))
        idx_now = ctx.enter_context(nc.sbuf_tensor("idx_now", [P, 2, 2], U32))
        top_idx = ctx.enter_context(nc.sbuf_tensor("top_idx", [P, 16], U32))
        ctl = ctx.enter_context(nc.sbuf_tensor("ctl", [1, 32], I32))
        PS = [ctx.enter_context(nc.psum_tensor(f"bank{b}", [P, 512], F32)) for b in range(8)]

        def part(at, size):
            return arena[:, at:at + size]

        xs = part(0, 4096).rearrange("p (i d) -> p i d", i=NT)
        ring = [part(4096 + 4096 * b, 4096).rearrange("p (k n) -> p k n", k=KD) for b in range(4)]
        hT = part(20480, 4096).rearrange("p (k t) -> p k t", k=KD)
        wout = [ring[3], part(20480, 4096).rearrange("p (k n) -> p k n", k=KD)]
        wslot = [part(4096, WE), part(4096 + WE, WE), part(24576, WE), part(4096 + 2 * WE, WE)]
        R = 24576
        bcum = part(R, 2048)
        L = [part(R + 2048, 2048), part(R + 4096, 2048)]
        xn = [part(R + 2048, 1024), part(R + 3072, 1024)]
        kdT = part(R, 1536).rearrange("p (c n) -> p c n", c=3)
        bias = part(R, 4096).rearrange("p (h n) -> p h n", h=AH)
        prob = [part(R + 4096, 512), part(R + 4608, 512)]
        probT = [part(R + 5120, 512), part(R + 5632, 512)]
        Q, K, S = 30720, 32768, 34816
        qT = part(Q, 2048)
        kT = part(K, 2048)
        states = part(Q, 1536).rearrange("p (c n) -> p c n", c=3)
        bc_ffn, bc_fin = part(Q, 1024), part(Q + 1024, 1024)
        Sasm = part(S, 2048).rearrange("p (b t) -> p b t", t=P)
        mixT = [part(K + 1024 * b, 1024).rearrange("p (k t) -> p k t", k=KD) for b in range(2)]
        h2T = [part(S + 1024 * b, 1024).rearrange("p (k t) -> p k t", k=KD) for b in range(2)]
        acc = part(36864, 512)
        V_, AQ, AK, AV = 37376, 39424, 41472, 43520
        vtok = part(V_, 2048).rearrange("p (c n) -> p c n", c=NT)
        h2tok = [part(V_, 1024), part(V_ + 1024, 1024)]
        aqT = part(AQ, 2048).rearrange("p (b t) -> p b t", b=4)
        akT = part(AK, 2048).rearrange("p (b t) -> p b t", b=4)
        avt = part(AV, 2048).rearrange("p (c n) -> p c n", c=NT)
        onehot_r = [part(AQ + 384 * b, 128) for b in range(2)]
        onehot_v = [part(AQ + 384 * b + 128, 256) for b in range(2)]
        lst = part(AQ + 768, 256)
        lst2 = part(AQ + 1024, 256)
        xg = [part(AK, 1024), part(AK + 1024, 1024)]
        xgT = [part(AV, 1024), part(AV + 1024, 1024)]
        M = 45568
        mixed = part(M, 4096).rearrange("p (i n) -> p i n", i=NT)
        ysb = [part(M, 1024), part(M + 1024, 1024)]
        sil = [part(M + 2048, 256), part(M + 2304, 256)]
        hid = [part(M + 2560, 256), part(M + 2816, 256)]
        hidT = [part(M + 3072, 256), part(M + 3328, 256)]
        yin = [part(M, 2048).rearrange("p (k n) -> p k n", k=2), part(AK, 2048).rearrange("p (k n) -> p k n", k=2)]
        junk = part(AV, 1024)
        cst = part(49664, C_END)
        vec = part(49664 + C_END, V_END)
        wr = part(49664 + C_END + V_END, KD * 36).rearrange("p (k n) -> p k n", k=KD)
        sm = 49664 + C_END + V_END + KD * 36 + 4
        small_at = [sm]

        def small(n):
            at = small_at[0]
            small_at[0] += n
            assert small_at[0] <= 50944
            return part(at, n)

        ident, upper, ones_, iota = (cst[:, c:c + P] for c in (C_ID, C_UP, C_ONE, C_IOTA))

        ssq = small(NT)
        rstd = small(NT)
        lbw = small(16)
        ebl = small(16)
        oss, ors = small(16), small(16)
        mx, nmx, den = small(8), small(8), small(8)
        rden, ams, ars = small(8), small(8), small(8)
        ssq2, rstd2 = small(NT), small(NT)
        gate = small(8).rearrange("p (i k) -> p i k", k=2)
        slotpos = small(16)
        expid = small(8)
        fssq, frstd = small(NT), small(NT)
        RW = 36864
        lg, gpad, gm8, goh, em, em8 = part(RW, 36), part(RW + 36, 8), part(RW + 44, 8), part(RW + 52, 4), part(RW + 56, 32), part(RW + 88, 8)
        gex, gsum, t4 = part(RW + 96, 4), part(RW + 100, 1), part(RW + 104, 8)
        A12 = part(RW + 112, 64)
        A = part(RW + 176, 128).rearrange("p (i e) -> p i e", i=NT)
        rkj, rr, rq, rt3 = part(RW + 304, 32), part(RW + 336, 2), part(RW + 338, 2), part(RW + 340, 6)

        XN = nc.dram_tensor("h2_rows", [T, D], F32, kind="Internal").ap()
        Y = nc.dram_tensor("expert_rows", [2 * T, D], F32, kind="Internal").ap()

        x_in, cst_in, win_in = [sem(f"x_in{i}") for i in range(NT)], sem("cst_in"), [sem(f"win_in{b}") for b in range(4)]
        wout_in, bias_in, bc_in = [sem("wout_in0"), sem("wout_in1")], sem("bias_in"), sem("bc_in")
        filled = [sem(f"bank_filled{b}") for b in range(8)]
        taken = [sem(f"bank_taken{b}") for b in range(8)]
        act_step, dve_step, pool_step = sem("act_step"), sem("dve_step"), sem("pool_step")
        x_sq, x_rt, x_var, xn_done = sem("x_squares"), sem("x_root"), sem("x_variance"), sem("xn_done")
        zprep_a, zprep_v = sem("gate_terms_act"), sem("gate_terms_dve")
        lv_sub, lv_exp, lv_mul = sem("level_diff"), sem("level_exp"), sem("level_operands")
        sasm_done = sem("scores_placed")
        o_sq, o_rt, o_var = sem("o_squares"), sem("o_root"), sem("o_variance")
        pr_max, pr_exp, pt_pe = sem("row_max"), sem("probs_exp"), sem("probs_transposed")
        at_sq, at_var, at_rt, at_done = sem("att_squares"), sem("att_variance"), sem("att_root"), sem("att_done")
        x2_sq, x2_var, x2_rt = sem("x2_squares"), sem("x2_variance"), sem("x2_root")
        h2_done, h2_out = sem("h2_done"), [sem("h2_stored0"), sem("h2_stored1")]
        r_exp_in, r_exp, assign_done = sem("router_exp_in"), sem("router_exp"), sem("assign_done")
        oh_done, oh_read, idx_done = sem("onehots_done"), sem("onehots_read"), sem("idx_done")
        w_in_sem = [sem(f"expert_weights_in{s}") for s in range(WSLOTS)]
        gi_now, gi_out, gat, sca = sem("idx_column"), sem("y_idx_column"), [sem("gathered0"), sem("gathered1")], [sem("scattered0"), sem("scattered1")]
        m_xt, m_xtc = sem("xT_products"), sem("xT_copied")
        m_h, m_sil, m_hid, m_ht, m_htc = sem("h13_products"), sem("silu_done"), sem("hidden_done"), sem("hidT_products"), sem("hidT_copied")
        m_y, m_yc = sem("y_products"), sem("y_copied")
        column_ready = sem("column_ready")
        xg_zero = sem("gather_rows_zeroed")
        f_in, f_sum, f_sq, f_var, f_rt, f_done, out_sem = [sem("y_in0"), sem("y_in1")], sem("final_sum"), sem("final_squares"), sem("final_variance"), sem("final_root"), sem("final_rows"), sem("out_stored")

        def bank(name):
            return PS[PLAN[name][0]]

        def claim(pe, *name):
            b, n = PLAN[name]
            if n:
                pe.wait_ge(taken[b], n)
            return PS[b]

        def fill(ins, *name):
            ins.then_inc(filled[PLAN[name][0]], 1)

        def wait_filled(eng, *name):
            b, n = PLAN[name]
            eng.wait_ge(filled[b], n + 1)
            return PS[b]

        def take(ins, *name):
            ins.then_inc(taken[PLAN[name][0]], 1)

        def wait_taken(eng, *name):
            b, n = PLAN[name]
            eng.wait_ge(taken[b], n + 1)

        x_d = x.rearrange("(i p) d -> i p d", p=P)
        out_d = out.rearrange("(i p) d -> i p d", p=P)
        w_in_d = w_in.rearrange("(k p) n -> p k n", p=P)
        w_out_d = w_out.rearrange("(k p) n -> p k n", p=P)
        w1_d = w1.rearrange("e (p k) f -> e p (k f)", p=P)
        w3_d = w3.rearrange("e (p k) f -> e p (k f)", p=P)
        w2_d = w2.rearrange("e (p k) n -> e p (k n)", p=P)
        Y_d = Y.rearrange("(i p k) n -> i p k n", p=P, k=2)

        def expert_views(s):
            w = wslot[s]
            w13 = w[:, 0:2 * W13].rearrange("p (m k f) -> p m k f", m=2, k=KD)
            return w13, w[:, 2 * W13:WE].rearrange("p (j n) -> p j n", j=2)

        block = ctx.enter_context(nc.Block())

        @block.sync
        def _(sp):
            def win(g, n):
                b = GROUP_BUF[g]
                sp.dma_start(ring[b], w_in_d[:, :, GROUP_COL[g]:GROUP_COL[g] + 512]).then_inc(win_in[b], 16)

            sp.dma_start(xs[:, 0, :], x_d[0]).then_inc(x_in[0], 16)
            sp.dma_start(cst, consts).then_inc(cst_in, 16)
            sp.dma_start(vec, vecs).then_inc(cst_in, 16)
            sp.dma_start(wr, w_route).then_inc(cst_in, 16)
            for i in range(1, NT):
                sp.dma_start(xs[:, i, :], x_d[i]).then_inc(x_in[i], 16)
            for n in range(4):
                win(GROUPS[n], n)
            wait_filled(sp, "f", 3)
            win("aq", 4)
            wait_filled(sp, "q", 3)
            win("av", 5)
            wait_filled(sp, "v", 3)
            win("g", 6)
            wait_filled(sp, "ak", 3)
            sp.dma_start(wout[0], w_out_d[:, :, 0:512]).then_inc(wout_in[0], 16)

            def expert(s, e, sem_):
                sp.dma_start(wslot[s][:, 0:W13], w1_d[e]).then_inc(sem_, 16)
                sp.dma_start(wslot[s][:, W13:2 * W13], w3_d[e]).then_inc(sem_, 16)
                sp.dma_start(wslot[s][:, 2 * W13:WE], w2_d[e]).then_inc(sem_, 16)

            wait_filled(sp, "av", 3)
            expert(0, 0, w_in_sem[0])
            wait_filled(sp, "g", 3)
            sp.dma_start(wout[1], w_out_d[:, :, 512:1024]).then_inc(wout_in[1], 16)
            wait_taken(sp, "delta", 2)
            wait_filled(sp, "o", 3)
            wait_taken(sp, "kT", 2)
            bsrc = bass.AP(rel_ext.tensor, 0, [[1, P], [639, AH], [1, 512]])
            sp.dma_start(bias, bsrc).then_inc(bias_in, 16)
            sp.dma_start(bc_ffn, norm_ffn.partition_broadcast(P)).then_inc(bc_in, 16)
            sp.dma_start(bc_fin, norm_final.partition_broadcast(P)).then_inc(bc_in, 16)
            expert(1, 1, w_in_sem[1])
            sp.wait_ge(at_done, NT)
            expert(2, 2, w_in_sem[2])
            wait_filled(sp, "out", 3, 1)
            expert(3, 3, w_in_sem[3])
            with sp.Fori(0, NE // WSLOTS - 1) as r:
                for s in range(WSLOTS):
                    sp.wait_ge(m_y, r * WSLOTS + s + 1)
                    expert(s, r * WSLOTS + (WSLOTS + s), w_in_sem[s])
            sp.wait_ge(idx_done, 2)
            n_ovf = sp.value_load(ctl[0:1, 0:1], min_val=0, max_val=OVF_MAX)
            with sp.If(n_ovf > 0):
                with sp.Fori(0, n_ovf) as j:
                    e = sp.value_load(ctl[0:1, bass.ds(j + 16, 1)], min_val=0, max_val=NE - 1)
                    sp.wait_ge(m_y, j + NE)
                    sp.dma_start(wslot[0][:, 0:W13], w1_d[bass.ds(e, 1)].rearrange("a p n -> (a p) n")).then_inc(w_in_sem[0], 16)
                    sp.dma_start(wslot[0][:, W13:2 * W13], w3_d[bass.ds(e, 1)].rearrange("a p n -> (a p) n")).then_inc(w_in_sem[0], 16)
                    sp.dma_start(wslot[0][:, 2 * W13:WE], w2_d[bass.ds(e, 1)].rearrange("a p n -> (a p) n")).then_inc(w_in_sem[0], 16)
            sp.wait_ge(pool_step, 2)
            for i in range(NT):
                if i >= 2:
                    sp.wait_ge(f_sum, i - 1)
                sp.dma_start(yin[i % 2], Y_d[i]).then_inc(f_in[i % 2], 16)
            for i in range(NT):
                sp.wait_ge(f_done, i + 1)
                sp.dma_start(out_d[i], xs[:, i, :]).then_inc(out_sem, 16)
            sp.wait_ge(out_sem, 16 * NT)

        @block.gpsimd
        def _(pool):
            pool.memset(acc, 1.0).then_inc(pool_step, 1)
            pool.wait_ge(pool_step, 1)
            pool.memset(acc.rearrange("p (c t) -> p c t", t=P)[:, :, 0:1], 0.0).then_inc(xg_zero, 1)
            pool.memset(Sasm, 0.0).then_inc(xg_zero, 1)
            wait_filled(pool, "pv", 3)
            for b in range(2):
                pool.memset(xg[b], 0.0).then_inc(xg_zero, 1)
            pool.wait_ge(xg_zero, 4)
            pool.wait_ge(idx_done, 1)
            for b in range(2):
                pool.wait_ge(h2_out[b], 16 * NT // 2)

            last_token, last_assignment = pool.to_reg(T - 1), pool.to_reg(2 * T - 1)

            def gather(b, col, ready):
                pool.tensor_copy(idx_now[:, b, 0:1], idx[:, 0, col]).then_inc(gi_now, 1)
                pool.wait_ge(gi_now, ready)
                pool.sem_inc(column_ready, 1)
                pool.indirect_dma_start(xg[b], None, XN, bass.IndirectOffsetOnAxis(ap=idx_now[:, b, 0:1], axis=0),
                                        bounds_check=last_token, oob_is_err=False).then_inc(gat[b], 16)

            def scatter(b, col, ready):
                pool.tensor_copy(idx_now[:, b, 1:2], idx[:, 1, col]).then_inc(gi_out, 1)
                pool.wait_ge(gi_out, ready)
                pool.sem_inc(column_ready, 1)
                pool.indirect_dma_start(Y, bass.IndirectOffsetOnAxis(ap=idx_now[:, b, 1:2], axis=0), ysb[b], None,
                                        bounds_check=last_assignment, oob_is_err=False).then_inc(sca[b], 16)

            gather(0, slice(0, 1), 1)
            gather(1, slice(1, 2), 2)
            with pool.Fori(0, NE // 2 - 1) as r:
                for b in range(2):
                    pool.wait_ge(m_xt, r * 2 + b + 1)
                    pool.wait_ge(gat[b], r * 16 + 16)
                    gather(b, bass.ds(r * 2 + (2 + b), 1), r * 2 + (3 + b))
                    pool.wait_ge(m_yc, r * 4 + 2 * b + 2)
                    scatter(b, bass.ds(r * 2 + b, 1), r * 2 + (1 + b))
                    pool.wait_ge(sca[b], r * 16 + 16)
            for b in range(2):
                pool.wait_ge(m_yc, 2 * (NE - 2 + b) + 2)
                scatter(b, slice(NE - 2 + b, NE - 1 + b), NE - 1 + b)
                pool.wait_ge(sca[b], 8 * NE)
            pool.wait_ge(idx_done, 2)
            n_ovf = pool.value_load(ctl[0:1, 0:1], min_val=0, max_val=OVF_MAX)
            with pool.If(n_ovf > 0):
                with pool.Fori(0, n_ovf) as j:
                    c = pool.value_load(ctl[0:1, bass.ds(j + 8, 1)], min_val=NE, max_val=BLOCKS * NE - 1)
                    gather(0, bass.ds(c, 1), j + NE + 1)
                    pool.wait_ge(m_yc, j * 2 + 2 * NE + 2)
                    scatter(0, bass.ds(c, 1), j + NE + 1)
                    pool.wait_ge(sca[0], j * 16 + (8 * NE + 16))
            pool.memset(idx_now[:, 0, 0:1], 0).then_inc(pool_step, 1)

        @block.tensor
        def _(pe):
            pe.wait_ge(cst_in, 48)
            for i in range(NT):
                pe.wait_ge(xn_done, i + 1)
                for half in range(2):
                    ps = claim(pe, "xT", i, half)
                    for c in range(4):
                        last = pe.transpose(ps[:, c * P:(c + 1) * P], xn[i % 2][:, (4 * half + c) * P:(4 * half + c + 1) * P], ident)
                    fill(last, "xT", i, half)

            def project(g, j):
                ps = claim(pe, g, j)
                w = ring[GROUP_BUF[g]]
                for k in range(KD):
                    if g in ("f", "q", "ak", "aq"):
                        last = pe.matmul(ps[:], w[:, k, j * P:(j + 1) * P], hT[:, k, :], start=k == 0, stop=k == KD - 1)
                    else:
                        last = pe.matmul(ps[:], hT[:, k, j * P:(j + 1) * P], w[:, k, :], start=k == 0, stop=k == KD - 1)
                fill(last, g, j)

            def begin(g):
                n = GROUPS.index(g)
                pe.wait_ge(win_in[GROUP_BUF[g]], 32 if n >= 4 else 16)

            for i in range(NT):
                wait_taken(pe, "xT", i, 0)
                wait_taken(pe, "xT", i, 1)
            for g in ("f", "q", "v", "ak"):
                begin(g)
                for j in range(4):
                    project(g, j)

            def small_blocks(ps, lhs, rhs):
                for hc in range(16):
                    for j in range(4):
                        at = hc * P + 32 * j
                        last = pe.matmul(ps[32 * j:32 * j + 32, 32 * hc:32 * hc + 32], lhs[:, at:at + 32], rhs[:, at:at + 32],
                                         start=True, stop=True)
                return last

            ps = claim(pe, "diag")
            pe.wait_ge(zprep_a, 8)
            for j in range(4):
                wait_taken(pe, "q", j)
            fill(small_blocks(ps, kT, qT), "diag")

            def level(li):
                pe.wait_ge(lv_mul, li + 1)
                buf = L[li % 2]
                if li == 0:
                    for half in range(2):
                        ps = claim(pe, "level", 0, half)
                        for n in range(8):
                            at = (8 * half + n) * P
                            last = pe.matmul(ps[0:64, 64 * n:64 * n + 64], buf[:, at:at + 64], buf[:, at + 64:at + 128],
                                             start=True, stop=True)
                        fill(last, "level", 0, half)
                elif li == 1:
                    ps = claim(pe, "level", 1, 0)
                    for hc in range(16):
                        for j in range(2):
                            at = hc * P + 64 * j
                            last = pe.matmul(ps[64 * j:64 * j + 32, 32 * hc:32 * hc + 32], buf[:, at:at + 32], buf[:, at + 32:at + 64],
                                             start=True, stop=True)
                    fill(last, "level", 1, 0)
                else:
                    fill(small_blocks(claim(pe, "level", li, 0), buf, buf), "level", li, 0)

            begin("aq")
            for li in range(7):
                if li == 4:
                    begin("av")
                if li < 4:
                    project("aq", li)
                else:
                    project("av", li - 4)
                level(li)
            project("av", 3)
            pe.wait_ge(lv_mul, 9)
            for c in range(3):
                ps = claim(pe, "kT", c)
                for h in range(RH):
                    last = pe.transpose(ps[:, h * P:(h + 1) * P], L[0][:, (4 * h + c) * P:(4 * h + c + 1) * P], ident)
                fill(last, "kT", c)
            begin("g")
            project("g", 0)
            for c in range(3):
                ps = claim(pe, "delta", c)
                wait_taken(pe, "kT", c)
                for h in range(RH):
                    last = pe.matmul(ps[:, h * P:(h + 1) * P], kdT[:, c, h * P:(h + 1) * P], vtok[:, c, h * P:(h + 1) * P],
                                     start=True, stop=True)
                fill(last, "delta", c)
            project("g", 1)

            def rec_out(c):
                ps = claim(pe, "o", c)
                pe.wait_ge(sasm_done, 1)
                if c:
                    wait_taken(pe, "delta", c - 1)
                for h in range(RH):
                    last = pe.matmul(ps[:, h * P:(h + 1) * P], Sasm[:, 4 * h + c, :], vtok[:, c, h * P:(h + 1) * P],
                                     start=True, stop=c == 0)
                    if c:
                        at = (4 * h + c) * P
                        last = pe.matmul(ps[:, h * P:(h + 1) * P], L[1][:, at:at + P], states[:, c - 1, h * P:(h + 1) * P],
                                         start=False, stop=True)
                fill(last, "o", c)

            rec_out(0)
            rec_out(1)
            project("g", 2)
            rec_out(2)
            rec_out(3)
            project("g", 3)

            for kind, i in STEPS:
                if kind == "att":
                    n = P * (i + 1)
                    for t in range(AH + 2):
                        if t < AH:
                            ps = claim(pe, "score", i, t)
                            o = 64 * (t % 2)
                            fill(pe.matmul(ps[:, 0:n], aqT[o:o + 64, t // 2, i * P:(i + 1) * P], akT[o:o + 64, t // 2, 0:n],
                                           start=True, stop=True), "score", i, t)
                        if 1 <= t <= AH:
                            h = t - 1
                            ps = claim(pe, "pT", i, h)
                            pe.wait_ge(pr_exp, AH * i + h + 1)
                            for j in range(i + 1):
                                last = pe.transpose(ps[:, j * P:(j + 1) * P], prob[h % 2][:, j * P:(j + 1) * P], ident)
                            fill(last, "pT", i, h)
                        if t >= 2:
                            h = t - 2
                            if h == 0:
                                pv = claim(pe, "pv", i)
                            wait_taken(pe, "pT", i, h)
                            for j in range(i + 1):
                                last = pe.matmul(pv[:, h * AD:(h + 1) * AD], probT[h % 2][:, j * P:(j + 1) * P],
                                                 avt[:, j, h * AD:(h + 1) * AD], start=j == 0, stop=j == i)
                            if h < AH - 1:
                                last.then_inc(pt_pe, 1)
                            else:
                                fill(last, "pv", i)
                if kind == "mo":
                    wait_taken(pe, "o", i)
                    pe.wait_ge(at_done, i + 1)
                    for half in range(2):
                        ps = claim(pe, "mT", i, half)
                        for c in range(4):
                            k = 4 * half + c
                            last = pe.transpose(ps[:, c * P:(c + 1) * P], mixed[:, i, k * P:(k + 1) * P], ident)
                        fill(last, "mT", i, half)
                    wait_taken(pe, "mT", i, 0)
                    wait_taken(pe, "mT", i, 1)
                    for half in range(2):
                        if i == 0:
                            pe.wait_ge(wout_in[half], 16)
                        ps = claim(pe, "out", i, half)
                        for k in range(KD):
                            last = pe.matmul(ps[:], mixT[i % 2][:, k, :], wout[half][:, k, :], start=k == 0, stop=k == KD - 1)
                        fill(last, "out", i, half)
                if kind == "rt":
                    pe.wait_ge(h2_done, i + 1)
                    for half in range(2):
                        ps = claim(pe, "hT2", i, half)
                        for c in range(4):
                            k = 4 * half + c
                            last = pe.transpose(ps[:, c * P:(c + 1) * P], h2tok[i % 2][:, k * P:(k + 1) * P], ident)
                        fill(last, "hT2", i, half)
                    wait_taken(pe, "hT2", i, 0)
                    wait_taken(pe, "hT2", i, 1)
                    ps = claim(pe, "logit", i)
                    for k in range(KD):
                        last = pe.matmul(ps[:, 0:36], h2T[i % 2][:, k, :], wr[:, k, :], start=k == 0, stop=k == KD - 1)
                    fill(last, "logit", i)
                if kind == "rk":
                    pe.wait_ge(assign_done, i + 1)
                    ps = claim(pe, "rank", i)
                    last = pe.matmul(ps[:, 0:NE], upper, A[:, i, :], start=True, stop=i == 0)
                    for j in range(i):
                        last = pe.matmul(ps[:, 0:NE], ones_, A[:, j, :], start=False, stop=j == i - 1)
                    fill(last, "rank", i)
                if kind == "list":
                    ps = claim(pe, "list")
                    for n in range(2 * NT):
                        pe.wait_ge(oh_done, n + 1)
                        last = pe.matmul(ps[:, 0:2 * P], onehot_r[n % 2], onehot_v[n % 2], start=n == 0, stop=n == 2 * NT - 1)
                        if n < 2 * NT - 1:
                            last.then_inc(oh_read, 1)
                    fill(last, "list")
            for b in range(8):
                pe.wait_ge(taken[b], BANK_USES[b])

            def x_turn(b, g):
                pe.wait_ge(gat[b], g)
                for half in range(2):
                    for c in range(4):
                        k = 4 * half + c
                        last = pe.transpose(PS[half][:, c * P:(c + 1) * P], xg[b][:, k * P:(k + 1) * P], ident)
                last.then_inc(m_xt, 1)

            def up(b, s, w_count, n):
                w13, _ = expert_views(s)
                pe.wait_ge(w_in_sem[s], w_count)
                pe.wait_ge(m_xtc, n)
                xt = xgT[b].rearrange("p (k t) -> p k t", k=KD)
                for k in range(KD):
                    last = pe.matmul(PS[2 + b][:], xt[:, k, :], w13[:, :, k, :], start=k == 0, stop=k == KD - 1)
                last.then_inc(m_h, 1)

            def h_turn(b, n):
                pe.wait_ge(m_hid, n)
                for j in range(2):
                    last = pe.transpose(PS[4 + b][:, j * P:(j + 1) * P], hid[b][:, j * P:(j + 1) * P], ident)
                last.then_inc(m_ht, 1)

            def down(b, s, n, ycopied):
                _, w2v = expert_views(s)
                pe.wait_ge(m_htc, n)
                if ycopied is not None:
                    pe.wait_ge(m_yc, ycopied)
                for half in range(2):
                    for j in range(2):
                        last = pe.matmul(PS[6 + half][:], hidT[b][:, j * P:(j + 1) * P], w2v[:, j, half * 512:(half + 1) * 512],
                                         start=j == 0, stop=j == 1)
                last.then_inc(m_y, 1)

            x_turn(0, 16)
            up(0, 0, 48, 2)
            x_turn(1, 16)
            h_turn(0, 1)

            for n in range(1, 4):
                b, s = n % 2, n % 4
                up(b, s, 48, 2 * n + 2)
                down(1 - b, s - 1, n, 2 * n - 2 if n > 1 else None)
                x_turn(1 - b, 16 * ((n + 1) // 2 + 1))
                h_turn(b, n + 1)
            with pe.Fori(1, NE // WSLOTS - 1) as r:
                for s in range(WSLOTS):
                    b = s % 2
                    up(b, s, r * 48 + 48, r * 8 + (2 * s + 2))
                    down(1 - b, (s - 1) % WSLOTS, r * 4 + s, r * 8 + (2 * s - 2))
                    x_turn(1 - b, r * 32 + 16 * ((s + 1) // 2 + 1))
                    h_turn(b, r * 4 + (s + 1))
            for n in range(NE - 4, NE):
                b, s = n % 2, n % 4
                up(b, s, 48 * (NE // 4), 2 * n + 2)
                down(1 - b, (s - 1) % 4, n, 2 * n - 2)
                if n < NE - 1:
                    x_turn(1 - b, 16 * ((n + 1) // 2 + 1))
                h_turn(b, n + 1)
            down(1, 3, NE, 2 * NE - 2)
            pe.wait_ge(idx_done, 2)
            n_ovf = pe.value_load(ctl[0:1, 0:1], min_val=0, max_val=OVF_MAX)
            with pe.If(n_ovf > 0):
                with pe.Fori(0, n_ovf) as j:
                    x_turn(0, j * 16 + (8 * NE + 16))
                    up(0, 0, j * 48 + (48 * (NE // 4) + 48), j * 2 + (2 * NE + 2))
                    h_turn(0, j + (NE + 1))
                    down(0, 0, j + (NE + 1), j * 2 + 2 * NE)

        @block.scalar
        def _(act):
            def a(out_, in_, f, **k):
                return act.activation(out_, in_, f, **k)

            steps = [0]

            def chain(ins):
                ins.then_inc(act_step, 1)
                steps[0] += 1
                act.wait_ge(act_step, steps[0])

            def copy_pt(i, h):
                n = P * (i + 1)
                wait_filled(act, "pT", i, h)
                k = (AH - 1) * i + h - 1
                if h >= 2:
                    act.wait_ge(pt_pe, k)
                elif i:
                    wait_filled(act, "pv", i - 1)
                take(a(probT[h % 2][:, 0:n], bank(("pT", i, h))[:, 0:n], ACT.Copy), "pT", i, h)

            for i in range(NT):
                act.wait_ge(x_in[i], 16)
                if i >= 1:
                    act.wait_ge(x_sq, i)
                a(part(AQ, 1024), xs[:, i, :], ACT.Square, accum_out=ssq[:, i:i + 1]).then_inc(x_sq, 1)
                act.wait_ge(x_var, i + 1)
                a(rstd[:, i:i + 1], rstd[:, i:i + 1], ACT.Sqrt).then_inc(x_rt, 1)
            act.wait_ge(zprep_v, 1)
            a(lbw[:, 4:8], lbw[:, 0:4], ACT.Exp).then_inc(zprep_a, 1)
            act.wait_ge(zprep_v, 2)
            a(lbw[:, 12:16], lbw[:, 8:12], ACT.Ln, scale=-1.0, bias=1.0).then_inc(zprep_a, 1)
            for j in range(4):
                wait_filled(act, "q", j)
                take(a(qT[:, j * 512:(j + 1) * 512], bank(("q", j))[:], ACT.Silu), "q", j)

            def copy_v(j):
                wait_filled(act, "v", j)
                take(a(vtok[:, j, :], bank(("v", j))[:], ACT.Copy), "v", j)

            def copy_ak(j):
                wait_filled(act, "ak", j)
                take(a(akT[:, j, :], bank(("ak", j))[:], ACT.Copy), "ak", j)

            for j in range(4):
                wait_taken(act, "f", j)
            a(L[0], bcum, ACT.Relu, scale=-1.0).then_inc(zprep_a, 1)
            copy_v(0)
            act.wait_ge(zprep_v, 3)
            chain(a(L[1], L[1], ACT.Exp, scale=-1.0))
            copy_v(1)
            a(L[1], L[1], ACT.Ln, bias=1.0).then_inc(zprep_a, 1)
            copy_v(2)
            act.wait_ge(zprep_v, 5)
            act.wait_ge(zprep_a, 2)
            for h in range(RH):
                a(kT[:, h * 512:(h + 1) * 512], L[1][:, h * 512:(h + 1) * 512], ACT.Exp, scale=-1.0,
                  bias=lbw[:, 12 + h:13 + h]).then_inc(zprep_a, 1)
            copy_v(3)
            act.wait_ge(zprep_v, 6)
            chain(a(L[1], L[1], ACT.Exp, scale=-1.0))
            copy_ak(0)
            for h in range(RH):
                ins = a(L[1][:, h * 512:(h + 1) * 512], L[1][:, h * 512:(h + 1) * 512], ACT.Ln,
                        scale=lbw[:, 8 + h:9 + h], bias=1.0)
            ins.then_inc(zprep_a, 1)
            copy_ak(1)
            for li in range(2):
                act.wait_ge(lv_sub, li + 1)
                a(L[li], L[li], ACT.Exp).then_inc(lv_exp, 1)
            copy_ak(2)
            copy_ak(3)
            for li in range(7):
                if li < 4:
                    wait_filled(act, "aq", li)
                    take(a(aqT[:, li, :], bank(("aq", li))[:], ACT.Copy, scale=AD ** -0.5), "aq", li)
                else:
                    wait_filled(act, "av", li - 4)
                    take(a(avt[:, li - 4, :], bank(("av", li - 4))[:], ACT.Copy), "av", li - 4)
                if li + 2 < 7:
                    act.wait_ge(lv_sub, li + 3)
                    a(L[li % 2], L[li % 2], ACT.Exp).then_inc(lv_exp, 1)
                elif li + 2 == 7:
                    wait_filled(act, "level", 5, 0)
                    a(L[1], bcum, ACT.Exp).then_inc(lv_exp, 1)
                else:
                    act.wait_ge(lv_sub, 8)
                    a(ebl, bcum.rearrange("p (b t) -> p b t", t=P)[:, :, P - 1], ACT.Exp).then_inc(act_step, 1)
                    steps[0] += 1
                    a(L[0], L[0], ACT.Exp).then_inc(lv_exp, 1)
            wait_filled(act, "av", 3)
            take(a(avt[:, 3, :], bank(("av", 3))[:], ACT.Copy), "av", 3)
            for c in range(3):
                wait_filled(act, "kT", c)
                take(a(kdT[:, c, :], bank(("kT", c))[:], ACT.Copy), "kT", c)

            def silu_g(i):
                wait_filled(act, "g", i)
                take(a(mixed[:, i, 0:512], bank(("g", i))[:], ACT.Silu), "g", i)

            silu_g(0)
            silu_g(1)
            silu_g(2)

            def squares(c):
                wait_filled(act, "o", c)
                for h in range(RH):
                    if c + h:
                        act.wait_ge(o_sq, RH * c + h)
                    a(part(K, 128), bank(("o", c))[:, h * P:(h + 1) * P], ACT.Square,
                      accum_out=oss[:, 4 * c + h:4 * c + h + 1]).then_inc(o_sq, 1)

            for c in range(NT):
                squares(c)
            silu_g(3)
            act.wait_ge(o_var, 1)
            a(ors, ors, ACT.Sqrt).then_inc(o_rt, 1)

            for kind, i in STEPS:
                if kind == "att":
                    for h in range(AH):
                        act.wait_ge(pr_max, AH * i + h + 1)
                        n = P * (i + 1)
                        a(prob[h % 2][:, 0:n], prob[h % 2][:, 0:n], ACT.Exp, bias=nmx[:, h:h + 1],
                          accum_out=den[:, h:h + 1]).then_inc(pr_exp, 1)
                        if h >= 1:
                            copy_pt(i, h - 1)
                    copy_pt(i, AH - 1)
                    wait_taken(act, "pv", i)
                    a(prob[0], mixed[:, i, 512:1024], ACT.Square).then_inc(at_sq, 1)
                    act.wait_ge(at_var, i + 1)
                    a(ars, ars, ACT.Sqrt).then_inc(at_rt, 1)
                if kind == "mo":
                    wait_taken(act, "out", i, 0)
                    wait_taken(act, "out", i, 1)
                    if i >= 1:
                        act.wait_ge(x2_sq, i)
                    a(part(M + 1024 * i, 1024), xs[:, i, :], ACT.Square, accum_out=ssq2[:, i:i + 1]).then_inc(x2_sq, 1)
                    act.wait_ge(x2_var, i + 1)
                    a(rstd2[:, i:i + 1], rstd2[:, i:i + 1], ACT.Sqrt).then_inc(x2_rt, 1)
                    act.wait_ge(h2_done, i + 1)
                    act.dma_start(XN[i * P:(i + 1) * P, :], h2tok[i % 2]).then_inc(h2_out[i % 2], 16)
                if kind == "rt":
                    for half in range(2):
                        wait_filled(act, "hT2", i, half)
                        take(a(h2T[i % 2].rearrange("p k t -> p (k t)")[:, half * 512:(half + 1) * 512], bank(("hT2", i, half))[:], ACT.Copy),
                             "hT2", i, half)
                    act.wait_ge(r_exp_in, 2 * i + 1)
                    a(gex, gex, ACT.Exp, accum_out=gsum).then_inc(r_exp, 1)
                    act.wait_ge(r_exp_in, 2 * i + 2)
                    a(t4[:, 1:2], t4[:, 0:1], ACT.Exp).then_inc(r_exp, 1)

            def x_copy(b, n):
                act.wait_ge(m_xt, n)
                a(xgT[b][:, 512:1024], PS[1][:], ACT.Copy).then_inc(m_xtc, 1)

            def silu(b, n):
                act.wait_ge(m_h, n)
                a(sil[b], PS[2 + b][:, 0:FF], ACT.Silu).then_inc(m_sil, 1)

            def y_copy(b, n, scattered):
                act.wait_ge(m_y, n)
                if scattered is not None:
                    act.wait_ge(sca[b], scattered)
                a(ysb[b][:, 0:512], PS[6][:], ACT.Copy).then_inc(m_yc, 1)

            x_copy(0, 1)
            silu(0, 1)
            x_copy(1, 2)
            for n in range(1, 4):
                b = n % 2
                silu(b, n + 1)
                y_copy(1 - b, n, None if n < 3 else 16)
                x_copy(1 - b, n + 2)
            with act.Fori(1, NE // WSLOTS - 1) as r:
                for s in range(WSLOTS):
                    b = s % 2
                    silu(b, r * 4 + (s + 1))
                    y_copy(1 - b, r * 4 + s, r * 32 + 16 * ((s - 1) // 2))
                    x_copy(1 - b, r * 4 + (s + 2))
            for n in range(NE - 4, NE):
                b = n % 2
                silu(b, n + 1)
                y_copy(1 - b, n, 16 * ((n - 1) // 2))
                if n < NE - 1:
                    x_copy(1 - b, n + 2)
            y_copy(1, NE, 16 * (NE // 2 - 1))
            act.wait_ge(idx_done, 2)
            n_ovf = act.value_load(ctl[0:1, 0:1], min_val=0, max_val=OVF_MAX)
            with act.If(n_ovf > 0):
                with act.Fori(0, n_ovf) as j:
                    x_copy(0, j + (NE + 1))
                    silu(0, j + (NE + 1))
                    y_copy(0, j + (NE + 1), j * 16 + 8 * NE)
            for i in range(NT):
                act.wait_ge(f_sum, i + 1)
                if i:
                    act.wait_ge(f_sq, i)
                a(junk, xs[:, i, :], ACT.Square, accum_out=fssq[:, i:i + 1]).then_inc(f_sq, 1)
                act.wait_ge(f_var, i + 1)
                a(frstd[:, i:i + 1], frstd[:, i:i + 1], ACT.Sqrt).then_inc(f_rt, 1)

        @block.vector
        def _(v):
            steps = [0]

            def chain(ins):
                ins.then_inc(dve_step, 1)
                steps[0] += 1
                v.wait_ge(dve_step, steps[0])

            def variance(out_, in_, n, done):
                v.tensor_scalar(out_, in_, 1.0 / n, EPS, ALU.mult, ALU.add).then_inc(done, 1)

            v.wait_ge(cst_in, 48)
            for i in range(NT):
                v.wait_ge(x_sq, i + 1)
                variance(rstd[:, i:i + 1], ssq[:, i:i + 1], D, x_var)
                v.wait_ge(x_rt, i + 1)
                chain(v.reciprocal(rstd[:, i:i + 1], rstd[:, i:i + 1]))
                if i >= 2:
                    wait_filled(v, "xT", i - 2, 1)
                v.tensor_scalar(xn[i % 2], xs[:, i, :], rstd[:, i:i + 1], None, ALU.mult).then_inc(xn_done, 1)
                for half in range(2):
                    ps = wait_filled(v, "xT", i, half)
                    w = vec[:, V_MIX + 4 * half:V_MIX + 4 * half + 4].unsqueeze(2).to_broadcast([P, 4, P])
                    take(v.tensor_tensor(hT[:, 4 * half:4 * half + 4, i * P:(i + 1) * P],
                                         ps[:].rearrange("p (c t) -> p c t", c=4), w, ALU.mult), "xT", i, half)
            lb_in = vec[:, V_LB:V_LB + 4]
            v.tensor_tensor(lbw[:, 0:4], lb_in, lb_in, ALU.subtract).then_inc(zprep_v, 1)
            v.wait_ge(zprep_a, 1)
            chain(v.reciprocal(lbw[:, 8:12], lbw[:, 4:8]))
            chain(v.tensor_tensor(lbw[:, 8:12], lbw[:, 8:12], lbw[:, 4:8], ALU.mult))
            v.tensor_tensor(lbw[:, 8:12], lbw[:, 8:12], lbw[:, 8:12], ALU.subtract).then_inc(zprep_v, 1)
            for j in range(4):
                ps = wait_filled(v, "f", j)
                take(v.tensor_copy(bcum[:, j * 512:(j + 1) * 512], ps[:]), "f", j)
            for j in range(4):
                wait_taken(v, "f", j)
            v.wait_ge(zprep_a, 3)
            v.scalar_tensor_tensor(L[1], L[0], 2.0, bcum, ALU.mult, ALU.add).then_inc(zprep_v, 1)
            v.wait_ge(zprep_a, 4)
            v.tensor_tensor(L[0], L[0], L[1], ALU.add).then_inc(zprep_v, 1)
            v.wait_ge(zprep_v, 4)
            v.tensor_tensor(L[1], bcum, L[0], ALU.add).then_inc(zprep_v, 1)
            v.wait_ge(zprep_a, 8)
            v.tensor_scalar(L[1], bcum, -80.0, None, ALU.max).then_inc(zprep_v, 1)
            v.wait_ge(zprep_a, 9)
            chain(v.tensor_tensor(L[1], L[1], L[0], ALU.subtract))
            v.wait_ge(xg_zero, 1)
            for h in range(RH):
                ins = v.tensor_tensor_scan(bcum[:, h * 512:(h + 1) * 512], acc, L[1][:, h * 512:(h + 1) * 512], 0.0, ALU.mult, ALU.add)
            chain(ins)

            bv = bcum.rearrange("p (n t) -> p n t", t=P)

            def diff(li):
                hs = HALVES[li]
                b4 = bcum.rearrange("p (n s t) -> p n s t", s=2, t=hs)
                l4 = L[li % 2].rearrange("p (n s t) -> p n s t", s=2, t=hs)
                mid = b4[:, :, 0, hs - 1:hs].to_broadcast([P, 1024 // hs, hs])
                v.tensor_tensor(l4[:, :, 0, :], mid, b4[:, :, 0, :], ALU.subtract)
                v.tensor_tensor(l4[:, :, 1, :], b4[:, :, 1, :], mid, ALU.subtract).then_inc(lv_sub, 1)

            def operands(li):
                hs = HALVES[li]
                l4, k4, q4 = (t.rearrange("p (n s t) -> p n s t", s=2, t=hs) for t in (L[li % 2], kT, qT))
                v.wait_ge(lv_exp, li + 1)
                v.tensor_tensor(l4[:, :, 0, :], l4[:, :, 0, :], k4[:, :, 0, :], ALU.mult)
                v.tensor_tensor(l4[:, :, 1, :], l4[:, :, 1, :], q4[:, :, 1, :], ALU.mult).then_inc(lv_mul, 1)

            def masked(ps, m):
                w = cst[:, C_MASK + 32 * m:C_MASK + 32 * m + 32].unsqueeze(1).to_broadcast([P, 16, 32])
                return ps[:].rearrange("p (b t) -> p b t", t=32), w

            acc3 = acc.rearrange("p (b t) -> p b t", t=32)
            tmp3 = part(M, 512).rearrange("p (b t) -> p b t", t=32)

            def place(li):
                if li == 0:
                    for half in range(2):
                        ps = wait_filled(v, "level", 0, half)
                        take(v.tensor_copy(Sasm[0:64, 8 * half:8 * half + 8, 64:128],
                                           ps[0:64, :].rearrange("p (b t) -> p b t", t=64)), "level", 0, half)
                elif li == 1:
                    ps = wait_filled(v, "level", 1, 0)
                    v.tensor_copy(Sasm[0:32, :, 32:64], ps[0:32, :].rearrange("p (b t) -> p b t", t=32))
                    take(v.tensor_copy(Sasm[64:96, :, 96:128], ps[64:96, :].rearrange("p (b t) -> p b t", t=32)), "level", 1, 0)
                else:
                    ps = wait_filled(v, "level", li, 0)
                    take(v.tensor_tensor(tmp3, *masked(ps, li - 2), ALU.mult), "level", li, 0)
                    wait_taken(v, "level", li, 0)
                    chain(v.tensor_tensor(acc3, acc3, tmp3, ALU.add))

            diff(0)
            diff(1)
            v.wait_ge(xg_zero, 2)
            ps = wait_filled(v, "diag")
            take(v.tensor_tensor(acc3, *masked(ps, 5), ALU.mult), "diag")
            wait_taken(v, "diag")
            for j in range(4):
                wait_taken(v, "q", j)
            operands(0)
            operands(1)
            for li in range(2, 7):
                wait_filled(v, "level", li - 2, 1 if li == 2 else 0)
                diff(li)
                place(li - 2)
                operands(li)
            place(5)
            v.wait_ge(lv_exp, 8)
            v.tensor_tensor(L[1], L[1], qT, ALU.mult).then_inc(lv_mul, 1)
            wait_filled(v, "level", 6, 0)
            last_b = bv[:, :, P - 1:P].to_broadcast([P, 16, P])
            v.tensor_tensor(L[0].rearrange("p (n t) -> p n t", t=P), last_b, bv, ALU.subtract).then_inc(lv_sub, 1)
            place(6)
            for j in range(4):
                ins = v.tensor_copy(Sasm[32 * j:32 * j + 32, :, 32 * j:32 * j + 32], acc3[32 * j:32 * j + 32])
            ins.then_inc(sasm_done, 1)
            v.wait_ge(lv_exp, 9)
            v.tensor_tensor(L[0], L[0], kT, ALU.mult).then_inc(lv_mul, 1)
            v.wait_ge(lv_mul, 9)
            for c in range(3):
                ps = wait_filled(v, "delta", c)
                if c == 0:
                    take(v.tensor_copy(states[:, 0, :], ps[:]), "delta", 0)
                else:
                    for h in range(RH):
                        ins = v.scalar_tensor_tensor(states[:, c, h * P:(h + 1) * P], states[:, c - 1, h * P:(h + 1) * P],
                                                     ebl[:, 4 * h + c:4 * h + c + 1], ps[:, h * P:(h + 1) * P], ALU.mult, ALU.add)
                    take(ins, "delta", c)
                wait_taken(v, "delta", c)
            v.wait_ge(o_sq, 16)
            variance(ors, oss, P, o_var)
            v.wait_ge(o_rt, 1)
            chain(v.reciprocal(ors, ors))
            for c in range(NT):
                ps = bank(("o", c))
                wait_taken(v, "g", c)
                for h in range(RH):
                    cols = slice(h * P, (h + 1) * P)
                    ins = v.scalar_tensor_tensor(mixed[:, c, cols], ps[:, cols], ors[:, 4 * c + h:4 * c + h + 1], mixed[:, c, cols],
                                                 ALU.mult, ALU.mult)
                take(ins, "o", c)
            def rel_bias(h, n):
                return bass.AP(arena, R + 512 * h + n - 1, [[arena.shape[1], P], [-1, n]])

            v.wait_ge(bias_in, 16)
            chain(v.memset(bias[0:64, :, 0:64], NEG))
            for kind, i in STEPS:
                if kind == "att":
                    n = P * (i + 1)
                    for h in range(AH):
                        ps = wait_filled(v, "score", i, h)
                        if h >= 2:
                            wait_filled(v, "pT", i, h - 2)
                        elif i:
                            v.wait_ge(at_sq, i)
                        take(v.tensor_tensor_reduce(prob[h % 2][:, 0:n], ps[:, 0:n], rel_bias(h, n), 1.0, -3.0e38,
                                                    ALU.add, ALU.max, mx[:, h:h + 1]), "score", i, h)
                        wait_taken(v, "score", i, h)
                        v.tensor_scalar(nmx[:, h:h + 1], mx[:, h:h + 1], -1.0, None, ALU.mult).then_inc(pr_max, 1)
                    v.wait_ge(pr_exp, AH * (i + 1))
                    chain(v.reciprocal(rden, den))
                    ps = wait_filled(v, "pv", i)
                    o3 = mixed[:, i, 512:1024].rearrange("p (h d) -> p h d", h=AH)
                    take(v.tensor_tensor(o3, ps[:].rearrange("p (h d) -> p h d", h=AH),
                                         rden.unsqueeze(2).to_broadcast([P, AH, AD]), ALU.mult), "pv", i)
                    wait_taken(v, "pv", i)
                    v.wait_ge(at_sq, i + 1)
                    chain(v.tensor_reduce(ams, prob[0].rearrange("p (h d) -> p h d", h=AH), AX_X, ALU.add))
                    variance(ars, ams, AD, at_var)
                    v.wait_ge(at_rt, i + 1)
                    chain(v.reciprocal(ars, ars))
                    v.tensor_tensor(o3, o3, ars.unsqueeze(2).to_broadcast([P, AH, AD]), ALU.mult).then_inc(at_done, 1)
                if kind == "mo":
                    for half in range(2):
                        ps = wait_filled(v, "mT", i, half)
                        w = vec[:, V_OUT + 4 * half:V_OUT + 4 * half + 4].unsqueeze(2).to_broadcast([P, 4, P])
                        take(v.tensor_tensor(mixT[i % 2][:, 4 * half:4 * half + 4, :], ps[:].rearrange("p (c t) -> p c t", c=4), w,
                                             ALU.mult), "mT", i, half)
                    for half in range(2):
                        ps = wait_filled(v, "out", i, half)
                        cols = slice(512 * half, 512 * half + 512)
                        take(v.tensor_tensor(xs[:, i, cols], xs[:, i, cols], ps[:], ALU.add), "out", i, half)
                    wait_taken(v, "out", i, 0)
                    wait_taken(v, "out", i, 1)
                    v.wait_ge(x2_sq, i + 1)
                    variance(rstd2[:, i:i + 1], ssq2[:, i:i + 1], D, x2_var)
                    v.wait_ge(x2_rt, i + 1)
                    chain(v.reciprocal(rstd2[:, i:i + 1], rstd2[:, i:i + 1]))
                    if i == 0:
                        v.wait_ge(bc_in, 32)
                    if i >= 2:
                        wait_filled(v, "hT2", i - 2, 1)
                        v.wait_ge(h2_out[i % 2], 16)
                    turn = "p (d k) -> p k d"
                    v.scalar_tensor_tensor(h2tok[i % 2].rearrange("p (k d) -> p k d", k=KD), xs[:, i, :].rearrange(turn, k=KD),
                                           rstd2[:, i:i + 1], bc_ffn.rearrange(turn, k=KD), ALU.mult, ALU.mult).then_inc(h2_done, 1)
                if kind == "rt":
                    ps = wait_filled(v, "logit", i)
                    take(v.tensor_copy(lg, ps[:, 0:36]), "logit", i)
                    if i == 0:
                        v.memset(gpad, NEG).then_inc(dve_step, 1)
                        steps[0] += 1
                        v.wait_ge(dve_step, steps[0])
                    wait_taken(v, "logit", i)
                    chain(v.tensor_copy(gpad[:, 0:NG], lg[:, 0:NG]))
                    chain(v.max(gm8, gpad))
                    chain(v.max_index(top_idx[:, 0:8], gm8, gpad))
                    chain(v.tensor_copy(t4[:, 4:5], top_idx[:, 0:1]))
                    chain(v.tensor_scalar(goh, iota[:, 0:NG], t4[:, 4:5], None, ALU.is_equal))
                    chain(v.tensor_scalar(goh, goh, -1.0, -NEG, ALU.add, ALU.mult))
                    v.tensor_scalar(gex, lg[:, 0:NG], gm8[:, 0:1], None, ALU.subtract).then_inc(r_exp_in, 1)
                    chain(v.tensor_tensor(em.rearrange("p (g e) -> p g e", g=NG), lg[:, NG:36].rearrange("p (g e) -> p g e", g=NG),
                                          goh.unsqueeze(2).to_broadcast([P, NG, EPG]), ALU.add))
                    chain(v.max(em8, em))
                    chain(v.max_index(top_idx[:, 8:16], em8, em))
                    v.tensor_tensor(t4[:, 0:1], em8[:, 1:2], em8[:, 0:1], ALU.subtract).then_inc(r_exp_in, 1)
                    chain(v.tensor_copy(expid[:, 2 * i:2 * i + 2], top_idx[:, 8:10]))
                    for k in range(2):
                        ins = v.tensor_scalar(A12[:, 32 * k:32 * k + 32], iota[:, 0:NE], expid[:, 2 * i + k:2 * i + k + 1], None, ALU.is_equal)
                    chain(ins)
                    v.tensor_tensor(A[:, i, :], A12[:, 0:32], A12[:, 32:64], ALU.add).then_inc(assign_done, 1)
                    v.wait_ge(r_exp, 2 * i + 2)
                    chain(v.tensor_scalar(t4[:, 2:3], t4[:, 1:2], 1.0, None, ALU.add))
                    chain(v.tensor_tensor(t4[:, 2:3], t4[:, 2:3], gsum, ALU.mult))
                    chain(v.reciprocal(gate[:, i, 0:1], t4[:, 2:3]))
                    chain(v.tensor_tensor(gate[:, i, 1:2], gate[:, i, 0:1], t4[:, 1:2], ALU.mult))
                if kind == "rk":
                    ps = wait_filled(v, "rank", i)
                    for k in range(2):
                        chain(v.tensor_scalar(A12[:, 0:32], iota[:, 0:NE], expid[:, 2 * i + k:2 * i + k + 1], None, ALU.is_equal))
                        ins = v.tensor_tensor_reduce(rkj, A12[:, 0:32], ps[:, 0:NE], 1.0, 0.0, ALU.mult, ALU.add, rr[:, k:k + 1])
                        if k == 0:
                            chain(ins)
                    take(ins, "rank", i)
                    wait_taken(v, "rank", i)
                    for n in range(1, BLOCKS):
                        ins = v.tensor_scalar(rt3[:, 2 * n - 2:2 * n], rr, float(SLOTS * n), None, ALU.is_ge)
                    chain(ins)
                    chain(v.tensor_tensor(rq, rt3[:, 0:2], rt3[:, 2:4], ALU.add))
                    chain(v.tensor_tensor(rq, rq, rt3[:, 4:6], ALU.add))
                    chain(v.scalar_tensor_tensor(slotpos[:, 2 * i:2 * i + 2], rq, -float(SLOTS), rr, ALU.mult, ALU.add))
                    chain(v.scalar_tensor_tensor(slotpos[:, 8 + 2 * i:10 + 2 * i], rq, float(NE), expid[:, 2 * i:2 * i + 2],
                                                 ALU.mult, ALU.add))
                if kind == "list":
                    for n in range(2 * NT):
                        i, k = n // 2, n % 2
                        if n >= 2:
                            v.wait_ge(oh_read, n - 1)
                        v.tensor_scalar(onehot_r[n % 2], iota, slotpos[:, 2 * i + k:2 * i + k + 1], None, ALU.is_equal)
                        v.tensor_scalar(onehot_v[n % 2][:, 0:P], iota, slotpos[:, 8 + 2 * i + k:9 + 2 * i + k],
                                        cst[:, C_TOK + 2 * i + k:C_TOK + 2 * i + k + 1], ALU.is_equal, ALU.mult)
                        chain(v.tensor_scalar(onehot_v[n % 2][:, P:2 * P], iota, slotpos[:, 8 + 2 * i + k:9 + 2 * i + k],
                                              cst[:, C_TOK + 2 * i + 1:C_TOK + 2 * i + 2], ALU.is_equal, ALU.mult))
                        v.tensor_scalar(onehot_v[n % 2][:, P:2 * P], onehot_v[n % 2][:, P:2 * P], 0.5, None,
                                        ALU.mult).then_inc(oh_done, 1)
                    ps = wait_filled(v, "list")
                    take(v.tensor_copy(lst, ps[:, 0:256]), "list")
                    wait_taken(v, "list")
                    chain(v.tensor_scalar(lst2, lst, 0.0, FAR, ALU.is_equal, ALU.mult))
                    chain(v.scalar_tensor_tensor(lst2, lst, -1.0, lst2, ALU.add, ALU.add))
                    v.tensor_copy(idx[:, 1, :], lst2[:, 0:P])
                    v.tensor_copy(idx[:, 0, :], lst2[:, P:2 * P]).then_inc(idx_done, 1)
                    NC = (BLOCKS - 1) * NE
                    F = part(AQ + 1280, NC)[0:1]
                    cum = part(AQ + 1280 + NC, NC)[0:1]
                    W = part(AQ, OVF_MAX * NC)[0:1].rearrange("p (j c) -> p j c", c=NC)
                    num = part(AQ + 1280 + 2 * NC, 32)[0:1]
                    chain(v.tensor_scalar(F, lst[0:1, NE:P], 0.0, None, ALU.is_gt))
                    chain(v.tensor_tensor_scan(cum, ones_[0:1, 0:NC], F, 0.0, ALU.mult, ALU.add))
                    chain(v.memset(num, 0.0))
                    chain(v.tensor_copy(num[:, 0:1], cum[:, NC - 1:NC]))
                    chain(v.tensor_tensor(W, cum.unsqueeze(1).to_broadcast([1, OVF_MAX, NC]),
                                          iota[0:1, 1:1 + OVF_MAX].unsqueeze(2).to_broadcast([1, OVF_MAX, NC]), ALU.is_equal))
                    chain(v.tensor_tensor(F, F, iota[0:1, NE:P], ALU.mult))
                    chain(v.tensor_tensor(W, W, F.unsqueeze(1).to_broadcast([1, OVF_MAX, NC]), ALU.mult))
                    chain(v.tensor_reduce(num[:, 8:8 + OVF_MAX], W, AX_X, ALU.add))
                    e = num[:, 16:16 + OVF_MAX]
                    chain(v.tensor_scalar(e, num[:, 8:8 + OVF_MAX], float(NE), float(-NE), ALU.is_ge, ALU.mult))
                    chain(v.tensor_tensor(e, e, num[:, 8:8 + OVF_MAX], ALU.add))
                    for n in range(2):
                        t = num[:, 24:24 + OVF_MAX]
                        chain(v.tensor_scalar(t, e, float(NE), float(-NE), ALU.is_ge, ALU.mult))
                        chain(v.tensor_tensor(e, e, t, ALU.add))
                    v.tensor_copy(ctl[:], num).then_inc(idx_done, 1)

            def x_copy(b, n):
                v.wait_ge(m_xt, n)
                v.tensor_copy(xgT[b][:, 0:512], PS[0][:]).then_inc(m_xtc, 1)

            def hidden(b, n):
                v.wait_ge(m_sil, n)
                turn = "p (d j) -> p j d"
                v.tensor_tensor(hid[b].rearrange("p (j d) -> p j d", j=2), sil[b].rearrange(turn, j=2),
                                PS[2 + b][:, FF:2 * FF].rearrange(turn, j=2), ALU.mult).then_inc(m_hid, 1)

            def h_copy(b, n):
                v.wait_ge(m_ht, n)
                v.tensor_copy(hidT[b], PS[4 + b][:, 0:256]).then_inc(m_htc, 1)

            def y_copy(b, n, scattered):
                v.wait_ge(m_y, n)
                if scattered is not None:
                    v.wait_ge(sca[b], scattered)
                v.tensor_copy(ysb[b][:, 512:1024], PS[7][:]).then_inc(m_yc, 1)

            x_copy(0, 1)
            x_copy(1, 2)
            hidden(0, 1)
            h_copy(0, 1)
            for n in range(1, 4):
                b = n % 2
                hidden(b, n + 1)
                y_copy(1 - b, n, None if n < 3 else 16)
                x_copy(1 - b, n + 2)
                h_copy(b, n + 1)
            with v.Fori(1, NE // WSLOTS - 1) as r:
                for s in range(WSLOTS):
                    b = s % 2
                    hidden(b, r * 4 + (s + 1))
                    y_copy(1 - b, r * 4 + s, r * 32 + 16 * ((s - 1) // 2))
                    x_copy(1 - b, r * 4 + (s + 2))
                    h_copy(b, r * 4 + (s + 1))
            for n in range(NE - 4, NE):
                b = n % 2
                hidden(b, n + 1)
                y_copy(1 - b, n, 16 * ((n - 1) // 2))
                if n < NE - 1:
                    x_copy(1 - b, n + 2)
                h_copy(b, n + 1)
            y_copy(1, NE, 16 * (NE // 2 - 1))
            v.wait_ge(idx_done, 2)
            n_ovf = v.value_load(ctl[0:1, 0:1], min_val=0, max_val=OVF_MAX)
            with v.If(n_ovf > 0):
                with v.Fori(0, n_ovf) as j:
                    x_copy(0, j + (NE + 1))
                    hidden(0, j + (NE + 1))
                    h_copy(0, j + (NE + 1))
                    y_copy(0, j + (NE + 1), j * 16 + 8 * NE)
            for i in range(NT):
                v.wait_ge(f_in[i % 2], 16 * (i // 2 + 1))
                chain(v.scalar_tensor_tensor(xs[:, i, :], yin[i % 2][:, 0, :], gate[:, i, 0:1], xs[:, i, :], ALU.mult, ALU.add))
                v.scalar_tensor_tensor(xs[:, i, :], yin[i % 2][:, 1, :], gate[:, i, 1:2], xs[:, i, :], ALU.mult, ALU.add).then_inc(f_sum, 1)
                v.wait_ge(f_sq, i + 1)
                variance(frstd[:, i:i + 1], fssq[:, i:i + 1], D, f_var)
                v.wait_ge(f_rt, i + 1)
                chain(v.reciprocal(frstd[:, i:i + 1], frstd[:, i:i + 1]))
                v.scalar_tensor_tensor(xs[:, i, :], xs[:, i, :], frstd[:, i:i + 1], bc_fin, ALU.mult, ALU.mult).then_inc(f_done, 1)


def constant_table():
    c = np.zeros((P, C_END), np.float32)
    p, t = np.arange(P)[:, None], np.arange(P)[None, :]
    c[:, C_ID:C_ID + P] = p == t
    c[:, C_UP:C_UP + P] = p < t
    c[:, C_ONE:C_ONE + P] = 1
    c[:, C_IOTA:C_IOTA + P] = t
    s, q = np.arange(P)[:, None] % 32, np.arange(32)[None, :]
    for m, h in enumerate(HALVES[2:]):
        c[:, C_MASK + 32 * m:C_MASK + 32 * m + 32] = (s // (2 * h) == q // (2 * h)) & (s // h % 2 == 0) & (q // h % 2 == 1)
    c[:, C_MASK + 160:C_MASK + 192] = s == q
    for i in range(NT):
        for k in range(2):
            c[:, C_TOK + 2 * i + k] = 2 * (P * i + np.arange(P)) + k + 1
    return c


def kernel(x, norm_mix_w, w_in, hgrn_lower_bounds, hgrn_gnorm_w, attn_rel_bias, attn_norm_w, w_out, norm_ffn_w,
           moe_w_group, moe_w_expert, moe_w1, moe_w3, moe_w2, final_norm_w):
    import concourse.bacc as bacc
    from concourse.bass_utils import run_bass_kernel_spmd

    f = np.ascontiguousarray
    order = np.minimum(np.arange(639) + 1, NREL - 1)
    arrays = {
        "x": f(np.asarray(x)[0]),
        "w_in": f(np.asarray(w_in)[0]),
        "w_out": f(np.asarray(w_out)[0]),
        "rel_ext": f(np.asarray(attn_rel_bias)[0][:, order]),
        "vecs": f(np.concatenate([np.asarray(a)[0].reshape(-1, P).T for a in (norm_mix_w, hgrn_lower_bounds, hgrn_gnorm_w, attn_norm_w)], axis=1)),
        "w_route": f(np.concatenate([np.asarray(moe_w_group)[0], np.asarray(moe_w_expert)[0]], axis=1).reshape(P, KD, 36)),
        "norm_ffn": f(np.asarray(norm_ffn_w)[0]),
        "norm_final": f(np.asarray(final_norm_w)),
        "w1": f(np.asarray(moe_w1)[0]),
        "w3": f(np.asarray(moe_w3)[0]),
        "w2": f(np.asarray(moe_w2)[0]),
        "consts": constant_table(),
    }
    nc = bacc.Bacc("TRN2", target_bir_lowering=False, num_devices=1)
    args = [nc.dram_tensor(f"in_{n}", a.shape, mybir.dt.from_np(a.dtype), kind="ExternalInput").ap() for n, a in arrays.items()]
    args.append(nc.dram_tensor("out_rows", (T, D), F32, kind="ExternalOutput").ap())
    trunk(nc, *args)
    r = run_bass_kernel_spmd(nc, [{f"in_{n}": a for n, a in arrays.items()}], core_ids=[0])
    return r.results[0]["out_rows"].reshape(1, T, D)
```

```python
from contextlib import ExitStack

import numpy as np
import concourse.bass as bass
from concourse import mybir

ALU = mybir.AluOpType
ACT = mybir.ActivationFunctionType
AX_X = mybir.AxisListType.X
F32 = mybir.dt.float32
I32 = mybir.dt.int32
U32 = mybir.dt.uint32

P = 128
T = 512
D = 1024
NT = T // P
KD = D // P
HW_ = 512
RH = 4
AH, AD = 8, 64
NREL = 257
NG, NE, EPG, FF = 4, 32, 8, 256
NA = 2 * T
NCH = NA // P
WIN = 96
MORE = (T - 1) // WIN
SL = NA + WIN
EPS = 1e-6
NEG = -1e30
HALVES = [64, 32, 16, 8, 4, 2, 1]
WSLOTS = 4
W13, W2, WE = KD * FF, 2 * D, 2 * KD * FF + 2 * D

C_ID, C_UP, C_ONE, C_IOTA, C_MASK, C_TOK, C_END = 0, 128, 256, 384, 512, 704, 712
V_MIX, V_LB, V_OUT, V_END = 0, 8, 12, 20
ARENA = 52800
GROUPS = ["f", "q", "v", "ak", "aq", "av", "g"]
GROUP_COL = {"q": 0, "f": 512, "v": 1024, "g": 1536, "aq": 2048, "ak": 2560, "av": 3072}
GROUP_BUF = {"f": 0, "q": 1, "v": 2, "ak": 3, "aq": 0, "av": 1, "g": 2}


def psum_plan():
    seen, plan = [0] * 8, {}

    def use(bank, *name):
        plan[name] = (bank, seen[bank])
        seen[bank] += 1

    for i in range(NT):
        for half in range(2):
            use(2 + (2 * i + half) % 4, "xT", i, half)
    n = 0
    for g in ("f", "q", "v", "ak"):
        for j in range(4):
            use(n % 2, g, j)
            n += 1
    use(6, "diag")
    blocks = [("aq", 0), ("aq", 1), ("aq", 2), ("aq", 3), ("av", 0), ("av", 1), ("av", 2), ("av", 3)]
    for li in range(7):
        use(n % 2, *blocks[li])
        n += 1
        if li == 0:
            use(2, "level", 0, 0)
            use(3, "level", 0, 1)
        else:
            use([4, 5, 2, 3, 4, 5][li - 1], "level", li, 0)
    use(n % 2, "av", 3)
    n += 1
    for c, b in enumerate((6, 7, 2)):
        use(b, "kT", c)
    use(n % 2, "g", 0)
    n += 1
    for c, b in enumerate((3, 4, 5)):
        use(b, "delta", c)
    use(n % 2, "g", 1)
    n += 1
    use(6, "o", 0)
    use(7, "o", 1)
    use(n % 2, "g", 2)
    n += 1
    use(2, "o", 2)
    use(3, "o", 3)
    use(n % 2, "g", 3)
    for kind, i in STEPS:
        if kind == "att":
            for t in range(AH + 2):
                if t < AH:
                    use(4 + t % 2, "score", i, t)
                if 1 <= t <= AH:
                    use(2 + (t - 1) % 2, "pT", i, t - 1)
                if t == 2:
                    use(6 + i % 2, "pv", i)
        if kind == "mo":
            use(2, "mT", i, 0)
            use(3, "mT", i, 1)
            use(0, "out", i, 0)
            use(1, "out", i, 1)
        if kind == "rt":
            use(4, "hT2", i, 0)
            use(5, "hT2", i, 1)
            use(6, "logit", i)
        if kind == "sort":
            use(7, "rank")
            use(2, "list")
    return plan, seen


STEPS = [("att", 0), ("att", 1), ("mo", 0), ("att", 2), ("mo", 1), ("rt", 0), ("att", 3), ("mo", 2),
         ("rt", 1), ("mo", 3), ("rt", 2), ("rt", 3), ("sort", 0)]
PLAN, BANK_USES = psum_plan()


def trunk(nc, x, w_in, w_out, rel_ext, vecs, w_route, norm_ffn, norm_final, w1, w3, w2, consts, out):
    ctx = ExitStack()
    with ctx:
        def sem(name):
            return ctx.enter_context(nc.semaphore(name))

        arena = ctx.enter_context(nc.sbuf_tensor("arena", [P, ARENA], F32))
        idx = ctx.enter_context(nc.sbuf_tensor("idx", [P, NCH], U32))
        pos_u = ctx.enter_context(nc.sbuf_tensor("pos_u", [P, NCH], U32))
        top_idx = ctx.enter_context(nc.sbuf_tensor("top_idx", [P, 16], U32))
        ctl = ctx.enter_context(nc.sbuf_tensor("ctl", [1, NE * (3 + MORE)], I32))
        PS = [ctx.enter_context(nc.psum_tensor(f"bank{b}", [P, 512], F32)) for b in range(8)]

        def part(at, size):
            return arena[:, at:at + size]

        xs = part(0, 4096).rearrange("p (i d) -> p i d", i=NT)
        ring = [part(4096 + 4096 * b, 4096).rearrange("p (k n) -> p k n", k=KD) for b in range(4)]
        hT = part(20480, 4096).rearrange("p (k t) -> p k t", k=KD)
        wout = [ring[3], part(20480, 4096).rearrange("p (k n) -> p k n", k=KD)]
        wslot = [part(4096, WE), part(4096 + WE, WE), part(24576, WE), part(4096 + 2 * WE, WE)]
        R = 24576
        bcum = part(R, 2048)
        L = [part(R + 2048, 2048), part(R + 4096, 2048)]
        xn = [part(R + 2048, 1024), part(R + 3072, 1024)]
        kdT = part(R, 1536).rearrange("p (c n) -> p c n", c=3)
        bias = part(R, 4096).rearrange("p (h n) -> p h n", h=AH)
        prob = [part(R + 4096, 512), part(R + 4608, 512)]
        probT = [part(R + 5120, 512), part(R + 5632, 512)]
        Q, K, S = 30720, 32768, 34816
        qT = part(Q, 2048)
        kT = part(K, 2048)
        states = part(Q, 1536).rearrange("p (c n) -> p c n", c=3)
        bc_ffn = part(Q, 1024)
        Sasm = part(S, 2048).rearrange("p (b t) -> p b t", t=P)
        mixT = [part(K + 1024 * b, 1024).rearrange("p (k t) -> p k t", k=KD) for b in range(2)]
        h2T = [part(S + 1024 * b, 1024).rearrange("p (k t) -> p k t", k=KD) for b in range(2)]
        acc = part(36864, 512)
        V_, AQ, AK, AV = 37376, 39424, 41472, 43520
        vtok = part(V_, 2048).rearrange("p (c n) -> p c n", c=NT)
        h2tok = [part(V_, 1024), part(V_ + 1024, 1024)]
        aqT = part(AQ, 2048).rearrange("p (b t) -> p b t", b=4)
        akT = part(AK, 2048).rearrange("p (b t) -> p b t", b=4)
        avt = part(AV, 2048).rearrange("p (c n) -> p c n", c=NT)
        XT_, YT_ = 30720, 30720 + KD * SL
        xt = part(XT_, KD * SL).rearrange("p (k t) -> p k t", k=KD)
        yt = part(YT_, KD * SL).rearrange("p (k t) -> p k t", k=KD)
        xg = [part(YT_ + 1024 * b, 1024) for b in range(4)]
        SC = YT_ + 4096
        onehot_p = part(SC, 1024).rearrange("p (a t) -> p a t", a=NCH)
        M = 45568
        mixed = part(M, 4096).rearrange("p (i n) -> p i n", i=NT)
        bc_fin = part(YT_ + KD * SL, 1024)
        yrow = [part(XT_ + 1024 * b, 1024) for b in range(4)]
        yin = [part(4096 + 1024 * n, 1024) for n in range(2 * NT)]
        junk = part(XT_ + 4096, 1024)
        cst = part(49664, C_END)
        vec = part(49664 + C_END, V_END)
        wr = part(49664 + C_END + V_END, KD * 36).rearrange("p (k n) -> p k n", k=KD)
        sm = 49664 + C_END + V_END + KD * 36 + 4
        small_at = [sm]

        def small(n):
            at = small_at[0]
            small_at[0] += n
            assert small_at[0] <= ARENA
            return part(at, n)

        ident, upper, ones_, iota = (cst[:, c:c + P] for c in (C_ID, C_UP, C_ONE, C_IOTA))

        ssq = small(NT)
        rstd = small(NT)
        lbw = small(16)
        ebl = small(16)
        oss, ors = small(16), small(16)
        mx, nmx, den = small(8), small(8), small(8)
        rden, ams, ars = small(8), small(8), small(8)
        ssq2, rstd2 = small(NT), small(NT)
        gate = small(8).rearrange("p (i k) -> p i k", k=2)
        expid = small(8)
        sil = [small(2 * WIN) for b in range(3)]
        hid = [small(2 * WIN) for b in range(3)]
        fssq, frstd = small(NT), small(NT)
        RW = 36864
        lg, gpad, gm8, goh, em, em8 = part(RW, 36), part(RW + 36, 8), part(RW + 44, 8), part(RW + 52, 4), part(RW + 56, 32), part(RW + 88, 8)
        gex, gsum, t4 = part(RW + 96, 4), part(RW + 100, 1), part(RW + 104, 8)
        A12 = part(RW + 112, 64)
        A = part(RW + 176, 128).rearrange("p (i e) -> p i e", i=NT)
        S0 = SC + 1024
        hot = part(S0, 256).rearrange("p (i k e) -> p i k e", i=NT, k=2)
        hotw = part(S0 + 256, 256).rearrange("p (i k e) -> p i k e", i=NT, k=2)
        cnt, incl, off = part(S0 + 512, 32), part(S0 + 544, 32), part(S0 + 576, 32)
        pos, chunk, within = part(S0 + 608, 8), part(S0 + 616, 8), part(S0 + 624, 8)
        edges = part(S0 + 632, 8)
        over = part(S0 + 640, 64).rearrange("p (a n) -> p a n", a=NCH)
        onehot_c = part(S0 + 704, 64).rearrange("p (a n) -> p a n", a=NCH)

        XN = nc.dram_tensor("h2_rows", [T, D], F32, kind="Internal").ap()
        Y = nc.dram_tensor("expert_rows", [NA, D], F32, kind="Internal").ap()

        x_in, cst_in, win_in = [sem(f"x_in{i}") for i in range(NT)], sem("cst_in"), [sem(f"win_in{b}") for b in range(4)]
        wout_in, bias_in, bc_in = [sem("wout_in0"), sem("wout_in1")], sem("bias_in"), sem("bc_in")
        filled = [sem(f"bank_filled{b}") for b in range(8)]
        taken = [sem(f"bank_taken{b}") for b in range(8)]
        act_step, dve_step, pool_step = sem("act_step"), sem("dve_step"), sem("pool_step")
        x_sq, x_rt, x_var, xn_done = sem("x_squares"), sem("x_root"), sem("x_variance"), sem("xn_done")
        zprep_a, zprep_v = sem("gate_terms_act"), sem("gate_terms_dve")
        lv_sub, lv_exp, lv_mul = sem("level_diff"), sem("level_exp"), sem("level_operands")
        sasm_done = sem("scores_placed")
        o_sq, o_rt, o_var = sem("o_squares"), sem("o_root"), sem("o_variance")
        pr_max, pr_exp, pt_pe = sem("row_max"), sem("probs_exp"), sem("probs_transposed")
        at_sq, at_var, at_rt, at_done = sem("att_squares"), sem("att_variance"), sem("att_root"), sem("att_done")
        x2_sq, x2_var, x2_rt = sem("x2_squares"), sem("x2_variance"), sem("x2_root")
        h2_done, h2_out = sem("h2_done"), [sem("h2_stored0"), sem("h2_stored1")]
        r_exp_in, r_exp, assign_done = sem("router_exp_in"), sem("router_exp"), sem("assign_done")
        oh_done, idx_done, ctl_done = sem("onehots_done"), sem("idx_done"), sem("windows_done")
        w_in_sem = [sem(f"expert_weights_in{s}") for s in range(WSLOTS)]
        gat, xg_turned, xt_a, xt_v, pads = [sem(f"rows_gathered{b}") for b in range(4)], sem("rows_transposed"), sem("xt_copied_act"), sem("xt_copied_dve"), sem("pads_cleared")
        m_h, m_sil, m_hid, m_y, m_yc_a, m_yc_v = sem("up_products"), sem("silu_done"), sem("hidden_done"), sem("down_products"), sem("y_copied_act"), sem("y_copied_dve")
        e_h, e_sil, e_hid, e_y, e_yc_a, e_yc_v = sem("more_up_products"), sem("more_silu_done"), sem("more_hidden_done"), sem("more_down_products"), sem("more_y_copied_act"), sem("more_y_copied_dve")
        y_turned, y_row_a, y_row_v, y_out = sem("y_transposed"), sem("y_rows_copied_act"), sem("y_rows_copied_dve"), [sem(f"y_rows_stored{b}") for b in range(4)]
        f_in = [sem(f"token_rows_in{i}") for i in range(NT)]
        f_sum, f_sq, f_var, f_rt, f_done, out_sem = sem("final_sum"), sem("final_squares"), sem("final_variance"), sem("final_root"), sem("final_rows"), sem("out_stored")
        bc2_in, cleared = sem("final_norm_in"), sem("cleared")

        def bank(name):
            return PS[PLAN[name][0]]

        def claim(pe, *name):
            b, n = PLAN[name]
            if n:
                pe.wait_ge(taken[b], n)
            return PS[b]

        def fill(ins, *name):
            ins.then_inc(filled[PLAN[name][0]], 1)

        def wait_filled(eng, *name):
            b, n = PLAN[name]
            eng.wait_ge(filled[b], n + 1)
            return PS[b]

        def take(ins, *name):
            ins.then_inc(taken[PLAN[name][0]], 1)

        def wait_taken(eng, *name):
            b, n = PLAN[name]
            eng.wait_ge(taken[b], n + 1)

        x_d = x.rearrange("(i p) d -> i p d", p=P)
        out_d = out.rearrange("(i p) d -> i p d", p=P)
        w_in_d = w_in.rearrange("(k p) n -> p k n", p=P)
        w_out_d = w_out.rearrange("(k p) n -> p k n", p=P)
        w1_d = w1.rearrange("e (p k) f -> e p (k f)", p=P)
        w3_d = w3.rearrange("e (p k) f -> e p (k f)", p=P)
        w2_d = w2.rearrange("e (j p) n -> e p j n", p=P)

        def expert_views(s):
            w = wslot[s]
            w13 = w[:, 0:2 * W13].rearrange("p (m k f) -> p m k f", m=2, k=KD)
            return w13, w[:, 2 * W13:WE].rearrange("p (j n) -> p j n", j=2)

        def first_of(eng, e):
            return eng.value_load(ctl[0:1, bass.ds(e, 1)], min_val=0, max_val=NA)

        block = ctx.enter_context(nc.Block())

        @block.sync
        def _(sp):
            def win(g, n):
                b = GROUP_BUF[g]
                sp.dma_start(ring[b], w_in_d[:, :, GROUP_COL[g]:GROUP_COL[g] + 512]).then_inc(win_in[b], 16)

            sp.dma_start(xs[:, 0, :], x_d[0]).then_inc(x_in[0], 16)
            sp.dma_start(cst, consts).then_inc(cst_in, 16)
            sp.dma_start(vec, vecs).then_inc(cst_in, 16)
            sp.dma_start(wr, w_route).then_inc(cst_in, 16)
            for i in range(1, NT):
                sp.dma_start(xs[:, i, :], x_d[i]).then_inc(x_in[i], 16)
            for n in range(4):
                win(GROUPS[n], n)
            wait_filled(sp, "f", 3)
            win("aq", 4)
            wait_filled(sp, "q", 3)
            win("av", 5)
            wait_filled(sp, "v", 3)
            win("g", 6)
            wait_filled(sp, "ak", 3)
            sp.dma_start(wout[0], w_out_d[:, :, 0:512]).then_inc(wout_in[0], 16)

            def expert(s, e, sem_):
                sp.dma_start(wslot[s][:, 0:W13], w1_d[e]).then_inc(sem_, 16)
                sp.dma_start(wslot[s][:, W13:2 * W13], w3_d[e]).then_inc(sem_, 16)
                sp.dma_start(expert_views(s)[1], w2_d[e]).then_inc(sem_, 16)

            wait_filled(sp, "av", 3)
            expert(0, 0, w_in_sem[0])
            wait_filled(sp, "g", 3)
            sp.dma_start(wout[1], w_out_d[:, :, 512:1024]).then_inc(wout_in[1], 16)
            wait_taken(sp, "delta", 2)
            wait_filled(sp, "o", 3)
            wait_taken(sp, "kT", 2)
            bsrc = bass.AP(rel_ext.tensor, 0, [[1, P], [639, AH], [1, 512]])
            sp.dma_start(bias, bsrc).then_inc(bias_in, 16)
            sp.dma_start(bc_ffn, norm_ffn.partition_broadcast(P)).then_inc(bc_in, 16)
            expert(1, 1, w_in_sem[1])
            sp.wait_ge(at_done, NT)
            expert(2, 2, w_in_sem[2])
            wait_filled(sp, "out", 3, 1)
            sp.wait_ge(x2_sq, NT)
            sp.dma_start(bc_fin, norm_final.partition_broadcast(P)).then_inc(bc2_in, 16)
            expert(3, 3, w_in_sem[3])
            with sp.Fori(0, NE // WSLOTS - 1) as r:
                for s in range(WSLOTS):
                    sp.wait_ge(m_y, r * WSLOTS + s + 1)
                    expert(s, r * WSLOTS + (WSLOTS + s), w_in_sem[s])
            for c in range(NCH):
                sp.wait_ge(y_row_a, c + 1)
                sp.wait_ge(y_row_v, c + 1)
                sp.dma_start(Y[c * P:(c + 1) * P, :], yrow[c % 4]).then_inc(y_out[c % 4], 16)
            for i in range(NT):
                sp.wait_ge(f_done, i + 1)
                sp.dma_start(out_d[i], xs[:, i, :]).then_inc(out_sem, 16)
            sp.wait_ge(out_sem, 16 * NT)

        @block.gpsimd
        def _(pool):
            pool.memset(acc, 1.0).then_inc(pool_step, 1)
            pool.wait_ge(pool_step, 1)
            pool.memset(acc.rearrange("p (c t) -> p c t", t=P)[:, :, 0:1], 0.0).then_inc(cleared, 1)
            pool.memset(Sasm, 0.0).then_inc(cleared, 1)
            pool.wait_ge(idx_done, 1)
            for b in range(2):
                pool.wait_ge(h2_out[b], 16 * NT // 2)
            pool.memset(xt[:, :, NA:SL], 0.0).then_inc(pads, 1)
            for c in range(NCH):
                if c >= 4:
                    pool.wait_ge(xg_turned, c - 3)
                pool.indirect_dma_start(xg[c % 4], None, XN, bass.IndirectOffsetOnAxis(ap=idx[:, c:c + 1], axis=0),
                                        bounds_check=T - 1).then_inc(gat[c % 4], 16)
            for b in range(4):
                pool.wait_ge(y_out[b], 16 * NCH // 4)
            for i in range(NT):
                for k in range(2):
                    n = 2 * i + k
                    pool.indirect_dma_start(yin[n], None, Y, bass.IndirectOffsetOnAxis(ap=pos_u[:, n:n + 1], axis=0),
                                            bounds_check=NA - 1).then_inc(f_in[i], 16)

        @block.tensor
        def _(pe):
            pe.wait_ge(cst_in, 48)
            for i in range(NT):
                pe.wait_ge(xn_done, i + 1)
                for half in range(2):
                    ps = claim(pe, "xT", i, half)
                    for c in range(4):
                        last = pe.transpose(ps[:, c * P:(c + 1) * P], xn[i % 2][:, (4 * half + c) * P:(4 * half + c + 1) * P], ident)
                    fill(last, "xT", i, half)

            def project(g, j):
                ps = claim(pe, g, j)
                w = ring[GROUP_BUF[g]]
                for k in range(KD):
                    if g in ("f", "q", "ak", "aq"):
                        last = pe.matmul(ps[:], w[:, k, j * P:(j + 1) * P], hT[:, k, :], start=k == 0, stop=k == KD - 1)
                    else:
                        last = pe.matmul(ps[:], hT[:, k, j * P:(j + 1) * P], w[:, k, :], start=k == 0, stop=k == KD - 1)
                fill(last, g, j)

            def begin(g):
                n = GROUPS.index(g)
                pe.wait_ge(win_in[GROUP_BUF[g]], 32 if n >= 4 else 16)

            for i in range(NT):
                wait_taken(pe, "xT", i, 0)
                wait_taken(pe, "xT", i, 1)
            for g in ("f", "q", "v", "ak"):
                begin(g)
                for j in range(4):
                    project(g, j)

            def small_blocks(ps, lhs, rhs):
                for hc in range(16):
                    for j in range(4):
                        at = hc * P + 32 * j
                        last = pe.matmul(ps[32 * j:32 * j + 32, 32 * hc:32 * hc + 32], lhs[:, at:at + 32], rhs[:, at:at + 32],
                                         start=True, stop=True)
                return last

            ps = claim(pe, "diag")
            pe.wait_ge(zprep_a, 8)
            for j in range(4):
                wait_taken(pe, "q", j)
            fill(small_blocks(ps, kT, qT), "diag")

            def level(li):
                pe.wait_ge(lv_mul, li + 1)
                buf = L[li % 2]
                if li == 0:
                    for half in range(2):
                        ps = claim(pe, "level", 0, half)
                        for n in range(8):
                            at = (8 * half + n) * P
                            last = pe.matmul(ps[0:64, 64 * n:64 * n + 64], buf[:, at:at + 64], buf[:, at + 64:at + 128],
                                             start=True, stop=True)
                        fill(last, "level", 0, half)
                elif li == 1:
                    ps = claim(pe, "level", 1, 0)
                    for hc in range(16):
                        for j in range(2):
                            at = hc * P + 64 * j
                            last = pe.matmul(ps[64 * j:64 * j + 32, 32 * hc:32 * hc + 32], buf[:, at:at + 32], buf[:, at + 32:at + 64],
                                             start=True, stop=True)
                    fill(last, "level", 1, 0)
                else:
                    fill(small_blocks(claim(pe, "level", li, 0), buf, buf), "level", li, 0)

            begin("aq")
            for li in range(7):
                if li == 4:
                    begin("av")
                if li < 4:
                    project("aq", li)
                else:
                    project("av", li - 4)
                level(li)
            project("av", 3)
            pe.wait_ge(lv_mul, 9)
            for c in range(3):
                ps = claim(pe, "kT", c)
                for h in range(RH):
                    last = pe.transpose(ps[:, h * P:(h + 1) * P], L[0][:, (4 * h + c) * P:(4 * h + c + 1) * P], ident)
                fill(last, "kT", c)
            begin("g")
            project("g", 0)
            for c in range(3):
                ps = claim(pe, "delta", c)
                wait_taken(pe, "kT", c)
                for h in range(RH):
                    last = pe.matmul(ps[:, h * P:(h + 1) * P], kdT[:, c, h * P:(h + 1) * P], vtok[:, c, h * P:(h + 1) * P],
                                     start=True, stop=True)
                fill(last, "delta", c)
            project("g", 1)

            def rec_out(c):
                ps = claim(pe, "o", c)
                pe.wait_ge(sasm_done, 1)
                if c:
                    wait_taken(pe, "delta", c - 1)
                for h in range(RH):
                    last = pe.matmul(ps[:, h * P:(h + 1) * P], Sasm[:, 4 * h + c, :], vtok[:, c, h * P:(h + 1) * P],
                                     start=True, stop=c == 0)
                    if c:
                        at = (4 * h + c) * P
                        last = pe.matmul(ps[:, h * P:(h + 1) * P], L[1][:, at:at + P], states[:, c - 1, h * P:(h + 1) * P],
                                         start=False, stop=True)
                fill(last, "o", c)

            rec_out(0)
            rec_out(1)
            project("g", 2)
            rec_out(2)
            rec_out(3)
            project("g", 3)

            for kind, i in STEPS:
                if kind == "att":
                    n = P * (i + 1)
                    for t in range(AH + 2):
                        if t < AH:
                            ps = claim(pe, "score", i, t)
                            o = 64 * (t % 2)
                            fill(pe.matmul(ps[:, 0:n], aqT[o:o + 64, t // 2, i * P:(i + 1) * P], akT[o:o + 64, t // 2, 0:n],
                                           start=True, stop=True), "score", i, t)
                        if 1 <= t <= AH:
                            h = t - 1
                            ps = claim(pe, "pT", i, h)
                            pe.wait_ge(pr_exp, AH * i + h + 1)
                            for j in range(i + 1):
                                last = pe.transpose(ps[:, j * P:(j + 1) * P], prob[h % 2][:, j * P:(j + 1) * P], ident)
                            fill(last, "pT", i, h)
                        if t >= 2:
                            h = t - 2
                            if h == 0:
                                pv = claim(pe, "pv", i)
                            wait_taken(pe, "pT", i, h)
                            for j in range(i + 1):
                                last = pe.matmul(pv[:, h * AD:(h + 1) * AD], probT[h % 2][:, j * P:(j + 1) * P],
                                                 avt[:, j, h * AD:(h + 1) * AD], start=j == 0, stop=j == i)
                            if h < AH - 1:
                                last.then_inc(pt_pe, 1)
                            else:
                                fill(last, "pv", i)
                if kind == "mo":
                    wait_taken(pe, "o", i)
                    pe.wait_ge(at_done, i + 1)
                    for half in range(2):
                        ps = claim(pe, "mT", i, half)
                        for c in range(4):
                            k = 4 * half + c
                            last = pe.transpose(ps[:, c * P:(c + 1) * P], mixed[:, i, k * P:(k + 1) * P], ident)
                        fill(last, "mT", i, half)
                    wait_taken(pe, "mT", i, 0)
                    wait_taken(pe, "mT", i, 1)
                    for half in range(2):
                        if i == 0:
                            pe.wait_ge(wout_in[half], 16)
                        ps = claim(pe, "out", i, half)
                        for k in range(KD):
                            last = pe.matmul(ps[:], mixT[i % 2][:, k, :], wout[half][:, k, :], start=k == 0, stop=k == KD - 1)
                        fill(last, "out", i, half)
                if kind == "rt":
                    pe.wait_ge(h2_done, i + 1)
                    for half in range(2):
                        ps = claim(pe, "hT2", i, half)
                        for c in range(4):
                            k = 4 * half + c
                            last = pe.transpose(ps[:, c * P:(c + 1) * P], h2tok[i % 2][:, k * P:(k + 1) * P], ident)
                        fill(last, "hT2", i, half)
                    wait_taken(pe, "hT2", i, 0)
                    wait_taken(pe, "hT2", i, 1)
                    ps = claim(pe, "logit", i)
                    for k in range(KD):
                        last = pe.matmul(ps[:, 0:36], h2T[i % 2][:, k, :], wr[:, k, :], start=k == 0, stop=k == KD - 1)
                    fill(last, "logit", i)
                if kind == "sort":
                    pe.wait_ge(assign_done, NT)
                    ps = claim(pe, "rank")
                    for t in range(NT + 1):
                        for j in range(min(t + 1, NT)):
                            last = pe.matmul(ps[:, t * NE:(t + 1) * NE], upper if j == t else ones_, A[:, j, :],
                                             start=j == 0, stop=j == min(t, NT - 1))
                    fill(last, "rank")
                    ps = claim(pe, "list")
                    pe.wait_ge(oh_done, 1)
                    for n in range(NCH):
                        last = pe.matmul(ps[:, 0:NCH], onehot_p[:, n, :], onehot_c[:, n, :], start=n == 0, stop=n == NCH - 1)
                    fill(last, "list")
            for b in range(8):
                pe.wait_ge(taken[b], BANK_USES[b])

            for c in range(NCH):
                pe.wait_ge(gat[c % 4], 16 * (c // 4 + 1))
                if c >= 2:
                    pe.wait_ge(xt_a, c - 1)
                    pe.wait_ge(xt_v, c - 1)
                for half in range(2):
                    for n in range(4):
                        k = 4 * half + n
                        last = pe.transpose(PS[4 * (c % 2) + half][:, n * P:(n + 1) * P], xg[c % 4][:, k * P:(k + 1) * P], ident)
                last.then_inc(xg_turned, 1)

            def up(ps, s, first, done):
                w13, _ = expert_views(s)
                for m in range(2):
                    for j in range(2):
                        for k in range(KD):
                            at = (2 * m + j) * WIN
                            last = pe.matmul(ps[:, at:at + WIN], w13[:, m, k, j * P:(j + 1) * P], xt[:, k, bass.ds(first, WIN)],
                                             start=k == 0, stop=k == KD - 1)
                last.then_inc(done, 1)

            def down(b0, h, s, done):
                _, w2v = expert_views(s)
                for c in range(KD):
                    for j in range(2):
                        last = pe.matmul(PS[b0 + c // 4][:, (c % 4) * WIN:(c % 4 + 1) * WIN], w2v[:, j, c * P:(c + 1) * P],
                                         h[:, j * WIN:(j + 1) * WIN], start=j == 0, stop=j == 1)
                last.then_inc(done, 1)

            def more(e, s):
                count = pe.value_load(ctl[0:1, bass.ds(e + NE, 1)], min_val=0, max_val=MORE)
                with pe.If(count > 0):
                    before = pe.value_load(ctl[0:1, bass.ds(e + 2 * NE, 1)], min_val=0, max_val=NCH + 3)
                    with pe.Fori(0, count) as w:
                        first = pe.value_load(ctl[0:1, bass.ds(e * MORE + w + 3 * NE, 1)], min_val=0, max_val=NA)
                        up(PS[4], s, first, e_h)
                        pe.wait_ge(e_hid, before + w + 1)
                        down(5, hid[2], s, e_y)
                        pe.wait_ge(e_yc_a, before + w + 1)
                        pe.wait_ge(e_yc_v, before + w + 1)

            pe.wait_ge(xt_a, NCH)
            pe.wait_ge(xt_v, NCH)
            pe.wait_ge(pads, 1)
            pe.wait_ge(ctl_done, 1)
            for e in range(WSLOTS):
                pe.wait_ge(w_in_sem[e], 48)
                more(e, e)
                up(PS[e % 2], e, first_of(pe, e), m_h)
                if e >= 1:
                    pe.wait_ge(m_hid, e)
                    if e >= 2:
                        pe.wait_ge(m_yc_a, e - 1)
                        pe.wait_ge(m_yc_v, e - 1)
                    down(2, hid[(e - 1) % 2], e - 1, m_y)
            with pe.Fori(1, NE // WSLOTS) as r:
                for s in range(WSLOTS):
                    pe.wait_ge(w_in_sem[s], r * 48 + 48)
                    more(r * WSLOTS + s, s)
                    up(PS[s % 2], s, first_of(pe, r * WSLOTS + s), m_h)
                    pe.wait_ge(m_hid, r * WSLOTS + s)
                    pe.wait_ge(m_yc_a, r * WSLOTS + (s - 1))
                    pe.wait_ge(m_yc_v, r * WSLOTS + (s - 1))
                    down(2, hid[(s - 1) % 2], (s - 1) % WSLOTS, m_y)
            pe.wait_ge(m_hid, NE)
            pe.wait_ge(m_yc_a, NE - 1)
            pe.wait_ge(m_yc_v, NE - 1)
            down(2, hid[1], WSLOTS - 1, m_y)
            pe.wait_ge(m_yc_a, NE)
            pe.wait_ge(m_yc_v, NE)
            for c in range(NCH):
                if c >= 2:
                    pe.wait_ge(y_row_a, c - 1)
                    pe.wait_ge(y_row_v, c - 1)
                for half in range(2):
                    for n in range(4):
                        last = pe.transpose(PS[4 * (c % 2) + half][:, n * P:(n + 1) * P], yt[:, 4 * half + n, c * P:(c + 1) * P], ident)
                last.then_inc(y_turned, 1)

        @block.scalar
        def _(act):
            def a(out_, in_, f, **k):
                return act.activation(out_, in_, f, **k)

            steps = [0]

            def chain(ins):
                ins.then_inc(act_step, 1)
                steps[0] += 1
                act.wait_ge(act_step, steps[0])

            def copy_pt(i, h):
                n = P * (i + 1)
                wait_filled(act, "pT", i, h)
                k = (AH - 1) * i + h - 1
                if h >= 2:
                    act.wait_ge(pt_pe, k)
                elif i:
                    wait_filled(act, "pv", i - 1)
                take(a(probT[h % 2][:, 0:n], bank(("pT", i, h))[:, 0:n], ACT.Copy), "pT", i, h)

            for i in range(NT):
                act.wait_ge(x_in[i], 16)
                if i >= 1:
                    act.wait_ge(x_sq, i)
                a(part(AQ, 1024), xs[:, i, :], ACT.Square, accum_out=ssq[:, i:i + 1]).then_inc(x_sq, 1)
                act.wait_ge(x_var, i + 1)
                a(rstd[:, i:i + 1], rstd[:, i:i + 1], ACT.Sqrt).then_inc(x_rt, 1)
            act.wait_ge(zprep_v, 1)
            a(lbw[:, 4:8], lbw[:, 0:4], ACT.Exp).then_inc(zprep_a, 1)
            act.wait_ge(zprep_v, 2)
            a(lbw[:, 12:16], lbw[:, 8:12], ACT.Ln, scale=-1.0, bias=1.0).then_inc(zprep_a, 1)
            for j in range(4):
                wait_filled(act, "q", j)
                take(a(qT[:, j * 512:(j + 1) * 512], bank(("q", j))[:], ACT.Silu), "q", j)

            def copy_v(j):
                wait_filled(act, "v", j)
                take(a(vtok[:, j, :], bank(("v", j))[:], ACT.Copy), "v", j)

            def copy_ak(j):
                wait_filled(act, "ak", j)
                take(a(akT[:, j, :], bank(("ak", j))[:], ACT.Copy), "ak", j)

            for j in range(4):
                wait_taken(act, "f", j)
            a(L[0], bcum, ACT.Relu, scale=-1.0).then_inc(zprep_a, 1)
            copy_v(0)
            act.wait_ge(zprep_v, 3)
            chain(a(L[1], L[1], ACT.Exp, scale=-1.0))
            copy_v(1)
            a(L[1], L[1], ACT.Ln, bias=1.0).then_inc(zprep_a, 1)
            copy_v(2)
            act.wait_ge(zprep_v, 5)
            act.wait_ge(zprep_a, 2)
            for h in range(RH):
                a(kT[:, h * 512:(h + 1) * 512], L[1][:, h * 512:(h + 1) * 512], ACT.Exp, scale=-1.0,
                  bias=lbw[:, 12 + h:13 + h]).then_inc(zprep_a, 1)
            copy_v(3)
            act.wait_ge(zprep_v, 6)
            chain(a(L[1], L[1], ACT.Exp, scale=-1.0))
            copy_ak(0)
            for h in range(RH):
                ins = a(L[1][:, h * 512:(h + 1) * 512], L[1][:, h * 512:(h + 1) * 512], ACT.Ln,
                        scale=lbw[:, 8 + h:9 + h], bias=1.0)
            ins.then_inc(zprep_a, 1)
            copy_ak(1)
            for li in range(2):
                act.wait_ge(lv_sub, li + 1)
                a(L[li], L[li], ACT.Exp).then_inc(lv_exp, 1)
            copy_ak(2)
            copy_ak(3)
            for li in range(7):
                if li < 4:
                    wait_filled(act, "aq", li)
                    take(a(aqT[:, li, :], bank(("aq", li))[:], ACT.Copy, scale=AD ** -0.5), "aq", li)
                else:
                    wait_filled(act, "av", li - 4)
                    take(a(avt[:, li - 4, :], bank(("av", li - 4))[:], ACT.Copy), "av", li - 4)
                if li + 2 < 7:
                    act.wait_ge(lv_sub, li + 3)
                    a(L[li % 2], L[li % 2], ACT.Exp).then_inc(lv_exp, 1)
                elif li + 2 == 7:
                    wait_filled(act, "level", 5, 0)
                    a(L[1], bcum, ACT.Exp).then_inc(lv_exp, 1)
                else:
                    act.wait_ge(lv_sub, 8)
                    a(ebl, bcum.rearrange("p (b t) -> p b t", t=P)[:, :, P - 1], ACT.Exp).then_inc(act_step, 1)
                    steps[0] += 1
                    a(L[0], L[0], ACT.Exp).then_inc(lv_exp, 1)
            wait_filled(act, "av", 3)
            take(a(avt[:, 3, :], bank(("av", 3))[:], ACT.Copy), "av", 3)
            for c in range(3):
                wait_filled(act, "kT", c)
                take(a(kdT[:, c, :], bank(("kT", c))[:], ACT.Copy), "kT", c)

            def silu_g(i):
                wait_filled(act, "g", i)
                take(a(mixed[:, i, 0:512], bank(("g", i))[:], ACT.Silu), "g", i)

            silu_g(0)
            silu_g(1)
            silu_g(2)

            def squares(c):
                wait_filled(act, "o", c)
                for h in range(RH):
                    if c + h:
                        act.wait_ge(o_sq, RH * c + h)
                    a(part(K, 128), bank(("o", c))[:, h * P:(h + 1) * P], ACT.Square,
                      accum_out=oss[:, 4 * c + h:4 * c + h + 1]).then_inc(o_sq, 1)

            for c in range(NT):
                squares(c)
            silu_g(3)
            act.wait_ge(o_var, 1)
            a(ors, ors, ACT.Sqrt).then_inc(o_rt, 1)

            for kind, i in STEPS:
                if kind == "att":
                    for h in range(AH):
                        act.wait_ge(pr_max, AH * i + h + 1)
                        n = P * (i + 1)
                        a(prob[h % 2][:, 0:n], prob[h % 2][:, 0:n], ACT.Exp, bias=nmx[:, h:h + 1],
                          accum_out=den[:, h:h + 1]).then_inc(pr_exp, 1)
                        if h >= 1:
                            copy_pt(i, h - 1)
                    copy_pt(i, AH - 1)
                    wait_taken(act, "pv", i)
                    a(prob[0], mixed[:, i, 512:1024], ACT.Square).then_inc(at_sq, 1)
                    act.wait_ge(at_var, i + 1)
                    a(ars, ars, ACT.Sqrt).then_inc(at_rt, 1)
                if kind == "mo":
                    wait_taken(act, "out", i, 0)
                    wait_taken(act, "out", i, 1)
                    if i >= 1:
                        act.wait_ge(x2_sq, i)
                    a(part(M + 1024 * i, 1024), xs[:, i, :], ACT.Square, accum_out=ssq2[:, i:i + 1]).then_inc(x2_sq, 1)
                    act.wait_ge(x2_var, i + 1)
                    a(rstd2[:, i:i + 1], rstd2[:, i:i + 1], ACT.Sqrt).then_inc(x2_rt, 1)
                    act.wait_ge(h2_done, i + 1)
                    act.dma_start(XN[i * P:(i + 1) * P, :], h2tok[i % 2]).then_inc(h2_out[i % 2], 16)
                if kind == "rt":
                    for half in range(2):
                        wait_filled(act, "hT2", i, half)
                        take(a(h2T[i % 2].rearrange("p k t -> p (k t)")[:, half * 512:(half + 1) * 512], bank(("hT2", i, half))[:], ACT.Copy),
                             "hT2", i, half)
                    act.wait_ge(r_exp_in, 2 * i + 1)
                    a(gex, gex, ACT.Exp, accum_out=gsum).then_inc(r_exp, 1)
                    act.wait_ge(r_exp_in, 2 * i + 2)
                    a(t4[:, 1:2], t4[:, 0:1], ACT.Exp).then_inc(r_exp, 1)

            for c in range(NCH):
                act.wait_ge(xg_turned, c + 1)
                a(xt[:, 4:8, c * P:(c + 1) * P], PS[4 * (c % 2) + 1][:].rearrange("p (k t) -> p k t", k=4), ACT.Copy).then_inc(xt_a, 1)

            def y_copy(b0, first, done):
                a(yt[:, 0:4, bass.ds(first, WIN)], PS[b0][:, 0:4 * WIN].rearrange("p (k t) -> p k t", k=4), ACT.Copy).then_inc(done, 1)

            def more(e):
                count = act.value_load(ctl[0:1, bass.ds(e + NE, 1)], min_val=0, max_val=MORE)
                with act.If(count > 0):
                    before = act.value_load(ctl[0:1, bass.ds(e + 2 * NE, 1)], min_val=0, max_val=NCH + 3)
                    with act.Fori(0, count) as w:
                        act.wait_ge(e_h, before + w + 1)
                        a(sil[2], PS[4][:, 0:2 * WIN], ACT.Silu).then_inc(e_sil, 1)
                        first = act.value_load(ctl[0:1, bass.ds(e * MORE + w + 3 * NE, 1)], min_val=0, max_val=NA)
                        act.wait_ge(e_y, before + w + 1)
                        y_copy(5, first, e_yc_a)

            act.wait_ge(ctl_done, 1)
            for e in range(WSLOTS):
                more(e)
                act.wait_ge(m_h, e + 1)
                a(sil[e % 2], PS[e % 2][:, 0:2 * WIN], ACT.Silu).then_inc(m_sil, 1)
                if e >= 1:
                    first = first_of(act, e - 1)
                    act.wait_ge(m_y, e)
                    y_copy(2, first, m_yc_a)
            with act.Fori(1, NE // WSLOTS) as r:
                for s in range(WSLOTS):
                    more(r * WSLOTS + s)
                    act.wait_ge(m_h, r * WSLOTS + s + 1)
                    a(sil[s % 2], PS[s % 2][:, 0:2 * WIN], ACT.Silu).then_inc(m_sil, 1)
                    first = first_of(act, r * WSLOTS + (s - 1))
                    act.wait_ge(m_y, r * WSLOTS + s)
                    y_copy(2, first, m_yc_a)
            first = first_of(act, NE - 1)
            act.wait_ge(m_y, NE)
            y_copy(2, first, m_yc_a)
            for c in range(NCH):
                act.wait_ge(y_turned, c + 1)
                if c >= 4:
                    act.wait_ge(y_out[c % 4], 16)
                a(yrow[c % 4][:, 512:1024], PS[4 * (c % 2) + 1][:], ACT.Copy).then_inc(y_row_a, 1)
            for i in range(NT):
                act.wait_ge(f_sum, i + 1)
                if i:
                    act.wait_ge(f_sq, i)
                a(junk, xs[:, i, :], ACT.Square, accum_out=fssq[:, i:i + 1]).then_inc(f_sq, 1)
                act.wait_ge(f_var, i + 1)
                a(frstd[:, i:i + 1], frstd[:, i:i + 1], ACT.Sqrt).then_inc(f_rt, 1)

        @block.vector
        def _(v):
            steps = [0]

            def chain(ins):
                ins.then_inc(dve_step, 1)
                steps[0] += 1
                v.wait_ge(dve_step, steps[0])

            def variance(out_, in_, n, done):
                v.tensor_scalar(out_, in_, 1.0 / n, EPS, ALU.mult, ALU.add).then_inc(done, 1)

            v.wait_ge(cst_in, 48)
            for i in range(NT):
                v.wait_ge(x_sq, i + 1)
                variance(rstd[:, i:i + 1], ssq[:, i:i + 1], D, x_var)
                v.wait_ge(x_rt, i + 1)
                chain(v.reciprocal(rstd[:, i:i + 1], rstd[:, i:i + 1]))
                if i >= 2:
                    wait_filled(v, "xT", i - 2, 1)
                v.tensor_scalar(xn[i % 2], xs[:, i, :], rstd[:, i:i + 1], None, ALU.mult).then_inc(xn_done, 1)
                for half in range(2):
                    ps = wait_filled(v, "xT", i, half)
                    w = vec[:, V_MIX + 4 * half:V_MIX + 4 * half + 4].unsqueeze(2).to_broadcast([P, 4, P])
                    take(v.tensor_tensor(hT[:, 4 * half:4 * half + 4, i * P:(i + 1) * P],
                                         ps[:].rearrange("p (c t) -> p c t", c=4), w, ALU.mult), "xT", i, half)
            lb_in = vec[:, V_LB:V_LB + 4]
            v.tensor_tensor(lbw[:, 0:4], lb_in, lb_in, ALU.subtract).then_inc(zprep_v, 1)
            v.wait_ge(zprep_a, 1)
            chain(v.reciprocal(lbw[:, 8:12], lbw[:, 4:8]))
            chain(v.tensor_tensor(lbw[:, 8:12], lbw[:, 8:12], lbw[:, 4:8], ALU.mult))
            v.tensor_tensor(lbw[:, 8:12], lbw[:, 8:12], lbw[:, 8:12], ALU.subtract).then_inc(zprep_v, 1)
            for j in range(4):
                ps = wait_filled(v, "f", j)
                take(v.tensor_copy(bcum[:, j * 512:(j + 1) * 512], ps[:]), "f", j)
            for j in range(4):
                wait_taken(v, "f", j)
            v.wait_ge(zprep_a, 3)
            v.scalar_tensor_tensor(L[1], L[0], 2.0, bcum, ALU.mult, ALU.add).then_inc(zprep_v, 1)
            v.wait_ge(zprep_a, 4)
            v.tensor_tensor(L[0], L[0], L[1], ALU.add).then_inc(zprep_v, 1)
            v.wait_ge(zprep_v, 4)
            v.tensor_tensor(L[1], bcum, L[0], ALU.add).then_inc(zprep_v, 1)
            v.wait_ge(zprep_a, 8)
            v.tensor_scalar(L[1], bcum, -80.0, None, ALU.max).then_inc(zprep_v, 1)
            v.wait_ge(zprep_a, 9)
            chain(v.tensor_tensor(L[1], L[1], L[0], ALU.subtract))
            v.wait_ge(cleared, 1)
            for h in range(RH):
                ins = v.tensor_tensor_scan(bcum[:, h * 512:(h + 1) * 512], acc, L[1][:, h * 512:(h + 1) * 512], 0.0, ALU.mult, ALU.add)
            chain(ins)

            bv = bcum.rearrange("p (n t) -> p n t", t=P)

            def diff(li):
                hs = HALVES[li]
                b4 = bcum.rearrange("p (n s t) -> p n s t", s=2, t=hs)
                l4 = L[li % 2].rearrange("p (n s t) -> p n s t", s=2, t=hs)
                mid = b4[:, :, 0, hs - 1:hs].to_broadcast([P, 1024 // hs, hs])
                v.tensor_tensor(l4[:, :, 0, :], mid, b4[:, :, 0, :], ALU.subtract)
                v.tensor_tensor(l4[:, :, 1, :], b4[:, :, 1, :], mid, ALU.subtract).then_inc(lv_sub, 1)

            def operands(li):
                hs = HALVES[li]
                l4, k4, q4 = (t.rearrange("p (n s t) -> p n s t", s=2, t=hs) for t in (L[li % 2], kT, qT))
                v.wait_ge(lv_exp, li + 1)
                v.tensor_tensor(l4[:, :, 0, :], l4[:, :, 0, :], k4[:, :, 0, :], ALU.mult)
                v.tensor_tensor(l4[:, :, 1, :], l4[:, :, 1, :], q4[:, :, 1, :], ALU.mult).then_inc(lv_mul, 1)

            def masked(ps, m):
                w = cst[:, C_MASK + 32 * m:C_MASK + 32 * m + 32].unsqueeze(1).to_broadcast([P, 16, 32])
                return ps[:].rearrange("p (b t) -> p b t", t=32), w

            acc3 = acc.rearrange("p (b t) -> p b t", t=32)
            tmp3 = part(M, 512).rearrange("p (b t) -> p b t", t=32)

            def place(li):
                if li == 0:
                    for half in range(2):
                        ps = wait_filled(v, "level", 0, half)
                        take(v.tensor_copy(Sasm[0:64, 8 * half:8 * half + 8, 64:128],
                                           ps[0:64, :].rearrange("p (b t) -> p b t", t=64)), "level", 0, half)
                elif li == 1:
                    ps = wait_filled(v, "level", 1, 0)
                    v.tensor_copy(Sasm[0:32, :, 32:64], ps[0:32, :].rearrange("p (b t) -> p b t", t=32))
                    take(v.tensor_copy(Sasm[64:96, :, 96:128], ps[64:96, :].rearrange("p (b t) -> p b t", t=32)), "level", 1, 0)
                else:
                    ps = wait_filled(v, "level", li, 0)
                    take(v.tensor_tensor(tmp3, *masked(ps, li - 2), ALU.mult), "level", li, 0)
                    wait_taken(v, "level", li, 0)
                    chain(v.tensor_tensor(acc3, acc3, tmp3, ALU.add))

            diff(0)
            diff(1)
            v.wait_ge(cleared, 2)
            ps = wait_filled(v, "diag")
            take(v.tensor_tensor(acc3, *masked(ps, 5), ALU.mult), "diag")
            wait_taken(v, "diag")
            for j in range(4):
                wait_taken(v, "q", j)
            operands(0)
            operands(1)
            for li in range(2, 7):
                wait_filled(v, "level", li - 2, 1 if li == 2 else 0)
                diff(li)
                place(li - 2)
                operands(li)
            place(5)
            v.wait_ge(lv_exp, 8)
            v.tensor_tensor(L[1], L[1], qT, ALU.mult).then_inc(lv_mul, 1)
            wait_filled(v, "level", 6, 0)
            last_b = bv[:, :, P - 1:P].to_broadcast([P, 16, P])
            v.tensor_tensor(L[0].rearrange("p (n t) -> p n t", t=P), last_b, bv, ALU.subtract).then_inc(lv_sub, 1)
            place(6)
            for j in range(4):
                ins = v.tensor_copy(Sasm[32 * j:32 * j + 32, :, 32 * j:32 * j + 32], acc3[32 * j:32 * j + 32])
            ins.then_inc(sasm_done, 1)
            v.wait_ge(lv_exp, 9)
            v.tensor_tensor(L[0], L[0], kT, ALU.mult).then_inc(lv_mul, 1)
            v.wait_ge(lv_mul, 9)
            for c in range(3):
                ps = wait_filled(v, "delta", c)
                if c == 0:
                    take(v.tensor_copy(states[:, 0, :], ps[:]), "delta", 0)
                else:
                    for h in range(RH):
                        ins = v.scalar_tensor_tensor(states[:, c, h * P:(h + 1) * P], states[:, c - 1, h * P:(h + 1) * P],
                                                     ebl[:, 4 * h + c:4 * h + c + 1], ps[:, h * P:(h + 1) * P], ALU.mult, ALU.add)
                    take(ins, "delta", c)
                wait_taken(v, "delta", c)
            v.wait_ge(o_sq, 16)
            variance(ors, oss, P, o_var)
            v.wait_ge(o_rt, 1)
            chain(v.reciprocal(ors, ors))
            for c in range(NT):
                ps = bank(("o", c))
                wait_taken(v, "g", c)
                for h in range(RH):
                    cols = slice(h * P, (h + 1) * P)
                    ins = v.scalar_tensor_tensor(mixed[:, c, cols], ps[:, cols], ors[:, 4 * c + h:4 * c + h + 1], mixed[:, c, cols],
                                                 ALU.mult, ALU.mult)
                take(ins, "o", c)
            def rel_bias(h, n):
                return bass.AP(arena, R + 512 * h + n - 1, [[arena.shape[1], P], [-1, n]])

            v.wait_ge(bias_in, 16)
            chain(v.memset(bias[0:64, :, 0:64], NEG))
            for kind, i in STEPS:
                if kind == "att":
                    n = P * (i + 1)
                    for h in range(AH):
                        ps = wait_filled(v, "score", i, h)
                        if h >= 2:
                            wait_filled(v, "pT", i, h - 2)
                        elif i:
                            v.wait_ge(at_sq, i)
                        take(v.tensor_tensor_reduce(prob[h % 2][:, 0:n], ps[:, 0:n], rel_bias(h, n), 1.0, -3.0e38,
                                                    ALU.add, ALU.max, mx[:, h:h + 1]), "score", i, h)
                        wait_taken(v, "score", i, h)
                        v.tensor_scalar(nmx[:, h:h + 1], mx[:, h:h + 1], -1.0, None, ALU.mult).then_inc(pr_max, 1)
                    v.wait_ge(pr_exp, AH * (i + 1))
                    chain(v.reciprocal(rden, den))
                    ps = wait_filled(v, "pv", i)
                    o3 = mixed[:, i, 512:1024].rearrange("p (h d) -> p h d", h=AH)
                    take(v.tensor_tensor(o3, ps[:].rearrange("p (h d) -> p h d", h=AH),
                                         rden.unsqueeze(2).to_broadcast([P, AH, AD]), ALU.mult), "pv", i)
                    wait_taken(v, "pv", i)
                    v.wait_ge(at_sq, i + 1)
                    chain(v.tensor_reduce(ams, prob[0].rearrange("p (h d) -> p h d", h=AH), AX_X, ALU.add))
                    variance(ars, ams, AD, at_var)
                    v.wait_ge(at_rt, i + 1)
                    chain(v.reciprocal(ars, ars))
                    v.tensor_tensor(o3, o3, ars.unsqueeze(2).to_broadcast([P, AH, AD]), ALU.mult).then_inc(at_done, 1)
                if kind == "mo":
                    for half in range(2):
                        ps = wait_filled(v, "mT", i, half)
                        w = vec[:, V_OUT + 4 * half:V_OUT + 4 * half + 4].unsqueeze(2).to_broadcast([P, 4, P])
                        take(v.tensor_tensor(mixT[i % 2][:, 4 * half:4 * half + 4, :], ps[:].rearrange("p (c t) -> p c t", c=4), w,
                                             ALU.mult), "mT", i, half)
                    for half in range(2):
                        ps = wait_filled(v, "out", i, half)
                        cols = slice(512 * half, 512 * half + 512)
                        take(v.tensor_tensor(xs[:, i, cols], xs[:, i, cols], ps[:], ALU.add), "out", i, half)
                    wait_taken(v, "out", i, 0)
                    wait_taken(v, "out", i, 1)
                    v.wait_ge(x2_sq, i + 1)
                    variance(rstd2[:, i:i + 1], ssq2[:, i:i + 1], D, x2_var)
                    v.wait_ge(x2_rt, i + 1)
                    chain(v.reciprocal(rstd2[:, i:i + 1], rstd2[:, i:i + 1]))
                    if i == 0:
                        v.wait_ge(bc_in, 16)
                    if i >= 2:
                        wait_filled(v, "hT2", i - 2, 1)
                        v.wait_ge(h2_out[i % 2], 16)
                    turn = "p (d k) -> p k d"
                    v.scalar_tensor_tensor(h2tok[i % 2].rearrange("p (k d) -> p k d", k=KD), xs[:, i, :].rearrange(turn, k=KD),
                                           rstd2[:, i:i + 1], bc_ffn.rearrange(turn, k=KD), ALU.mult, ALU.mult).then_inc(h2_done, 1)
                if kind == "rt":
                    ps = wait_filled(v, "logit", i)
                    take(v.tensor_copy(lg, ps[:, 0:36]), "logit", i)
                    if i == 0:
                        v.memset(gpad, NEG).then_inc(dve_step, 1)
                        steps[0] += 1
                        v.wait_ge(dve_step, steps[0])
                    wait_taken(v, "logit", i)
                    chain(v.tensor_copy(gpad[:, 0:NG], lg[:, 0:NG]))
                    chain(v.max(gm8, gpad))
                    chain(v.max_index(top_idx[:, 0:8], gm8, gpad))
                    chain(v.tensor_copy(t4[:, 4:5], top_idx[:, 0:1]))
                    chain(v.tensor_scalar(goh, iota[:, 0:NG], t4[:, 4:5], None, ALU.is_equal))
                    chain(v.tensor_scalar(goh, goh, -1.0, -NEG, ALU.add, ALU.mult))
                    v.tensor_scalar(gex, lg[:, 0:NG], gm8[:, 0:1], None, ALU.subtract).then_inc(r_exp_in, 1)
                    chain(v.tensor_tensor(em.rearrange("p (g e) -> p g e", g=NG), lg[:, NG:36].rearrange("p (g e) -> p g e", g=NG),
                                          goh.unsqueeze(2).to_broadcast([P, NG, EPG]), ALU.add))
                    chain(v.max(em8, em))
                    chain(v.max_index(top_idx[:, 8:16], em8, em))
                    v.tensor_tensor(t4[:, 0:1], em8[:, 1:2], em8[:, 0:1], ALU.subtract).then_inc(r_exp_in, 1)
                    chain(v.tensor_copy(expid[:, 2 * i:2 * i + 2], top_idx[:, 8:10]))
                    for k in range(2):
                        ins = v.tensor_scalar(A12[:, 32 * k:32 * k + 32], iota[:, 0:NE], expid[:, 2 * i + k:2 * i + k + 1], None, ALU.is_equal)
                    chain(ins)
                    v.tensor_tensor(A[:, i, :], A12[:, 0:32], A12[:, 32:64], ALU.add).then_inc(assign_done, 1)
                    v.wait_ge(r_exp, 2 * i + 2)
                    chain(v.tensor_scalar(t4[:, 2:3], t4[:, 1:2], 1.0, None, ALU.add))
                    chain(v.tensor_tensor(t4[:, 2:3], t4[:, 2:3], gsum, ALU.mult))
                    chain(v.reciprocal(gate[:, i, 0:1], t4[:, 2:3]))
                    chain(v.tensor_tensor(gate[:, i, 1:2], gate[:, i, 0:1], t4[:, 1:2], ALU.mult))
                if kind == "sort":
                    i8 = iota[:, 0:NE].unsqueeze(1).unsqueeze(1).to_broadcast([P, NT, 2, NE])
                    chain(v.tensor_tensor(hot, i8, expid.rearrange("p (i k) -> p i k", k=2).unsqueeze(3).to_broadcast([P, NT, 2, NE]),
                                          ALU.is_equal))
                    chain(v.tensor_scalar(edges, iota[:, 1:9], float(P), None, ALU.mult))
                    ps = wait_filled(v, "rank")
                    chain(v.tensor_copy(cnt, ps[:, NT * NE:(NT + 1) * NE]))
                    chain(v.tensor_tensor_scan(incl, ones_[:, 0:NE], cnt, 0.0, ALU.mult, ALU.add))
                    chain(v.tensor_tensor(off, incl, cnt, ALU.subtract))
                    rank4 = ps[:, 0:NT * NE].rearrange("p (i e) -> p i e", i=NT).unsqueeze(2).to_broadcast([P, NT, 2, NE])
                    take(v.tensor_tensor(hotw, hot, rank4, ALU.mult), "rank")
                    chain(v.tensor_tensor(hot, hot, off.unsqueeze(1).unsqueeze(1).to_broadcast([P, NT, 2, NE]), ALU.mult))
                    wait_taken(v, "rank")
                    chain(v.tensor_tensor(hotw, hotw, hot, ALU.add))
                    chain(v.tensor_reduce(pos, hotw.rearrange("p i k e -> p (i k) e"), AX_X, ALU.add))
                    chain(v.tensor_tensor(over, pos.unsqueeze(2).to_broadcast([P, NCH, 8]),
                                          edges.unsqueeze(1).to_broadcast([P, NCH, 8]), ALU.is_ge))
                    chain(v.tensor_reduce(chunk, over, AX_X, ALU.add))
                    chain(v.scalar_tensor_tensor(within, chunk, -float(P), pos, ALU.mult, ALU.add))
                    chain(v.tensor_tensor(onehot_c, iota[:, 0:NCH].unsqueeze(1).to_broadcast([P, NCH, NCH]),
                                          chunk.unsqueeze(2).to_broadcast([P, NCH, NCH]), ALU.is_equal))
                    chain(v.tensor_tensor(onehot_c, onehot_c, cst[:, C_TOK:C_TOK + NCH].unsqueeze(2).to_broadcast([P, NCH, NCH]), ALU.mult))
                    v.tensor_tensor(onehot_p, iota.unsqueeze(1).to_broadcast([P, NCH, P]),
                                    within.unsqueeze(2).to_broadcast([P, NCH, P]), ALU.is_equal).then_inc(oh_done, 1)
                    ps = wait_filled(v, "list")
                    take(v.tensor_copy(idx[:], ps[:, 0:NCH]), "list")
                    wait_taken(v, "list")
                    v.tensor_copy(pos_u[:], pos).then_inc(idx_done, 1)
                    n1, o1 = cnt[0:1], off[0:1]
                    W0 = SC
                    tbl = part(W0, NE * (3 + MORE))[0:1]
                    tw = part(W0 + NE * (3 + MORE), NE * MORE)[0:1].rearrange("p (e w) -> p e w", w=MORE)
                    wl = part(W0 + NE * (3 + 2 * MORE), MORE)[0:1]
                    rest = part(W0 + NE * (3 + 2 * MORE) + 8, NE)[0:1]
                    chain(v.tensor_copy(tbl[:, 0:NE], o1))
                    chain(v.tensor_scalar(wl, iota[0:1, 1:1 + MORE], float(WIN), None, ALU.mult))
                    wlb = wl.unsqueeze(1).to_broadcast([1, NE, MORE])
                    chain(v.tensor_tensor(tw, n1.unsqueeze(2).to_broadcast([1, NE, MORE]), wlb, ALU.is_gt))
                    chain(v.tensor_reduce(tbl[:, NE:2 * NE], tw, AX_X, ALU.add))
                    chain(v.tensor_tensor_scan(rest, ones_[0:1, 0:NE], tbl[:, NE:2 * NE], 0.0, ALU.mult, ALU.add))
                    chain(v.tensor_tensor(tbl[:, 2 * NE:3 * NE], rest, tbl[:, NE:2 * NE], ALU.subtract))
                    chain(v.tensor_scalar(rest, n1, -float(WIN), None, ALU.add))
                    st = tbl[:, 3 * NE:].rearrange("p (e w) -> p e w", w=MORE)
                    chain(v.tensor_tensor(tw, rest.unsqueeze(2).to_broadcast([1, NE, MORE]), wlb, ALU.min))
                    chain(v.tensor_tensor(st, tw, o1.unsqueeze(2).to_broadcast([1, NE, MORE]), ALU.add))
                    v.tensor_copy(ctl[:], tbl).then_inc(ctl_done, 1)

            for c in range(NCH):
                v.wait_ge(xg_turned, c + 1)
                v.tensor_copy(xt[:, 0:4, c * P:(c + 1) * P], PS[4 * (c % 2)][:].rearrange("p (k t) -> p k t", k=4)).then_inc(xt_v, 1)

            def hidden(ps, b, done):
                v.tensor_tensor(hid[b], sil[b], ps[:, 2 * WIN:4 * WIN], ALU.mult).then_inc(done, 1)

            def y_copy(b0, first, done):
                v.tensor_copy(yt[:, 4:8, bass.ds(first, WIN)], PS[b0 + 1][:, 0:4 * WIN].rearrange("p (k t) -> p k t", k=4)).then_inc(done, 1)

            def more(e):
                count = v.value_load(ctl[0:1, bass.ds(e + NE, 1)], min_val=0, max_val=MORE)
                with v.If(count > 0):
                    before = v.value_load(ctl[0:1, bass.ds(e + 2 * NE, 1)], min_val=0, max_val=NCH + 3)
                    with v.Fori(0, count) as w:
                        v.wait_ge(e_sil, before + w + 1)
                        hidden(PS[4], 2, e_hid)
                        first = v.value_load(ctl[0:1, bass.ds(e * MORE + w + 3 * NE, 1)], min_val=0, max_val=NA)
                        v.wait_ge(e_y, before + w + 1)
                        y_copy(5, first, e_yc_v)

            v.wait_ge(ctl_done, 1)
            for e in range(WSLOTS):
                more(e)
                v.wait_ge(m_sil, e + 1)
                hidden(PS[e % 2], e % 2, m_hid)
                if e >= 1:
                    first = first_of(v, e - 1)
                    v.wait_ge(m_y, e)
                    y_copy(2, first, m_yc_v)
            with v.Fori(1, NE // WSLOTS) as r:
                for s in range(WSLOTS):
                    more(r * WSLOTS + s)
                    v.wait_ge(m_sil, r * WSLOTS + s + 1)
                    hidden(PS[s % 2], s % 2, m_hid)
                    first = first_of(v, r * WSLOTS + (s - 1))
                    v.wait_ge(m_y, r * WSLOTS + s)
                    y_copy(2, first, m_yc_v)
            first = first_of(v, NE - 1)
            v.wait_ge(m_y, NE)
            y_copy(2, first, m_yc_v)
            for c in range(NCH):
                v.wait_ge(y_turned, c + 1)
                if c >= 4:
                    v.wait_ge(y_out[c % 4], 16)
                v.tensor_copy(yrow[c % 4][:, 0:512], PS[4 * (c % 2)][:]).then_inc(y_row_v, 1)
            for i in range(NT):
                v.wait_ge(f_in[i], 32)
                if i == 0:
                    v.wait_ge(bc2_in, 16)
                chain(v.scalar_tensor_tensor(xs[:, i, :], yin[2 * i], gate[:, i, 0:1], xs[:, i, :], ALU.mult, ALU.add))
                v.scalar_tensor_tensor(xs[:, i, :], yin[2 * i + 1], gate[:, i, 1:2], xs[:, i, :], ALU.mult, ALU.add).then_inc(f_sum, 1)
                v.wait_ge(f_sq, i + 1)
                variance(frstd[:, i:i + 1], fssq[:, i:i + 1], D, f_var)
                v.wait_ge(f_rt, i + 1)
                chain(v.reciprocal(frstd[:, i:i + 1], frstd[:, i:i + 1]))
                v.scalar_tensor_tensor(xs[:, i, :], xs[:, i, :], frstd[:, i:i + 1], bc_fin, ALU.mult, ALU.mult).then_inc(f_done, 1)


def constant_table():
    c = np.zeros((P, C_END), np.float32)
    p, t = np.arange(P)[:, None], np.arange(P)[None, :]
    c[:, C_ID:C_ID + P] = p == t
    c[:, C_UP:C_UP + P] = p < t
    c[:, C_ONE:C_ONE + P] = 1
    c[:, C_IOTA:C_IOTA + P] = t
    s, q = np.arange(P)[:, None] % 32, np.arange(32)[None, :]
    for m, h in enumerate(HALVES[2:]):
        c[:, C_MASK + 32 * m:C_MASK + 32 * m + 32] = (s // (2 * h) == q // (2 * h)) & (s // h % 2 == 0) & (q // h % 2 == 1)
    c[:, C_MASK + 160:C_MASK + 192] = s == q
    for i in range(NT):
        for k in range(2):
            c[:, C_TOK + 2 * i + k] = P * i + np.arange(P)
    return c


def kernel(x, norm_mix_w, w_in, hgrn_lower_bounds, hgrn_gnorm_w, attn_rel_bias, attn_norm_w, w_out, norm_ffn_w,
           moe_w_group, moe_w_expert, moe_w1, moe_w3, moe_w2, final_norm_w):
    import concourse.bacc as bacc
    from concourse.bass_utils import run_bass_kernel_spmd

    f = np.ascontiguousarray
    order = np.minimum(np.arange(639) + 1, NREL - 1)
    arrays = {
        "x": f(np.asarray(x)[0]),
        "w_in": f(np.asarray(w_in)[0]),
        "w_out": f(np.asarray(w_out)[0]),
        "rel_ext": f(np.asarray(attn_rel_bias)[0][:, order]),
        "vecs": f(np.concatenate([np.asarray(a)[0].reshape(-1, P).T for a in (norm_mix_w, hgrn_lower_bounds, hgrn_gnorm_w, attn_norm_w)], axis=1)),
        "w_route": f(np.concatenate([np.asarray(moe_w_group)[0], np.asarray(moe_w_expert)[0]], axis=1).reshape(P, KD, 36)),
        "norm_ffn": f(np.asarray(norm_ffn_w)[0]),
        "norm_final": f(np.asarray(final_norm_w)),
        "w1": f(np.asarray(moe_w1)[0]),
        "w3": f(np.asarray(moe_w3)[0]),
        "w2": f(np.asarray(moe_w2)[0]),
        "consts": constant_table(),
    }
    nc = bacc.Bacc("TRN2", target_bir_lowering=False, num_devices=1)
    args = [nc.dram_tensor(f"in_{n}", a.shape, mybir.dt.from_np(a.dtype), kind="ExternalInput").ap() for n, a in arrays.items()]
    args.append(nc.dram_tensor("out_rows", (T, D), F32, kind="ExternalOutput").ap())
    trunk(nc, *args)
    r = run_bass_kernel_spmd(nc, [{f"in_{n}": a for n, a in arrays.items()}], core_ids=[0])
    return r.results[0]["out_rows"].reshape(1, T, D)
```

```python
from contextlib import ExitStack

import numpy as np
import concourse.bass as bass
from concourse import mybir

ALU = mybir.AluOpType
ACT = mybir.ActivationFunctionType
AX_X = mybir.AxisListType.X
F32 = mybir.dt.float32
I32 = mybir.dt.int32
BF16 = mybir.dt.bfloat16
U32 = mybir.dt.uint32

P = 128
T = 512
D = 1024
NT = T // P
KD = D // P
RH = 4
AH, AD = 8, 64
NREL = 257
NG, NE, EPG, FF = 4, 32, 8, 256
NA = 2 * T
NCH = NA // P
WIN = 64
MORE = (T - 1) // WIN
EXTRA = NA // WIN
SL = NA + WIN
CLEARS = 16 * EXTRA * WIN // (2 * P)
EPS = 1e-6
NEG = -1e30
HALVES = [64, 32, 16, 8, 4, 2, 1]
WSLOTS = 5
PEEL, BODY = 7, 5
TURN = [0, 1, 0, 1, 2]
W13, W2 = KD * FF, 2 * D

C_ID, C_UP, C_ONE, C_IOTA, C_MASK, C_TOK, C_END = 0, 128, 256, 384, 512, 704, 720
V_MIX, V_LB, V_OUT, V_END = 0, 8, 12, 20
ARENA = 52800
GROUPS = ["f", "q", "v", "ak", "aq", "av", "g"]
GROUP_COL = {"q": 0, "f": 512, "v": 1024, "g": 1536, "aq": 2048, "ak": 2560, "av": 3072}
GROUP_BUF = {"f": 0, "q": 1, "v": 2, "ak": 3, "aq": 0, "av": 1, "g": 2}


def psum_plan():
    seen, plan = [0] * 8, {}

    def use(bank, *name):
        plan[name] = (bank, seen[bank])
        seen[bank] += 1

    for i in range(NT):
        for half in range(2):
            use(2 + (2 * i + half) % 4, "xT", i, half)
    n = 0
    for g in ("f", "q", "v", "ak"):
        for j in range(4):
            use(n % 2, g, j)
            n += 1
    use(6, "diag")
    blocks = [("aq", 0), ("aq", 1), ("aq", 2), ("aq", 3), ("av", 0), ("av", 1), ("av", 2), ("av", 3)]
    for li in range(7):
        use(n % 2, *blocks[li])
        n += 1
        if li == 0:
            use(2, "level", 0, 0)
            use(3, "level", 0, 1)
        else:
            use([4, 5, 2, 3, 4, 5][li - 1], "level", li, 0)
    use(n % 2, "av", 3)
    n += 1
    for c, b in enumerate((6, 7, 2)):
        use(b, "kT", c)
    use(n % 2, "g", 0)
    n += 1
    for c, b in enumerate((3, 4, 5)):
        use(b, "delta", c)
    use(n % 2, "g", 1)
    n += 1
    for c, b in enumerate((6, 7, 2, 3)):
        use(b, "o", c)
    for step in STEPS:
        kind, i = step[0], step[1]
        if kind == "g" and step[2] == 0:
            use(n % 2, "g", i)
            n += 1
        if kind == "score":
            use(4 + step[2] % 2, "score", i, step[2])
        if kind == "turn":
            use(2 + step[2] % 2, "pT", i, step[2])
        if kind == "value" and step[2] == 0:
            use(6 + i % 2, "pv", i)
        if kind == "mixT":
            use(6 + i % 2 if i < NT - 1 else 2 + step[2], "mT", i, step[2])
        if kind == "out" and step[3] == 0:
            use(step[2], "out", i, step[2])
        if kind == "h2T":
            use((6, 6, 4 + step[2], 2 + step[2])[i], "hT2", i, step[2])
        if kind == "logit":
            use(6, "logit", i)
        if kind == "rank" and i == 0:
            use(7, "rank", 0)
        if kind == "sort":
            use(4, "list")
    return plan, seen


def steps_after_recurrence():
    beats = [[] for _ in range(NT * AH + 17)]

    def put(beat, *step):
        beats[beat].append(step)

    for c in range(NT):
        put(c, "o_squares", c)
    put(NT - 1, "o_root", 0)
    for q in range(8):
        put(q, "g", 2 + q // 4, q % 4)
    for b, c in ((6, 0), (7, 1), (11, 2), (12, 3)):
        put(b, "gate", c)
    put(9, "silu_g", 2)
    put(9, "silu_g", 3)
    for i in range(NT):
        at = 8 * i + 10
        outs = (15, 23, 32, 40)[i]
        for b, *step in ((at + 2, "att_scale", i), (outs - 2, "mixT", i, 0), (outs - 1, "mixT", i, 1),
                         *((outs + q, "out", i, q // 4, q % 4) for q in range(8)),
                         (outs + 8, "ffn_in", i)):
            put(b, *step)
        after = outs + 8
        for b, *step in ((after, "h2", i), (after + 4, "h2T", i, 0), (after + 5, "h2T", i, 1), (after + 6, "logit", i),
                         (after + 7, "h2_scaled", i), (after + 7, "route", i)):
            put(min(b, len(beats) - 1), *step)
    for b, i in ((42, 0), (42, 1), (len(beats) - 1, 2), (len(beats) - 1, 3)):
        put(b, *(("rank", i) if i < 3 else ("sort", 0)))
    steps = []
    for u, between in enumerate(beats):
        if u < NT * AH and u % 2 == 0:
            steps += [("score", u // AH, u % AH), ("score", u // AH, u % AH + 1)]
        steps += between
        if 0 <= u - 2 < NT * AH:
            steps.append(("turn", (u - 2) // AH, (u - 2) % AH))
        if 0 <= u - 3 < NT * AH:
            steps.append(("value", (u - 3) // AH, (u - 3) % AH))
            if (u - 3) % AH == AH - 1:
                steps.append(("att_norm", (u - 3) // AH))
    return steps


STEPS = steps_after_recurrence()
PLAN, BANK_USES = psum_plan()


def trunk(nc, x, w_in, w_out, rel_ext, vecs, w_route, norm_ffn, norm_final, w1, w3, w2, consts, out):
    ctx = ExitStack()
    with ctx:
        def sem(name):
            return ctx.enter_context(nc.semaphore(name))

        arena = ctx.enter_context(nc.sbuf_tensor("arena", [P, ARENA], F32))
        idx = ctx.enter_context(nc.sbuf_tensor("idx", [P, NCH], U32))
        pos_u = ctx.enter_context(nc.sbuf_tensor("pos_u", [P, NCH], U32))
        top_idx = ctx.enter_context(nc.sbuf_tensor("top_idx", [P, 16], U32))
        ctl = ctx.enter_context(nc.sbuf_tensor("ctl", [1, NE * (3 + MORE)], I32))
        PS = [ctx.enter_context(nc.psum_tensor(f"bank{b}", [P, 512], F32)) for b in range(8)]

        def part(at, size):
            return arena[:, at:at + size]

        xs = part(0, 4096).rearrange("p (i d) -> p i d", i=NT)
        ring = [part(4096 + 4096 * b, 4096).rearrange("p (k n) -> p k n", k=KD) for b in range(4)]
        hT = part(20480, 4096).rearrange("p (k t) -> p k t", k=KD)
        wout = [ring[3], part(20480, 4096).rearrange("p (k n) -> p k n", k=KD)]
        up_slot = [part(at, 2 * W13) for at in (24576, 12288, 4096, 39424, 16384)]
        down_slot = [part(at, W2) for at in (28672, 10240, 8192, 43520, 20480)]
        R = 24576
        bcum = part(R, 2048)
        L = [part(R + 2048, 2048), part(R + 4096, 2048)]
        xn = [part(R + 2048 + 1024 * i, 1024) for i in range(NT)]
        kdT = part(R, 1536).rearrange("p (c n) -> p c n", c=3)
        BIAS = 4096
        bias = part(BIAS, 4096).rearrange("p (h n) -> p h n", h=AH)
        prob = [part(8192 + 512 * b, 512) for b in range(4)]
        probT = [part(8192 + 512 * (4 + b), 512) for b in range(4)]
        Q, K, S = 30720, 32768, 34816
        qT = part(Q, 2048)
        kT = part(K, 2048)
        states = part(Q, 1536).rearrange("p (c n) -> p c n", c=3)
        bc_ffn = part(Q, 1024)
        att_sq = part(Q + 1536, 512)
        Sasm = part(S, 2048).rearrange("p (b t) -> p b t", t=P)
        mixT = [part(K + 1024 * b, 1024).rearrange("p (k t) -> p k t", k=KD) for b in range(2)]
        h2T = [part(S + 1024 * b, 1024).rearrange("p (k t) -> p k t", k=KD) for b in range(2)]
        acc = part(36864, 512)
        V_, AQ, AK, AV = 37376, 39424, 41472, 43520
        vtok = part(V_, 2048).rearrange("p (c n) -> p c n", c=NT)
        h2tok = [part(V_, 1024), part(V_ + 1024, 1024)]
        aqT = part(AQ, 2048).rearrange("p (b t) -> p b t", b=4)
        akT = part(AK, 2048).rearrange("p (b t) -> p b t", b=4)
        avt = part(AV, 2048).rearrange("p (c n) -> p c n", c=NT)
        XT_ = 30720
        xt = part(XT_, KD * SL).rearrange("p (k t) -> p k t", k=KD)
        M = 45568
        mixed = part(M, 4096).rearrange("p (i n) -> p i n", i=NT)
        h2_scaled = [part(M + 1024 * i, 1024) for i in range(NT)]
        xg = [part(M + 1024 * b, 1024) for b in range(4)]
        SC = M + 1024
        onehot_p = part(SC, 512).bitcast(BF16).rearrange("p (a t) -> p a t", a=NCH)
        xwin = [part(M + 512 * b, 512).rearrange("p (k t) -> p k t", k=KD) for b in range(4)]
        y_rows = [part(M + 512 * (4 + b), 512) for b in range(4)]
        gu = [part(22528 + 256 * b, 256) for b in range(4)]
        sil, hid = ([part(at + WIN * 2 * b, 2 * WIN).rearrange("p (j t) -> p j t", j=2) for b in range(4)] for at in (23552, 24064))
        bc_fin = part(XT_ + 1024, 1024)
        yin = [part(4096 + 1024 * n, 1024) for n in range(2 * NT)]
        junk = part(XT_, 1024)
        cst = part(49664, C_END)
        vec = part(49664 + C_END, V_END)
        wr = part(49664 + C_END + V_END, KD * 36).rearrange("p (k n) -> p k n", k=KD)
        sm = 49664 + C_END + V_END + KD * 36 + 4
        small_at = [sm]

        def small(n):
            at = small_at[0]
            small_at[0] += n
            assert small_at[0] <= ARENA
            return part(at, n)

        ident, upper, ones_, iota = (cst[:, c:c + P] for c in (C_ID, C_UP, C_ONE, C_IOTA))

        ssq = small(NT)
        rstd = small(NT)
        lbw = small(16)
        ebl = small(16)
        oss, ors = small(16), small(16)
        mx, rden = small(8), small(8)
        nmx, den, ams, ars = ([small(8) for b in range(2)] for n in range(4))
        ssq2, rstd2 = small(NT), small(NT)
        gate = small(8).rearrange("p (i k) -> p i k", k=2)
        expid = small(8)
        fssq, frstd = small(NT), small(NT)
        root_scratch, pool_scratch = small(12), small(48)
        y_rows += [small(512) for b in range(WSLOTS - 3)]
        RW = 36864
        lg, gpad, gm8, goh, em, em8 = part(RW, 36), part(RW + 36, 8), part(RW + 44, 8), part(RW + 52, 4), part(RW + 56, 32), part(RW + 88, 8)
        gex, gsum, t4 = part(RW + 96, 4), part(RW + 100, 1), part(RW + 104, 8)
        A12 = part(RW + 112, 64)
        A = part(RW + 176, 128).rearrange("p (i e) -> p i e", i=NT)
        Apre = part(RW + 304, 96).rearrange("p (i e) -> p i e", i=3)
        S0 = 22528
        hot, hotw, hot1 = (part(S0 + 256 * n, 256).rearrange("p (i k e) -> p i k e", i=NT, k=2) for n in range(3))
        cnt, incl, off = (part(S0 + 768 + 32 * n, 32) for n in range(3))
        pos, chunk, within, edges, rank, row, late, wl = (part(S0 + 864 + 8 * n, 8) for n in range(8))
        wl = wl[:, 0:MORE]
        over = part(S0 + 928, 64).rearrange("p (a n) -> p a n", a=NCH)
        onehot_c = part(SC + 512, 64).rearrange("p (a n) -> p a n", a=NCH)
        token_c = part(SC + 576, 64).bitcast(BF16).rearrange("p (a m n) -> p a m n", a=NCH, m=2)
        listed = part(SC + 640, 16)
        tbl = part(S0 + 1056, NE * (3 + MORE))
        tw = part(S0 + 1056 + NE * (3 + MORE), NE * MORE).rearrange("p (e w) -> p e w", w=MORE)
        rest = part(S0 + 1056 + NE * (3 + 2 * MORE), NE)
        assert S0 + 1056 + NE * (4 + 2 * MORE) <= 24576

        XN = nc.dram_tensor("h2_rows", [T, D], F32, kind="Internal").ap()
        Y = nc.dram_tensor("expert_rows", [(NE + EXTRA) * WIN, D], F32, kind="Internal").ap()

        x_in, cst_in, win_in = [sem(f"x_in{i}") for i in range(NT)], sem("cst_in"), [sem(f"win_in{b}") for b in range(4)]
        wout_in, bias_in, bc_in = [sem("wout_in0"), sem("wout_in1")], sem("bias_in"), sem("bc_in")
        filled = [sem(f"bank_filled{b}") for b in range(8)]
        taken = [sem(f"bank_taken{b}") for b in range(8)]
        act_step, dve_step, pool_step = sem("act_step"), sem("dve_step"), sem("pool_step")
        x_sq, x_root, xn_done = sem("x_squares"), sem("x_root"), sem("xn_done")
        zprep_a, zprep_v = sem("gate_terms_act"), sem("gate_terms_dve")
        lv_sub, lv_exp, lv_mul = sem("level_diff"), sem("level_exp"), sem("level_operands")
        sasm_done = sem("scores_placed")
        o_sq, o_root, o_kept = sem("o_squares"), sem("o_root"), sem("o_kept")
        pr_max, pr_exp, pt_pe = sem("row_max"), sem("probs_exp"), sem("probs_transposed")
        at_ms, at_root, at_done = sem("att_squares"), sem("att_root"), sem("att_done")
        x2_sq, x2_root = sem("x2_squares"), sem("x2_root")
        h2_done, h2_ready, h2_out = sem("h2_done"), sem("h2_scaled"), [sem(f"h2_stored{i}") for i in range(NT)]
        r_exp_in, r_exp, assign_done = sem("router_exp_in"), sem("router_exp"), sem("assign_done")
        rows_done = sem("output_rows_known")
        oh_done, idx_done, ctl_done = sem("onehots_done"), sem("idx_done"), sem("windows_done")
        w13_in, w2_in = ([sem(f"{n}_in{s}") for s in range(WSLOTS)] for n in ("w1_w3", "w2"))
        gat, xg_turned = [sem(f"rows_gathered{b}") for b in range(4)], sem("rows_transposed")
        xt_a, xt_v, pads = sem("xt_copied_act"), sem("xt_copied_dve"), sem("pads_cleared")
        m_w, m_h, m_gu, m_t, m_sil, m_hid, m_y, m_yc = (sem(n) for n in (
            "window_copied", "up_products", "gate_up_copied", "gate_up_transposed", "silu_done", "hidden_done", "down_products", "y_copied"))
        e_w, e_h, e_gu, e_t, e_sil, e_hid, e_y, e_yc, e_out = (sem(n) for n in (
            "more_window_copied", "more_up_products", "more_gate_up_copied", "more_gate_up_transposed", "more_silu_done",
            "more_hidden_done", "more_down_products", "more_y_copied", "more_y_stored"))
        y_out = [sem(f"y_stored{b}") for b in range(WSLOTS)]
        f_in = [sem(f"token_rows_in{i}") for i in range(NT)]
        f_half, f_inv, f_scaled, f_last = sem("first_expert_added"), sem("final_inverse"), sem("final_scaled"), sem("last_rows")
        f_sum, f_sq, f_var, f_rt = sem("final_sum"), sem("final_squares"), sem("final_variance"), sem("final_root")
        f_done, out_sem = sem("final_rows"), sem("out_stored")
        bc2_in, cleared = sem("final_norm_in"), sem("cleared")

        def bank(name):
            return PS[PLAN[name][0]]

        def claim(pe, *name):
            b, n = PLAN[name]
            if n:
                pe.wait_ge(taken[b], n)
            return PS[b]

        def fill(ins, *name):
            ins.then_inc(filled[PLAN[name][0]], 1)

        def wait_filled(eng, *name):
            b, n = PLAN[name]
            eng.wait_ge(filled[b], n + 1)
            return PS[b]

        def take(ins, *name):
            ins.then_inc(taken[PLAN[name][0]], 1)

        def wait_taken(eng, *name):
            b, n = PLAN[name]
            eng.wait_ge(taken[b], n + 1)

        x_d = x.rearrange("(i p) d -> i p d", p=P)
        out_d = out.rearrange("(i p) d -> i p d", p=P)
        w_in_d = w_in.rearrange("(k p) n -> p k n", p=P)
        w_out_d = w_out.rearrange("(k p) n -> p k n", p=P)
        w1_d = w1.rearrange("e (p k) f -> e p (k f)", p=P)
        w3_d = w3.rearrange("e (p k) f -> e p (k f)", p=P)
        w2_d = w2.rearrange("e (j p) n -> e p j n", p=P)

        def expert_views(s):
            return (up_slot[s].rearrange("p (m k f) -> p m k f", m=2, k=KD), down_slot[s].rearrange("p (j n) -> p j n", j=2))

        def turned(ps, m):
            return ps[:, 2 * P:4 * P].rearrange("p (j m t) -> p j m t", j=2, m=2)[:, :, m, :]

        def first_of(eng, e):
            return eng.value_load(ctl[0:1, bass.ds(e, 1)], min_val=0, max_val=NA)

        def at(r, j, n=BODY):
            return j if r is None else r * n + j

        def buf(j):
            return TURN[j % BODY]

        def all_experts(eng, one):
            for j in range(PEEL):
                one(None, j)
            with eng.Fori(0, (NE - PEEL) // BODY) as r:
                for j in range(PEEL, PEEL + BODY):
                    one(r, j)

        def further_windows(eng, e, window):
            count = eng.value_load(ctl[0:1, bass.ds(e + NE, 1)], min_val=0, max_val=MORE)
            with eng.If(count > 0):
                before = eng.value_load(ctl[0:1, bass.ds(e + 2 * NE, 1)], min_val=0, max_val=EXTRA)
                with eng.Fori(0, count) as w:
                    window(before, w, e)

        def inverse_root(eng, chain, scratch, width, out_, in_, n):
            m = out_.shape[-1]
            u, y, w = (scratch[:, width * b:width * b + m] for b in range(3))
            chain(eng.tensor_scalar(u, in_, 1.0 / n, EPS, ALU.mult, ALU.add))
            chain(eng.tensor_scalar(y.bitcast(I32), u.bitcast(I32), -0.5, float(0x5F3759DF), ALU.mult, ALU.add))
            for step in range(3):
                chain(eng.tensor_tensor(w, y, y, ALU.mult))
                chain(eng.tensor_tensor(w, w, u, ALU.mult))
                chain(eng.tensor_scalar(w, w, -0.5, 1.5, ALU.mult, ALU.add))
                last = eng.tensor_tensor(out_ if step == 2 else y, w, y, ALU.mult)
                if step < 2:
                    chain(last)
            return last

        block = ctx.enter_context(nc.Block())

        @block.sync
        def _(sp):
            def win(g, n):
                b = GROUP_BUF[g]
                sp.dma_start(ring[b], w_in_d[:, :, GROUP_COL[g]:GROUP_COL[g] + 512]).then_inc(win_in[b], 16)

            for i in range(NT):
                sp.dma_start(xs[:, i, :], x_d[i]).then_inc(x_in[i], 16)
            sp.dma_start(cst, consts).then_inc(cst_in, 16)
            sp.dma_start(vec, vecs).then_inc(cst_in, 16)
            sp.dma_start(wr, w_route).then_inc(cst_in, 16)
            for n in range(4):
                win(GROUPS[n], n)
            wait_filled(sp, "f", 3)
            win("aq", 4)
            wait_filled(sp, "q", 3)
            win("av", 5)
            wait_filled(sp, "v", 3)
            win("g", 6)
            wait_filled(sp, "ak", 3)
            sp.dma_start(wout[0], w_out_d[:, :, 0:512]).then_inc(wout_in[0], 16)

            def load_up(s, e):
                sp.dma_start(up_slot[s][:, 0:W13], w1_d[e]).then_inc(w13_in[s], 16)
                sp.dma_start(up_slot[s][:, W13:2 * W13], w3_d[e]).then_inc(w13_in[s], 16)

            def load_down(s, e):
                sp.dma_start(expert_views(s)[1], w2_d[e]).then_inc(w2_in[s], 16)

            def expert(e):
                load_up(e, e)
                load_down(e, e)

            wait_filled(sp, "aq", 3)
            bsrc = bass.AP(rel_ext.tensor, 0, [[1, P], [639, AH], [1, 512]])
            sp.dma_start(bias, bsrc).then_inc(bias_in, 16)
            wait_filled(sp, "o", 3)
            sp.dma_start(bc_ffn, norm_ffn.partition_broadcast(P)).then_inc(bc_in, 16)
            wait_filled(sp, "g", 3)
            sp.dma_start(wout[1], w_out_d[:, :, 512:1024]).then_inc(wout_in[1], 16)
            expert(0)
            load_up(1, 1)

            def store_h2(i):
                sp.wait_ge(h2_ready, i + 1)
                sp.dma_start(XN[i * P:(i + 1) * P, :], h2_scaled[i]).then_inc(h2_out[i], 16)

            store_h2(0)
            store_h2(1)
            sp.wait_ge(at_done, NT)
            load_down(1, 1)
            expert(2)
            store_h2(2)
            expert(3)
            store_h2(3)
            wait_filled(sp, "out", 3, 1)
            expert(4)

            def reload(r, j):
                sp.wait_ge(m_h, at(r, j + 1))
                load_up(j % WSLOTS, at(r, j + WSLOTS))

            def follow(r, j):
                sp.wait_ge(m_y, at(r, j + 1))
                load_down(j % WSLOTS, at(r, j + WSLOTS))

            for j in range(PEEL):
                reload(None, j)
                if j >= 1:
                    follow(None, j - 1)
            with sp.Fori(0, (NE - PEEL) // BODY - 1) as r:
                for j in range(PEEL, PEEL + BODY):
                    reload(r, j)
                    follow(r, j - 1)
            follow(None, NE - WSLOTS - 1)
            sp.wait_ge(m_h, NE)
            sp.dma_start(bc_fin, norm_final.partition_broadcast(P)).then_inc(bc2_in, 16)
            for i in range(NT):
                if i < NT - 1:
                    sp.wait_ge(f_done, i + 1)
                else:
                    sp.wait_ge(f_last, 1)
                sp.dma_start(out_d[i], xs[:, i, :]).then_inc(out_sem, 16)
            sp.wait_ge(out_sem, 16 * NT)

        @block.gpsimd
        def _(pool):
            pool.memset(acc, 1.0).then_inc(pool_step, 1)
            pool.wait_ge(pool_step, 1)
            pool.memset(acc.rearrange("p (c t) -> p c t", t=P)[:, :, 0:1], 0.0).then_inc(cleared, 1)
            pool.memset(Sasm, 0.0).then_inc(cleared, 1)
            steps = [1]

            def chain(ins):
                ins.then_inc(pool_step, 1)
                steps[0] += 1
                pool.wait_ge(pool_step, steps[0])

            for kind, i, *_ in STEPS:
                if kind == "o_root":
                    pool.wait_ge(o_sq, NT * RH)
                    inverse_root(pool, chain, pool_scratch, 16, ors, oss, P).then_inc(o_root, 1)
                if kind == "att_norm":
                    pool.wait_ge(at_ms, i + 1)
                    inverse_root(pool, chain, pool_scratch, 16, ars[i % 2], ams[i % 2], AD).then_inc(at_root, 1)
                if kind == "ffn_in":
                    pool.wait_ge(x2_sq, i + 1)
                    inverse_root(pool, chain, pool_scratch, 16, rstd2[:, i:i + 1], ssq2[:, i:i + 1], D).then_inc(x2_root, 1)
            pool.wait_ge(idx_done, 1)
            for i in range(NT):
                pool.wait_ge(h2_out[i], 16)
            for c in range(NCH):
                if c == 4:
                    pool.memset(xt[:, :, NA:SL], 0.0).then_inc(pads, 1)
                if c >= 4:
                    pool.wait_ge(xg_turned, c - 3)
                pool.indirect_dma_start(xg[c % 4], None, XN, bass.IndirectOffsetOnAxis(ap=idx[:, c:c + 1], axis=0),
                                        bounds_check=T - 1).then_inc(gat[c % 4], 16)
            pool.wait_ge(rows_done, 1)
            for b in range(WSLOTS):
                pool.wait_ge(y_out[b], 32 * len(range(b, NE, WSLOTS)))
            for i in range(NT):
                for k in range(2):
                    n = 2 * i + k
                    pool.indirect_dma_start(yin[n], None, Y, bass.IndirectOffsetOnAxis(ap=pos_u[:, n:n + 1], axis=0),
                                            bounds_check=(NE + EXTRA) * WIN - 1).then_inc(f_in[i], 16)
            pool.wait_ge(bc2_in, 16)
            for i in range(NT - 1):
                pool.wait_ge(f_scaled, i + 1)
                pool.tensor_tensor(xs[:, i, :], xs[:, i, :], bc_fin, ALU.mult).then_inc(f_done, 1)

        @block.tensor
        def _(pe):
            pe.wait_ge(cst_in, 48)
            for i in range(NT):
                pe.wait_ge(xn_done, i + 1)
                for half in range(2):
                    ps = claim(pe, "xT", i, half)
                    for c in range(4):
                        last = pe.transpose(ps[:, c * P:(c + 1) * P], xn[i][:, (4 * half + c) * P:(4 * half + c + 1) * P], ident)
                    fill(last, "xT", i, half)

            def project(g, j, ks=range(KD)):
                ps = claim(pe, g, j) if ks[0] == 0 else bank((g, j))
                w = ring[GROUP_BUF[g]]
                for k in ks:
                    if g in ("f", "q", "ak", "aq"):
                        last = pe.matmul(ps[:], w[:, k, j * P:(j + 1) * P], hT[:, k, :], start=k == 0, stop=k == KD - 1)
                    else:
                        last = pe.matmul(ps[:], hT[:, k, j * P:(j + 1) * P], w[:, k, :], start=k == 0, stop=k == KD - 1)
                if ks[-1] == KD - 1:
                    fill(last, g, j)

            def begin(g):
                n = GROUPS.index(g)
                pe.wait_ge(win_in[GROUP_BUF[g]], 32 if n >= 4 else 16)

            for i in range(NT):
                wait_taken(pe, "xT", i, 0)
                wait_taken(pe, "xT", i, 1)
            for g in ("f", "q", "v", "ak"):
                begin(g)
                for j in range(4):
                    project(g, j)

            def small_blocks(ps, lhs, rhs):
                for hc in range(16):
                    for j in range(4):
                        at = hc * P + 32 * j
                        last = pe.matmul(ps[32 * j:32 * j + 32, 32 * hc:32 * hc + 32], lhs[:, at:at + 32], rhs[:, at:at + 32],
                                         start=True, stop=True)
                return last

            ps = claim(pe, "diag")
            pe.wait_ge(zprep_a, 8)
            for j in range(4):
                wait_taken(pe, "q", j)
            fill(small_blocks(ps, kT, qT), "diag")

            def level(li):
                pe.wait_ge(lv_mul, li + 1)
                buf = L[li % 2]
                if li == 0:
                    for half in range(2):
                        ps = claim(pe, "level", 0, half)
                        for n in range(8):
                            at = (8 * half + n) * P
                            last = pe.matmul(ps[0:64, 64 * n:64 * n + 64], buf[:, at:at + 64], buf[:, at + 64:at + 128],
                                             start=True, stop=True)
                        fill(last, "level", 0, half)
                elif li == 1:
                    ps = claim(pe, "level", 1, 0)
                    for hc in range(16):
                        for j in range(2):
                            at = hc * P + 64 * j
                            last = pe.matmul(ps[64 * j:64 * j + 32, 32 * hc:32 * hc + 32], buf[:, at:at + 32], buf[:, at + 32:at + 64],
                                             start=True, stop=True)
                    fill(last, "level", 1, 0)
                else:
                    fill(small_blocks(claim(pe, "level", li, 0), buf, buf), "level", li, 0)

            begin("aq")
            for li in range(7):
                if li == 4:
                    begin("av")
                if li < 4:
                    project("aq", li)
                else:
                    project("av", li - 4)
                level(li)
            project("av", 3)
            pe.wait_ge(lv_mul, 9)
            for c in range(3):
                ps = claim(pe, "kT", c)
                for h in range(RH):
                    last = pe.transpose(ps[:, h * P:(h + 1) * P], L[0][:, (4 * h + c) * P:(4 * h + c + 1) * P], ident)
                fill(last, "kT", c)
            begin("g")
            project("g", 0)
            for c in range(3):
                ps = claim(pe, "delta", c)
                wait_taken(pe, "kT", c)
                for h in range(RH):
                    last = pe.matmul(ps[:, h * P:(h + 1) * P], kdT[:, c, h * P:(h + 1) * P], vtok[:, c, h * P:(h + 1) * P],
                                     start=True, stop=True)
                fill(last, "delta", c)
            project("g", 1)

            def rec_out(c):
                ps = claim(pe, "o", c)
                pe.wait_ge(sasm_done, 1)
                if c:
                    wait_taken(pe, "delta", c - 1)
                for h in range(RH):
                    last = pe.matmul(ps[:, h * P:(h + 1) * P], Sasm[:, 4 * h + c, :], vtok[:, c, h * P:(h + 1) * P],
                                     start=True, stop=c == 0)
                    if c:
                        at = (4 * h + c) * P
                        last = pe.matmul(ps[:, h * P:(h + 1) * P], L[1][:, at:at + P], states[:, c - 1, h * P:(h + 1) * P],
                                         start=False, stop=True)
                fill(last, "o", c)

            for c in range(NT):
                rec_out(c)

            def ranks(t):
                cols = bank(("rank", 0))[:, t * NE:(t + 1) * NE]
                if t:
                    pe.matmul(cols, ones_, A[:, 0, :] if t == 1 else Apre[:, t - 1, :], start=True, stop=False)
                pe.matmul(cols, upper, A[:, t, :], start=t == 0, stop=True)

            for step in STEPS:
                kind, i = step[0], step[1]
                n = P * (i + 1)
                if kind == "g":
                    project("g", i, range(2 * step[2], 2 * step[2] + 2))
                if kind == "score":
                    h = step[2]
                    ps = claim(pe, "score", i, h)
                    o = 64 * (h % 2)
                    fill(pe.matmul(ps[:, 0:n], aqT[o:o + 64, h // 2, i * P:(i + 1) * P], akT[o:o + 64, h // 2, 0:n],
                                   start=True, stop=True), "score", i, h)
                if kind == "turn":
                    h = step[2]
                    ps = claim(pe, "pT", i, h)
                    pe.wait_ge(pr_exp, AH * i + h + 1)
                    for j in range(i + 1):
                        last = pe.transpose(ps[:, j * P:(j + 1) * P], prob[h % 4][:, j * P:(j + 1) * P], ident)
                    fill(last, "pT", i, h)
                if kind == "value":
                    h = step[2]
                    pv = claim(pe, "pv", i) if h == 0 else bank(("pv", i))
                    wait_taken(pe, "pT", i, h)
                    for j in range(i + 1):
                        last = pe.matmul(pv[:, h * AD:(h + 1) * AD], probT[h % 4][:, j * P:(j + 1) * P],
                                         avt[:, j, h * AD:(h + 1) * AD], start=j == 0, stop=j == i)
                    if h < AH - 1:
                        last.then_inc(pt_pe, 1)
                    else:
                        fill(last, "pv", i)
                if kind == "mixT":
                    half = step[2]
                    if half == 0:
                        pe.wait_ge(at_done, i + 1)
                    ps = claim(pe, "mT", i, half)
                    for c in range(4):
                        k = 4 * half + c
                        last = pe.transpose(ps[:, c * P:(c + 1) * P], mixed[:, i, k * P:(k + 1) * P], ident)
                    fill(last, "mT", i, half)
                if kind == "out":
                    half, q = step[2], step[3]
                    if q == 0:
                        if half == 0:
                            wait_taken(pe, "mT", i, 0)
                            wait_taken(pe, "mT", i, 1)
                        if i == 0:
                            pe.wait_ge(wout_in[half], 16)
                        ps = claim(pe, "out", i, half)
                    else:
                        ps = bank(("out", i, half))
                    for k in range(2 * q, 2 * q + 2):
                        last = pe.matmul(ps[:], mixT[i % 2][:, k, :], wout[half][:, k, :], start=k == 0, stop=k == KD - 1)
                    if q == 3:
                        fill(last, "out", i, half)
                if kind == "h2T":
                    half = step[2]
                    if half == 0:
                        pe.wait_ge(h2_done, i + 1)
                    ps = claim(pe, "hT2", i, half)
                    for c in range(4):
                        k = 4 * half + c
                        last = pe.transpose(ps[:, c * P:(c + 1) * P], h2tok[i % 2][:, k * P:(k + 1) * P], ident)
                    fill(last, "hT2", i, half)
                if kind == "logit":
                    wait_taken(pe, "hT2", i, 0)
                    wait_taken(pe, "hT2", i, 1)
                    ps = claim(pe, "logit", i)
                    for k in range(KD):
                        last = pe.matmul(ps[:, 0:36], h2T[i % 2][:, k, :], wr[:, k, :], start=k == 0, stop=k == KD - 1)
                    fill(last, "logit", i)
                if kind == "rank":
                    pe.wait_ge(assign_done, i + 1)
                    if i == 0:
                        claim(pe, "rank", 0)
                    ranks(i)
                if kind == "sort":
                    pe.wait_ge(assign_done, NT)
                    ps = bank(("rank", 0))
                    ranks(NT - 1)
                    pe.matmul(ps[:, NT * NE:(NT + 1) * NE], ones_, Apre[:, NT - 2, :], start=True, stop=False)
                    fill(pe.matmul(ps[:, NT * NE:(NT + 1) * NE], ones_, A[:, NT - 1, :], start=False, stop=True), "rank", 0)
                    ps = claim(pe, "list")
                    pe.wait_ge(oh_done, 1)
                    for n in range(NCH):
                        last = pe.matmul(ps[:, 0:2 * NCH], onehot_p[:, n, :], token_c[:, n].rearrange("p m n -> p (m n)"),
                                         start=n == 0, stop=n == NCH - 1)
                    fill(last, "list")
            for b in range(8):
                pe.wait_ge(taken[b], BANK_USES[b])

            for c in range(NCH):
                pe.wait_ge(gat[c % 4], 16 * (c // 4 + 1))
                if c >= 2:
                    pe.wait_ge(xt_a, c - 1)
                    pe.wait_ge(xt_v, c - 1)
                for half in range(2):
                    for n in range(4):
                        k = 4 * half + n
                        last = pe.transpose(PS[4 * (c % 2) + half][:, n * P:(n + 1) * P], xg[c % 4][:, k * P:(k + 1) * P], ident)
                last.then_inc(xg_turned, 1)

            def up(ps, s, xw, done):
                w13, _ = expert_views(s)
                for k in range(KD):
                    for m in range(2):
                        last = pe.matmul(ps[m * WIN:(m + 1) * WIN, 0:FF], xw[:, k, :], w13[:, m, k, :], start=k == 0, stop=k == KD - 1)
                last.then_inc(done, 1)

            def turn(ps, g, done):
                for j in range(2):
                    last = pe.transpose(ps[:, (2 + j) * P:(3 + j) * P], g[:, j * P:(j + 1) * P], ident)
                last.then_inc(done, 1)

            def down(ps, h, s, done):
                _, w2v = expert_views(s)
                for j in range(2):
                    for half in range(2):
                        last = pe.matmul(ps[half * WIN:(half + 1) * WIN, :], h[:, j, :], w2v[:, j, half * 512:(half + 1) * 512],
                                         start=j == 0, stop=j == 1)
                last.then_inc(done, 1)

            def previous_down(r, j):
                pe.wait_ge(w2_in[(j - 1) % WSLOTS], at(r, 16 * ((j - 1) // WSLOTS + 1), 16))
                pe.wait_ge(m_hid, at(r, j))
                if j >= 3:
                    pe.wait_ge(m_yc, at(r, j - 2))
                down(PS[3 + buf(j - 1)], hid[buf(j - 1)], (j - 1) % WSLOTS, m_y)

            def one(r, j):
                s = j % WSLOTS
                pe.wait_ge(w13_in[s], at(r, 32 * (j // WSLOTS + 1), 32))

                def window(before, w, e):
                    pe.wait_ge(e_w, before + w + 1)
                    up(PS[6], s, xwin[3], e_h)
                    pe.wait_ge(e_gu, before + w + 1)
                    turn(PS[6], gu[3], e_t)
                    pe.wait_ge(e_hid, before + w + 1)
                    pe.wait_ge(w2_in[s], at(r, 16 * (j // WSLOTS + 1), 16))
                    down(PS[7], hid[3], s, e_y)
                    pe.wait_ge(e_yc, before + w + 1)

                further_windows(pe, at(r, j), window)
                pe.wait_ge(m_w, at(r, j + 1))
                if j >= 2:
                    pe.wait_ge(m_hid, at(r, j - 1))
                up(PS[buf(j)], s, xwin[buf(j)], m_h)
                if j >= 1:
                    previous_down(r, j)
                pe.wait_ge(m_gu, at(r, j + 1))
                turn(PS[buf(j)], gu[buf(j)], m_t)

            pe.wait_ge(ctl_done, 1)
            all_experts(pe, one)
            previous_down(None, NE)

        @block.scalar
        def _(act):
            def a(out_, in_, f, **k):
                return act.activation(out_, in_, f, **k)

            steps = [0]

            def chain(ins):
                ins.then_inc(act_step, 1)
                steps[0] += 1
                act.wait_ge(act_step, steps[0])

            def copy_pt(i, h):
                n = P * (i + 1)
                wait_filled(act, "pT", i, h)
                if h >= 4:
                    act.wait_ge(pt_pe, (AH - 1) * i + h - 3)
                elif i and h < 3:
                    act.wait_ge(pt_pe, (AH - 1) * (i - 1) + h + 5)
                elif i:
                    wait_filled(act, "pv", i - 1)
                take(a(probT[h % 4][:, 0:n], bank(("pT", i, h))[:, 0:n], ACT.Copy), "pT", i, h)

            for i in range(NT):
                act.wait_ge(x_in[i], 16)
                if i >= 1:
                    act.wait_ge(x_sq, i)
                a(part(AQ, 1024), xs[:, i, :], ACT.Square, accum_out=ssq[:, i:i + 1]).then_inc(x_sq, 1)
            act.wait_ge(cleared, 2)
            for n in range(EXTRA * WIN // (2 * P)):
                first = NE * WIN + n * 2 * P
                act.dma_start(Y[first:first + 2 * P].rearrange("(p r) d -> p (r d)", r=2), Sasm.rearrange("p b t -> p (b t)")).then_inc(e_out, 16)
            act.wait_ge(x_root, 1)
            for i in range(NT):
                a(xn[i], xs[:, i, :], ACT.Copy, scale=rstd[:, i:i + 1]).then_inc(xn_done, 1)
            act.wait_ge(zprep_v, 1)
            a(lbw[:, 4:8], lbw[:, 0:4], ACT.Exp).then_inc(zprep_a, 1)
            act.wait_ge(zprep_v, 2)
            a(lbw[:, 12:16], lbw[:, 8:12], ACT.Ln, scale=-1.0, bias=1.0).then_inc(zprep_a, 1)
            for j in range(4):
                wait_filled(act, "q", j)
                take(a(qT[:, j * 512:(j + 1) * 512], bank(("q", j))[:], ACT.Silu), "q", j)

            def copy_v(j):
                wait_filled(act, "v", j)
                take(a(vtok[:, j, :], bank(("v", j))[:], ACT.Copy), "v", j)

            def copy_ak(j):
                wait_filled(act, "ak", j)
                take(a(akT[:, j, :], bank(("ak", j))[:], ACT.Copy), "ak", j)

            for j in range(4):
                wait_taken(act, "f", j)
            a(L[0], bcum, ACT.Relu, scale=-1.0).then_inc(zprep_a, 1)
            copy_v(0)
            act.wait_ge(zprep_v, 3)
            chain(a(L[1], L[1], ACT.Exp, scale=-1.0))
            copy_v(1)
            a(L[1], L[1], ACT.Ln, bias=1.0).then_inc(zprep_a, 1)
            copy_v(2)
            act.wait_ge(zprep_v, 5)
            act.wait_ge(zprep_a, 2)
            for h in range(RH):
                a(kT[:, h * 512:(h + 1) * 512], L[1][:, h * 512:(h + 1) * 512], ACT.Exp, scale=-1.0,
                  bias=lbw[:, 12 + h:13 + h]).then_inc(zprep_a, 1)
            copy_v(3)
            act.wait_ge(zprep_v, 6)
            chain(a(L[1], L[1], ACT.Exp, scale=-1.0))
            copy_ak(0)
            for h in range(RH):
                ins = a(L[1][:, h * 512:(h + 1) * 512], L[1][:, h * 512:(h + 1) * 512], ACT.Ln,
                        scale=lbw[:, 8 + h:9 + h], bias=1.0)
            ins.then_inc(zprep_a, 1)
            copy_ak(1)
            for li in range(2):
                act.wait_ge(lv_sub, li + 1)
                a(L[li], L[li], ACT.Exp).then_inc(lv_exp, 1)
            copy_ak(2)
            copy_ak(3)
            for li in range(7):
                if li < 4:
                    wait_filled(act, "aq", li)
                    take(a(aqT[:, li, :], bank(("aq", li))[:], ACT.Copy, scale=AD ** -0.5), "aq", li)
                else:
                    wait_filled(act, "av", li - 4)
                    take(a(avt[:, li - 4, :], bank(("av", li - 4))[:], ACT.Copy), "av", li - 4)
                if li + 2 < 7:
                    act.wait_ge(lv_sub, li + 3)
                    a(L[li % 2], L[li % 2], ACT.Exp).then_inc(lv_exp, 1)
                elif li + 2 == 7:
                    wait_filled(act, "level", 5, 0)
                    a(L[1], bcum, ACT.Exp).then_inc(lv_exp, 1)
                else:
                    act.wait_ge(lv_sub, 8)
                    a(ebl, bcum.rearrange("p (b t) -> p b t", t=P)[:, :, P - 1], ACT.Exp).then_inc(act_step, 1)
                    steps[0] += 1
                    a(L[0], L[0], ACT.Exp).then_inc(lv_exp, 1)
            wait_filled(act, "av", 3)
            take(a(avt[:, 3, :], bank(("av", 3))[:], ACT.Copy), "av", 3)
            for c in range(3):
                wait_filled(act, "kT", c)
                take(a(kdT[:, c, :], bank(("kT", c))[:], ACT.Copy), "kT", c)

            def silu_g(i):
                wait_filled(act, "g", i)
                take(a(mixed[:, i, 512:1024], bank(("g", i))[:], ACT.Silu), "g", i)

            silu_g(0)
            silu_g(1)

            for step in STEPS:
                kind, i = step[0], step[1]
                if kind == "score":
                    h, n = step[2], P * (i + 1)
                    act.wait_ge(pr_max, AH * i + h + 1)
                    a(prob[h % 4][:, 0:n], prob[h % 4][:, 0:n], ACT.Exp, bias=nmx[i % 2][:, h:h + 1],
                      accum_out=den[i % 2][:, h:h + 1]).then_inc(pr_exp, 1)
                if kind == "o_squares":
                    act.wait_ge(o_kept, i + 1)
                    for h in range(RH):
                        if i + h:
                            act.wait_ge(o_sq, RH * i + h)
                        a(part(K, 128), mixed[:, i, h * P:(h + 1) * P], ACT.Square,
                          accum_out=oss[:, 4 * i + h:4 * i + h + 1]).then_inc(o_sq, 1)
                if kind == "turn":
                    copy_pt(i, step[2])
                if kind == "silu_g":
                    silu_g(i)
                if kind == "ffn_in":
                    wait_taken(act, "out", i, 0)
                    wait_taken(act, "out", i, 1)
                    if i >= 1:
                        act.wait_ge(x2_sq, i)
                    a(part(M + 1024 * i, 1024), xs[:, i, :], ACT.Square, accum_out=ssq2[:, i:i + 1]).then_inc(x2_sq, 1)
                if kind == "h2T":
                    half = step[2]
                    wait_filled(act, "hT2", i, half)
                    take(a(h2T[i % 2].rearrange("p k t -> p (k t)")[:, half * 512:(half + 1) * 512], bank(("hT2", i, half))[:], ACT.Copy),
                         "hT2", i, half)
                if kind == "h2_scaled":
                    act.wait_ge(h2_done, i + 1)
                    act.wait_ge(x2_root, i + 1)
                    a(h2_scaled[i], h2tok[i % 2], ACT.Copy, scale=rstd2[:, i:i + 1]).then_inc(h2_ready, 1)
                if kind == "route":
                    act.wait_ge(r_exp_in, 2 * i + 1)
                    a(gex, gex, ACT.Exp, accum_out=gsum).then_inc(r_exp, 1)
                    act.wait_ge(r_exp_in, 2 * i + 2)
                    a(t4[:, 1:2], t4[:, 0:1], ACT.Exp).then_inc(r_exp, 1)

            for c in range(NCH):
                act.wait_ge(xg_turned, c + 1)
                a(xt[:, 4:8, c * P:(c + 1) * P], PS[4 * (c % 2) + 1][:].rearrange("p (k t) -> p k t", k=4), ACT.Copy).then_inc(xt_a, 1)

            def keep_y(r, j):
                act.wait_ge(m_y, at(r, j + 1))
                b = j % WSLOTS
                if j >= WSLOTS:
                    act.wait_ge(y_out[b], at(r, 32 * (j // WSLOTS), 32))
                a(y_rows[b], PS[3 + buf(j)][:], ACT.Copy).then_inc(m_yc, 1)
                act.wait_ge(m_yc, at(r, j + 1))
                for half in range(2):
                    act.dma_start(Y[bass.ds(at(r, WIN * j, WIN * BODY), WIN), half * 512:(half + 1) * 512],
                                  y_rows[b][half * WIN:(half + 1) * WIN, :]).then_inc(y_out[b], 16)

            def one(r, j):
                def window(before, w, e):
                    act.wait_ge(e_h, before + w + 1)
                    a(gu[3], PS[6][:, 0:FF], ACT.Copy).then_inc(e_gu, 1)
                    act.wait_ge(e_t, before + w + 1)
                    a(sil[3], turned(PS[6], 0), ACT.Silu).then_inc(e_sil, 1)
                    act.wait_ge(e_y, before + w + 1)
                    act.wait_ge(e_out, (before + w) * 32 + CLEARS)
                    a(y_rows[WSLOTS], PS[7][:], ACT.Copy).then_inc(e_yc, 1)
                    act.wait_ge(e_yc, before + w + 1)
                    row = nc.s_assert_within((before + w) * WIN + NE * WIN, NE * WIN, (NE + EXTRA - 1) * WIN,
                                             skip_runtime_bounds_check_because="1024 assignments make fewer than 16 further windows")
                    for half in range(2):
                        act.dma_start(Y[bass.ds(row, WIN), half * 512:(half + 1) * 512],
                                      y_rows[WSLOTS][half * WIN:(half + 1) * WIN, :]).then_inc(e_out, 16)

                further_windows(act, at(r, j), window)
                act.wait_ge(m_h, at(r, j + 1))
                if j >= 2:
                    act.wait_ge(m_t, at(r, j - 1))
                a(gu[buf(j)], PS[buf(j)][:, 0:FF], ACT.Copy).then_inc(m_gu, 1)
                if j >= 1:
                    keep_y(r, j - 1)
                act.wait_ge(m_t, at(r, j + 1))
                if j >= 2:
                    act.wait_ge(m_hid, at(r, j - 1))
                a(sil[buf(j)], turned(PS[buf(j)], 0), ACT.Silu).then_inc(m_sil, 1)

            act.wait_ge(ctl_done, 1)
            all_experts(act, one)
            total = (act.value_load(ctl[0:1, 2 * NE - 1:2 * NE], min_val=0, max_val=MORE)
                     + act.value_load(ctl[0:1, 3 * NE - 1:3 * NE], min_val=0, max_val=EXTRA))
            act.wait_ge(e_out, total * 32 + CLEARS)
            keep_y(None, NE - 1)
            for i in range(NT):
                act.wait_ge(f_sum, i + 1)
                if i:
                    act.wait_ge(f_sq, i)
                a(junk, xs[:, i, :], ACT.Square, accum_out=fssq[:, i:i + 1]).then_inc(f_sq, 1)
                act.wait_ge(f_var, i + 1)
                a(frstd[:, i:i + 1], frstd[:, i:i + 1], ACT.Sqrt).then_inc(f_rt, 1)
                if i >= 1:
                    act.wait_ge(f_inv, i)
                    a(xs[:, i - 1, :], xs[:, i - 1, :], ACT.Copy, scale=frstd[:, i - 1:i]).then_inc(f_scaled, 1)

        @block.vector
        def _(v):
            steps = [0]

            def chain(ins):
                ins.then_inc(dve_step, 1)
                steps[0] += 1
                v.wait_ge(dve_step, steps[0])

            v.wait_ge(x_sq, NT)
            inverse_root(v, chain, root_scratch, 4, rstd, ssq, D).then_inc(x_root, 1)
            v.wait_ge(cst_in, 48)
            for i in range(NT):
                for half in range(2):
                    ps = wait_filled(v, "xT", i, half)
                    w = vec[:, V_MIX + 4 * half:V_MIX + 4 * half + 4].unsqueeze(2).to_broadcast([P, 4, P])
                    take(v.tensor_tensor(hT[:, 4 * half:4 * half + 4, i * P:(i + 1) * P],
                                         ps[:].rearrange("p (c t) -> p c t", c=4), w, ALU.mult), "xT", i, half)
            lb_in = vec[:, V_LB:V_LB + 4]
            v.tensor_tensor(lbw[:, 0:4], lb_in, lb_in, ALU.subtract).then_inc(zprep_v, 1)
            v.wait_ge(zprep_a, 1)
            chain(v.reciprocal(lbw[:, 8:12], lbw[:, 4:8]))
            chain(v.tensor_tensor(lbw[:, 8:12], lbw[:, 8:12], lbw[:, 4:8], ALU.mult))
            v.tensor_tensor(lbw[:, 8:12], lbw[:, 8:12], lbw[:, 8:12], ALU.subtract).then_inc(zprep_v, 1)
            for j in range(4):
                ps = wait_filled(v, "f", j)
                take(v.tensor_copy(bcum[:, j * 512:(j + 1) * 512], ps[:]), "f", j)
            for j in range(4):
                wait_taken(v, "f", j)
            v.wait_ge(zprep_a, 3)
            v.scalar_tensor_tensor(L[1], L[0], 2.0, bcum, ALU.mult, ALU.add).then_inc(zprep_v, 1)
            v.wait_ge(zprep_a, 4)
            v.tensor_tensor(L[0], L[0], L[1], ALU.add).then_inc(zprep_v, 1)
            v.wait_ge(zprep_v, 4)
            v.tensor_tensor(L[1], bcum, L[0], ALU.add).then_inc(zprep_v, 1)
            v.wait_ge(zprep_a, 8)
            v.tensor_scalar(L[1], bcum, -80.0, None, ALU.max).then_inc(zprep_v, 1)
            v.wait_ge(zprep_a, 9)
            chain(v.tensor_tensor(L[1], L[1], L[0], ALU.subtract))
            v.wait_ge(cleared, 1)
            for h in range(RH):
                ins = v.tensor_tensor_scan(bcum[:, h * 512:(h + 1) * 512], acc, L[1][:, h * 512:(h + 1) * 512], 0.0, ALU.mult, ALU.add)
            chain(ins)

            bv = bcum.rearrange("p (n t) -> p n t", t=P)

            def diff(li):
                hs = HALVES[li]
                b4 = bcum.rearrange("p (n s t) -> p n s t", s=2, t=hs)
                l4 = L[li % 2].rearrange("p (n s t) -> p n s t", s=2, t=hs)
                mid = b4[:, :, 0, hs - 1:hs].to_broadcast([P, 1024 // hs, hs])
                v.tensor_tensor(l4[:, :, 0, :], mid, b4[:, :, 0, :], ALU.subtract)
                v.tensor_tensor(l4[:, :, 1, :], b4[:, :, 1, :], mid, ALU.subtract).then_inc(lv_sub, 1)

            def operands(li):
                hs = HALVES[li]
                l4, k4, q4 = (t.rearrange("p (n s t) -> p n s t", s=2, t=hs) for t in (L[li % 2], kT, qT))
                v.wait_ge(lv_exp, li + 1)
                v.tensor_tensor(l4[:, :, 0, :], l4[:, :, 0, :], k4[:, :, 0, :], ALU.mult)
                v.tensor_tensor(l4[:, :, 1, :], l4[:, :, 1, :], q4[:, :, 1, :], ALU.mult).then_inc(lv_mul, 1)

            def masked(ps, m):
                w = cst[:, C_MASK + 32 * m:C_MASK + 32 * m + 32].unsqueeze(1).to_broadcast([P, 16, 32])
                return ps[:].rearrange("p (b t) -> p b t", t=32), w

            acc3 = acc.rearrange("p (b t) -> p b t", t=32)
            tmp3 = part(M, 512).rearrange("p (b t) -> p b t", t=32)

            def place(li):
                if li == 0:
                    v.wait_ge(e_out, CLEARS)
                    for half in range(2):
                        ps = wait_filled(v, "level", 0, half)
                        take(v.tensor_copy(Sasm[0:64, 8 * half:8 * half + 8, 64:128],
                                           ps[0:64, :].rearrange("p (b t) -> p b t", t=64)), "level", 0, half)
                elif li == 1:
                    ps = wait_filled(v, "level", 1, 0)
                    v.tensor_copy(Sasm[0:32, :, 32:64], ps[0:32, :].rearrange("p (b t) -> p b t", t=32))
                    take(v.tensor_copy(Sasm[64:96, :, 96:128], ps[64:96, :].rearrange("p (b t) -> p b t", t=32)), "level", 1, 0)
                else:
                    ps = wait_filled(v, "level", li, 0)
                    take(v.tensor_tensor(tmp3, *masked(ps, li - 2), ALU.mult), "level", li, 0)
                    wait_taken(v, "level", li, 0)
                    chain(v.tensor_tensor(acc3, acc3, tmp3, ALU.add))

            diff(0)
            diff(1)
            v.wait_ge(cleared, 2)
            ps = wait_filled(v, "diag")
            take(v.tensor_tensor(acc3, *masked(ps, 5), ALU.mult), "diag")
            wait_taken(v, "diag")
            for j in range(4):
                wait_taken(v, "q", j)
            operands(0)
            operands(1)
            for li in range(2, 7):
                wait_filled(v, "level", li - 2, 1 if li == 2 else 0)
                diff(li)
                place(li - 2)
                operands(li)
            place(5)
            v.wait_ge(lv_exp, 8)
            v.tensor_tensor(L[1], L[1], qT, ALU.mult).then_inc(lv_mul, 1)
            wait_filled(v, "level", 6, 0)
            last_b = bv[:, :, P - 1:P].to_broadcast([P, 16, P])
            v.tensor_tensor(L[0].rearrange("p (n t) -> p n t", t=P), last_b, bv, ALU.subtract).then_inc(lv_sub, 1)
            place(6)
            for j in range(4):
                ins = v.tensor_copy(Sasm[32 * j:32 * j + 32, :, 32 * j:32 * j + 32], acc3[32 * j:32 * j + 32])
            ins.then_inc(sasm_done, 1)
            v.wait_ge(lv_exp, 9)
            v.tensor_tensor(L[0], L[0], kT, ALU.mult).then_inc(lv_mul, 1)
            v.wait_ge(lv_mul, 9)
            for c in range(3):
                ps = wait_filled(v, "delta", c)
                if c == 0:
                    take(v.tensor_copy(states[:, 0, :], ps[:]), "delta", 0)
                else:
                    for h in range(RH):
                        ins = v.scalar_tensor_tensor(states[:, c, h * P:(h + 1) * P], states[:, c - 1, h * P:(h + 1) * P],
                                                     ebl[:, 4 * h + c:4 * h + c + 1], ps[:, h * P:(h + 1) * P], ALU.mult, ALU.add)
                    take(ins, "delta", c)
                wait_taken(v, "delta", c)
            for c in range(NT):
                ps = wait_filled(v, "o", c)
                take(v.tensor_copy(mixed[:, c, 0:512], ps[:]), "o", c)
                wait_taken(v, "o", c)
                v.sem_inc(o_kept, 1)

            def rel_bias(h, n):
                return bass.AP(arena, BIAS + 512 * h + n - 1, [[arena.shape[1], P], [-1, n]])

            v.wait_ge(bias_in, 16)
            chain(v.memset(bias[0:64, :, 0:64], NEG))
            for step in STEPS:
                kind, i = step[0], step[1]
                if kind == "score":
                    h, n = step[2], P * (i + 1)
                    ps = wait_filled(v, "score", i, h)
                    if h >= 4:
                        wait_filled(v, "pT", i, h - 4)
                    elif i:
                        wait_filled(v, "pT", i - 1, h + 4)
                    take(v.tensor_tensor_reduce(prob[h % 4][:, 0:n], ps[:, 0:n], rel_bias(h, n), 1.0, -3.0e38,
                                                ALU.add, ALU.max, mx[:, h:h + 1]), "score", i, h)
                    wait_taken(v, "score", i, h)
                    v.tensor_scalar(nmx[i % 2][:, h:h + 1], mx[:, h:h + 1], -1.0, None, ALU.mult).then_inc(pr_max, 1)
                if kind == "att_norm":
                    v.wait_ge(pr_exp, AH * (i + 1))
                    chain(v.reciprocal(rden, den[i % 2]))
                    ps = wait_filled(v, "pv", i)
                    o3 = mixed[:, i, 512:1024].rearrange("p (h d) -> p h d", h=AH)
                    take(v.tensor_tensor(o3, ps[:].rearrange("p (h d) -> p h d", h=AH),
                                         rden.unsqueeze(2).to_broadcast([P, AH, AD]), ALU.mult), "pv", i)
                    wait_taken(v, "pv", i)
                    chain(v.tensor_tensor(att_sq, mixed[:, i, 512:1024], mixed[:, i, 512:1024], ALU.mult))
                    v.tensor_reduce(ams[i % 2], att_sq.rearrange("p (h d) -> p h d", h=AH), AX_X, ALU.add).then_inc(at_ms, 1)
                if kind == "att_scale":
                    v.wait_ge(at_root, i + 1)
                    o3 = mixed[:, i, 512:1024].rearrange("p (h d) -> p h d", h=AH)
                    v.tensor_tensor(o3, o3, ars[i % 2].unsqueeze(2).to_broadcast([P, AH, AD]), ALU.mult).then_inc(at_done, 1)
                if kind == "gate":
                    wait_taken(v, "g", i)
                    v.wait_ge(o_root, 1)
                    for h in range(RH):
                        cols = slice(h * P, (h + 1) * P)
                        v.scalar_tensor_tensor(mixed[:, i, cols], mixed[:, i, cols], ors[:, 4 * i + h:4 * i + h + 1],
                                               mixed[:, i, 512 + h * P:512 + (h + 1) * P], ALU.mult, ALU.mult)
                if kind == "mixT":
                    half = step[2]
                    ps = wait_filled(v, "mT", i, half)
                    w = vec[:, V_OUT + 4 * half:V_OUT + 4 * half + 4].unsqueeze(2).to_broadcast([P, 4, P])
                    take(v.tensor_tensor(mixT[i % 2][:, 4 * half:4 * half + 4, :], ps[:].rearrange("p (c t) -> p c t", c=4), w,
                                         ALU.mult), "mT", i, half)
                if kind == "out" and step[3] == 3:
                    half = step[2]
                    ps = wait_filled(v, "out", i, half)
                    cols = slice(512 * half, 512 * half + 512)
                    take(v.tensor_tensor(xs[:, i, cols], xs[:, i, cols], ps[:], ALU.add), "out", i, half)
                if kind == "h2":
                    if i == 0:
                        v.wait_ge(bc_in, 16)
                    if i >= 2:
                        wait_filled(v, "hT2", i - 2, 1)
                        v.wait_ge(h2_ready, i - 1)
                    wait_taken(v, "out", i, 0)
                    wait_taken(v, "out", i, 1)
                    turn = "p (d k) -> p k d"
                    v.tensor_tensor(h2tok[i % 2].rearrange("p (k d) -> p k d", k=KD), xs[:, i, :].rearrange(turn, k=KD),
                                    bc_ffn.rearrange(turn, k=KD), ALU.mult).then_inc(h2_done, 1)
                if kind == "logit":
                    ps = wait_filled(v, "logit", i)
                    v.wait_ge(x2_root, i + 1)
                    take(v.tensor_scalar(lg, ps[:, 0:36], rstd2[:, i:i + 1], None, ALU.mult), "logit", i)
                if kind == "route":
                    if i == 0:
                        v.memset(gpad, NEG).then_inc(dve_step, 1)
                        steps[0] += 1
                        v.wait_ge(dve_step, steps[0])
                    wait_taken(v, "logit", i)
                    chain(v.tensor_copy(gpad[:, 0:NG], lg[:, 0:NG]))
                    chain(v.max(gm8, gpad))
                    chain(v.max_index(top_idx[:, 0:8], gm8, gpad))
                    chain(v.tensor_copy(t4[:, 4:5], top_idx[:, 0:1]))
                    chain(v.tensor_scalar(goh, iota[:, 0:NG], t4[:, 4:5], None, ALU.is_equal))
                    chain(v.tensor_scalar(goh, goh, -1.0, -NEG, ALU.add, ALU.mult))
                    v.tensor_scalar(gex, lg[:, 0:NG], gm8[:, 0:1], None, ALU.subtract).then_inc(r_exp_in, 1)
                    chain(v.tensor_tensor(em.rearrange("p (g e) -> p g e", g=NG), lg[:, NG:36].rearrange("p (g e) -> p g e", g=NG),
                                          goh.unsqueeze(2).to_broadcast([P, NG, EPG]), ALU.add))
                    chain(v.max(em8, em))
                    chain(v.max_index(top_idx[:, 8:16], em8, em))
                    v.tensor_tensor(t4[:, 0:1], em8[:, 1:2], em8[:, 0:1], ALU.subtract).then_inc(r_exp_in, 1)
                    chain(v.tensor_copy(expid[:, 2 * i:2 * i + 2], top_idx[:, 8:10]))
                    for k in range(2):
                        ins = v.tensor_scalar(A12[:, 32 * k:32 * k + 32], iota[:, 0:NE], expid[:, 2 * i + k:2 * i + k + 1], None, ALU.is_equal)
                    chain(ins)
                    ins = v.tensor_tensor(A[:, i, :], A12[:, 0:32], A12[:, 32:64], ALU.add)
                    if i in (1, 2):
                        chain(ins)
                        ins = v.tensor_tensor(Apre[:, i, :], A[:, 0, :] if i == 1 else Apre[:, 1, :], A[:, i, :], ALU.add)
                    ins.then_inc(assign_done, 1)
                    v.wait_ge(r_exp, 2 * i + 2)
                    chain(v.tensor_scalar(t4[:, 2:3], t4[:, 1:2], 1.0, None, ALU.add))
                    chain(v.tensor_tensor(t4[:, 2:3], t4[:, 2:3], gsum, ALU.mult))
                    chain(v.reciprocal(gate[:, i, 0:1], t4[:, 2:3]))
                    chain(v.tensor_tensor(gate[:, i, 1:2], gate[:, i, 0:1], t4[:, 1:2], ALU.mult))
                if kind == "sort":
                    v.wait_ge(h2_out[1], 16)
                    i8 = iota[:, 0:NE].unsqueeze(1).unsqueeze(1).to_broadcast([P, NT, 2, NE])
                    chain(v.tensor_tensor(hot1, i8, expid.rearrange("p (i k) -> p i k", k=2).unsqueeze(3).to_broadcast([P, NT, 2, NE]),
                                          ALU.is_equal))
                    chain(v.tensor_scalar(edges, iota[:, 1:9], float(P), None, ALU.mult))
                    ps = wait_filled(v, "rank", 0)
                    chain(v.tensor_copy(cnt, ps[:, NT * NE:(NT + 1) * NE]))
                    chain(v.tensor_tensor_scan(incl, ones_[:, 0:NE], cnt, 0.0, ALU.mult, ALU.add))
                    chain(v.tensor_tensor(off, incl, cnt, ALU.subtract))
                    rank4 = ps[:, 0:NT * NE].rearrange("p (i e) -> p i e", i=NT).unsqueeze(2).to_broadcast([P, NT, 2, NE])
                    take(v.tensor_tensor(hotw, hot1, rank4, ALU.mult), "rank", 0)
                    chain(v.tensor_tensor(hot, hot1, off.unsqueeze(1).unsqueeze(1).to_broadcast([P, NT, 2, NE]), ALU.mult))
                    wait_taken(v, "rank", 0)
                    chain(v.tensor_tensor(hotw, hotw, hot, ALU.add))
                    chain(v.tensor_reduce(pos, hotw.rearrange("p i k e -> p (i k) e"), AX_X, ALU.add))
                    chain(v.tensor_tensor(over, pos.unsqueeze(2).to_broadcast([P, NCH, 8]),
                                          edges.unsqueeze(1).to_broadcast([P, NCH, 8]), ALU.is_ge))
                    chain(v.tensor_reduce(chunk, over, AX_X, ALU.add))
                    chain(v.scalar_tensor_tensor(within, chunk, -float(P), pos, ALU.mult, ALU.add))
                    chain(v.tensor_tensor(onehot_c, iota[:, 0:NCH].unsqueeze(1).to_broadcast([P, NCH, NCH]),
                                          chunk.unsqueeze(2).to_broadcast([P, NCH, NCH]), ALU.is_equal))
                    v.tensor_tensor(token_c[:, :, 0, :], onehot_c, cst[:, C_TOK:C_TOK + NCH].unsqueeze(2).to_broadcast([P, NCH, NCH]), ALU.mult)
                    v.tensor_tensor(token_c[:, :, 1, :], onehot_c, cst[:, C_TOK + NCH:C_END].unsqueeze(2).to_broadcast([P, NCH, NCH]), ALU.mult)
                    v.tensor_tensor(onehot_p, iota.unsqueeze(1).to_broadcast([P, NCH, P]),
                                    within.unsqueeze(2).to_broadcast([P, NCH, P]), ALU.is_equal).then_inc(oh_done, 1)
                    ps = wait_filled(v, "list")
                    take(v.tensor_copy(listed, ps[:, 0:2 * NCH]), "list")
                    wait_taken(v, "list")
                    chain(v.tensor_tensor(idx[:], listed[:, 0:NCH], listed[:, NCH:2 * NCH], ALU.add))
                    v.sem_inc(idx_done, 1)
                    chain(v.tensor_copy(tbl[:, 0:NE], off))
                    chain(v.tensor_scalar(wl, iota[:, 1:1 + MORE], float(WIN), None, ALU.mult))
                    wlb = wl.unsqueeze(1).to_broadcast([P, NE, MORE])
                    chain(v.tensor_tensor(tw, cnt.unsqueeze(2).to_broadcast([P, NE, MORE]), wlb, ALU.is_gt))
                    chain(v.tensor_reduce(tbl[:, NE:2 * NE], tw, AX_X, ALU.add))
                    chain(v.tensor_tensor_scan(rest, ones_[:, 0:NE], tbl[:, NE:2 * NE], 0.0, ALU.mult, ALU.add))
                    chain(v.tensor_tensor(tbl[:, 2 * NE:3 * NE], rest, tbl[:, NE:2 * NE], ALU.subtract))
                    chain(v.tensor_tensor(tbl[:, 3 * NE:].rearrange("p (e w) -> p e w", w=MORE), wlb,
                                          off.unsqueeze(2).to_broadcast([P, NE, MORE]), ALU.add))
                    v.tensor_copy(ctl[:], tbl[0:1]).then_inc(ctl_done, 1)
                    chain(v.tensor_tensor(hotw, hot1, off.unsqueeze(1).unsqueeze(1).to_broadcast([P, NT, 2, NE]), ALU.mult))
                    chain(v.tensor_reduce(rank, hotw.rearrange("p i k e -> p (i k) e"), AX_X, ALU.add))
                    chain(v.tensor_tensor(rank, pos, rank, ALU.subtract))
                    chain(v.tensor_tensor(hotw, hot1, tbl[:, 2 * NE:3 * NE].unsqueeze(1).unsqueeze(1).to_broadcast([P, NT, 2, NE]), ALU.mult))
                    chain(v.tensor_reduce(row, hotw.rearrange("p i k e -> p (i k) e"), AX_X, ALU.add))
                    chain(v.tensor_scalar(row, row, float(NE - 1), None, ALU.add))
                    chain(v.tensor_tensor(row, row, expid, ALU.subtract))
                    chain(v.tensor_scalar(late, rank, float(WIN), None, ALU.is_ge))
                    chain(v.tensor_tensor(row, row, late, ALU.mult))
                    chain(v.tensor_tensor(row, row, expid, ALU.add))
                    chain(v.scalar_tensor_tensor(row, row, float(WIN), rank, ALU.mult, ALU.add))
                    v.tensor_copy(pos_u[:], row).then_inc(rows_done, 1)

            for c in range(NCH):
                v.wait_ge(xg_turned, c + 1)
                v.tensor_copy(xt[:, 0:4, c * P:(c + 1) * P], PS[4 * (c % 2)][:].rearrange("p (k t) -> p k t", k=4)).then_inc(xt_v, 1)

            def hidden(ps, b, done):
                v.tensor_tensor(hid[b], sil[b], turned(ps, 1), ALU.mult).then_inc(done, 1)

            def copy_window(b, first, done):
                v.tensor_copy(xwin[b], xt[:, :, bass.ds(first, WIN)]).then_inc(done, 1)

            def previous_hidden(r, j):
                v.wait_ge(m_sil, at(r, j))
                if j >= 3:
                    v.wait_ge(m_y, at(r, j - 2))
                hidden(PS[buf(j - 1)], buf(j - 1), m_hid)

            def one(r, j):
                def window(before, w, e):
                    copy_window(3, v.value_load(ctl[0:1, bass.ds(e * MORE + w + 3 * NE, 1)], min_val=0, max_val=NA), e_w)
                    v.wait_ge(e_sil, before + w + 1)
                    hidden(PS[6], 3, e_hid)

                further_windows(v, at(r, j), window)
                first = first_of(v, at(r, j))
                if j >= 2:
                    v.wait_ge(m_h, at(r, j - 1))
                copy_window(buf(j), first, m_w)
                if j >= 1:
                    previous_hidden(r, j)

            for c in range(NCH):
                v.wait_ge(xt_v, c + 1)
            v.wait_ge(xt_a, NCH)
            v.wait_ge(pads, 1)
            v.wait_ge(ctl_done, 1)
            all_experts(v, one)
            previous_hidden(None, NE)
            def final_variance(i):
                v.wait_ge(f_sq, i + 1)
                v.tensor_scalar(frstd[:, i:i + 1], fssq[:, i:i + 1], 1.0 / D, EPS, ALU.mult, ALU.add).then_inc(f_var, 1)

            def final_inverse(i):
                v.wait_ge(f_rt, i + 1)
                v.reciprocal(frstd[:, i:i + 1], frstd[:, i:i + 1]).then_inc(f_inv, 1)

            for i in range(NT):
                v.wait_ge(f_in[i], 32)
                v.scalar_tensor_tensor(xs[:, i, :], yin[2 * i], gate[:, i, 0:1], xs[:, i, :], ALU.mult, ALU.add).then_inc(f_half, 1)
                if i:
                    final_variance(i - 1)
                v.wait_ge(f_half, i + 1)
                v.scalar_tensor_tensor(xs[:, i, :], yin[2 * i + 1], gate[:, i, 1:2], xs[:, i, :], ALU.mult, ALU.add).then_inc(f_sum, 1)
                if i:
                    final_inverse(i - 1)
            final_variance(NT - 1)
            final_inverse(NT - 1)
            v.wait_ge(bc2_in, 16)
            v.wait_ge(f_inv, NT)
            i = NT - 1
            v.scalar_tensor_tensor(xs[:, i, :], xs[:, i, :], frstd[:, i:i + 1], bc_fin, ALU.mult, ALU.mult).then_inc(f_last, 1)


def constant_table():
    c = np.zeros((P, C_END), np.float32)
    p, t = np.arange(P)[:, None], np.arange(P)[None, :]
    c[:, C_ID:C_ID + P] = p == t
    c[:, C_UP:C_UP + P] = p < t
    c[:, C_ONE:C_ONE + P] = 1
    c[:, C_IOTA:C_IOTA + P] = t
    s, q = np.arange(P)[:, None] % 32, np.arange(32)[None, :]
    for m, h in enumerate(HALVES[2:]):
        c[:, C_MASK + 32 * m:C_MASK + 32 * m + 32] = (s // (2 * h) == q // (2 * h)) & (s // h % 2 == 0) & (q // h % 2 == 1)
    c[:, C_MASK + 160:C_MASK + 192] = s == q
    for i in range(NT):
        for k in range(2):
            c[:, C_TOK + 2 * i + k] = np.arange(P)
            c[:, C_TOK + NCH + 2 * i + k] = P * i
    return c


def kernel(x, norm_mix_w, w_in, hgrn_lower_bounds, hgrn_gnorm_w, attn_rel_bias, attn_norm_w, w_out, norm_ffn_w,
           moe_w_group, moe_w_expert, moe_w1, moe_w3, moe_w2, final_norm_w):
    import concourse.bacc as bacc
    from concourse.bass_utils import run_bass_kernel_spmd

    f = np.ascontiguousarray
    order = np.minimum(np.arange(639) + 1, NREL - 1)
    arrays = {
        "x": f(np.asarray(x)[0]),
        "w_in": f(np.asarray(w_in)[0]),
        "w_out": f(np.asarray(w_out)[0]),
        "rel_ext": f(np.asarray(attn_rel_bias)[0][:, order]),
        "vecs": f(np.concatenate([np.asarray(a)[0].reshape(-1, P).T for a in (norm_mix_w, hgrn_lower_bounds, hgrn_gnorm_w, attn_norm_w)], axis=1)),
        "w_route": f(np.concatenate([np.asarray(moe_w_group)[0], np.asarray(moe_w_expert)[0]], axis=1).reshape(P, KD, 36)),
        "norm_ffn": f(np.asarray(norm_ffn_w)[0]),
        "norm_final": f(np.asarray(final_norm_w)),
        "w1": f(np.asarray(moe_w1)[0]),
        "w3": f(np.asarray(moe_w3)[0]),
        "w2": f(np.asarray(moe_w2)[0]),
        "consts": constant_table(),
    }
    nc = bacc.Bacc("TRN2", target_bir_lowering=False, num_devices=1)
    args = [nc.dram_tensor(f"in_{n}", a.shape, mybir.dt.from_np(a.dtype), kind="ExternalInput").ap() for n, a in arrays.items()]
    args.append(nc.dram_tensor("out_rows", (T, D), F32, kind="ExternalOutput").ap())
    trunk(nc, *args)
    r = run_bass_kernel_spmd(nc, [{f"in_{n}": a for n, a in arrays.items()}], core_ids=[0])
    return r.results[0]["out_rows"].reshape(1, T, D)
```
